# Optimizing a Trainium2 kernel written in Bass

```python
import math
import jax, jax.numpy as jnp
from jax import lax
import numpy as np

D_MODEL = 1024
BATCH = 1
SEQ = 1024
DEPTH = 1
DEC_BATCH = 1
DEC_SEQ = 256
PAST_LEN = 128

N_MEM = 256
EPS = 1e-6
HG_HEADS = 4
HG_DK = D_MODEL // 8
HG_DV = D_MODEL // 8
HG_WIDTH = HG_HEADS * HG_DV
HG_CHUNK = 64
DA_HEADS = 4
DA_DK = D_MODEL // 16
DA_DV = 2 * DA_DK
DA_WIDTH = DA_HEADS * DA_DV
Q_BLOCK = 128
MIX_WIDTH = HG_WIDTH + DA_WIDTH
IN_COLS = 3 * HG_HEADS * HG_DK + 2 * HG_HEADS * HG_DV + 2 * DA_HEADS * 2 * DA_DK + DA_HEADS * DA_DV
CA_HEADS = 4
CA_DH = D_MODEL // CA_HEADS
N_GROUPS = 4
EXP_PER_GROUP = 8
N_EXPERTS = N_GROUPS * EXP_PER_GROUP
TOP_K = 2
D_EXPERT = D_MODEL // 2
MOE_BLOCK = 128

kernel_name = 'hymba_hgrn2_diffattn_hmoe_encoder'

def rms_norm(x, g):
    x32 = x.astype(jnp.float32)
    y = x32 * lax.rsqrt(jnp.mean(x32 * x32, axis=-1, keepdims=True) + EPS)
    return (y * g.astype(jnp.float32)).astype(x.dtype)

def head_rms(o, g):
    o32 = o.astype(jnp.float32)
    return o32 * lax.rsqrt(jnp.mean(o32 * o32, axis=-1, keepdims=True) + EPS) * g.astype(jnp.float32)

def alibi_slopes(n_heads):
    return jnp.power(2.0, -8.0 * jnp.arange(1, n_heads + 1, dtype=jnp.float32) / n_heads)

def hgrn2_chunk_scan(q, k, v, log_f):
    B, S, H, DK = q.shape
    DV = v.shape[-1]
    n = S // HG_CHUNK

    def to_chunks(t):
        return jnp.moveaxis(t.reshape(B, n, HG_CHUNK, H, t.shape[-1]), 1, 0).transpose(0, 1, 3, 2, 4)

    qc, kc, vc, fc = to_chunks(q), to_chunks(k), to_chunks(v), to_chunks(log_f)
    lower = jnp.tril(jnp.ones((HG_CHUNK, HG_CHUNK), dtype=bool))[:, :, None]

    def step(state, inp):
        qb, kb, vb, fb = inp
        b = jnp.cumsum(fb, axis=2)
        o_inter = jnp.einsum('bhtd,bhdv->bhtv', qb * jnp.exp(b), state)
        diff = b[:, :, :, None, :] - b[:, :, None, :, :]
        decay = jnp.exp(jnp.where(lower, diff, -jnp.inf))
        scores = jnp.einsum('bhtd,bhsd,bhtsd->bhts', qb, kb, decay)
        o_intra = jnp.einsum('bhts,bhsv->bhtv', scores, vb)
        b_last = b[:, :, -1:, :]
        state = jnp.exp(b_last[:, :, 0, :])[..., None] * state + jnp.einsum('bhsd,bhsv->bhdv', kb * jnp.exp(b_last - b), vb)
        return state, o_inter + o_intra

    s0 = jnp.zeros((B, H, DK, DV), jnp.float32)
    _, o = lax.scan(step, s0, (qc, kc, vc, fc))
    return o.transpose(1, 0, 3, 2, 4).reshape(B, S, H, DV)

def diff_attention(q, k, v, lam):
    B, S, H = q.shape[:3]
    nb = S // Q_BLOCK
    scale = DA_DK ** -0.5
    slopes = alibi_slopes(H)
    qb = jnp.moveaxis(q.transpose(0, 2, 3, 1, 4).reshape(B, H, 2, nb, Q_BLOCK, DA_DK), 3, 0)
    kt = k.transpose(0, 2, 3, 1, 4)
    vt = v.transpose(0, 2, 1, 3)
    pos_k = jnp.arange(S)

    def block(inp):
        qblk, idx = inp
        pos_q = idx * Q_BLOCK + jnp.arange(Q_BLOCK)
        dist = jnp.abs(pos_q[:, None] - pos_k[None, :]).astype(jnp.float32)
        bias = -slopes[:, None, None] * dist
        s = jnp.einsum('bhcqd,bhckd->bhcqk', qblk, kt).astype(jnp.float32) * scale + bias[None, :, None]
        p = jax.nn.softmax(s, axis=-1)
        attn = p[:, :, 0] - lam * p[:, :, 1]
        return jnp.einsum('bhqk,bhkv->bhqv', attn.astype(v.dtype), vt)

    o = lax.map(block, (qb, jnp.arange(nb)))
    return jnp.moveaxis(o, 0, 2).reshape(B, H, S, DA_DV).transpose(0, 2, 1, 3)

def memory_cross_attention(h, m, w_cq, w_ckv, w_co):
    B, S, D = h.shape
    q = (h @ w_cq).reshape(B, S, CA_HEADS, CA_DH)
    kv = m @ w_ckv
    k = kv[..., :D].reshape(B, N_MEM, CA_HEADS, CA_DH)
    v = kv[..., D:].reshape(B, N_MEM, CA_HEADS, CA_DH)
    s = jnp.einsum('bqhd,bkhd->bhqk', q, k).astype(jnp.float32) * (CA_DH ** -0.5)
    p = jax.nn.softmax(s, axis=-1).astype(v.dtype)
    o = jnp.einsum('bhqk,bkhd->bqhd', p, v).reshape(B, S, D)
    return o @ w_co

def hier_moe(h, w_rg, b_rg, w_re, b_re, w_gate, w_up, w_down):
    B, S, D = h.shape
    T = B * S
    xt = h.reshape(T, D)
    g_prob = jax.nn.softmax((xt @ w_rg).astype(jnp.float32) + b_rg.astype(jnp.float32), axis=-1)
    g_val, g_idx = lax.top_k(g_prob, 1)
    e_logits = ((xt @ w_re).astype(jnp.float32) + b_re.astype(jnp.float32)).reshape(T, N_GROUPS, EXP_PER_GROUP)
    e_in_group = e_logits[jnp.arange(T), g_idx[:, 0]]
    e_val, e_idx = lax.top_k(e_in_group, TOP_K)
    gate = g_val * jax.nn.softmax(e_val, axis=-1)
    expert = (g_idx * EXP_PER_GROUP + e_idx).reshape(-1)
    weight = gate.reshape(-1)
    token = jnp.repeat(jnp.arange(T, dtype=jnp.int32), TOP_K)
    n_assign = T * TOP_K
    order = jnp.argsort(expert)
    e_sorted, tok_sorted, w_sorted = expert[order], token[order], weight[order]
    counts = jnp.bincount(expert, length=N_EXPERTS)
    starts = jnp.cumsum(counts) - counts
    padded = (counts + MOE_BLOCK - 1) // MOE_BLOCK * MOE_BLOCK
    pad_end = jnp.cumsum(padded)
    pad_start = pad_end - padded
    dest = pad_start[e_sorted] + jnp.arange(n_assign) - starts[e_sorted]
    n_slots = (n_assign + MOE_BLOCK - 1) // MOE_BLOCK * MOE_BLOCK + N_EXPERTS * MOE_BLOCK
    slot_tok = jnp.full((n_slots,), T, dtype=jnp.int32).at[dest].set(tok_sorted)
    slot_w = jnp.zeros((n_slots,), jnp.float32).at[dest].set(w_sorted)
    nb = n_slots // MOE_BLOCK
    block_expert = jnp.minimum(jnp.searchsorted(pad_end, jnp.arange(nb) * MOE_BLOCK, side='right'), N_EXPERTS - 1)
    x_pad = jnp.concatenate([xt, jnp.zeros((1, D), xt.dtype)], axis=0)
    xs = x_pad[slot_tok].reshape(nb, MOE_BLOCK, D)

    def run(inp):
        xb, e = inp
        return (jax.nn.silu(xb @ w_gate[e]) * (xb @ w_up[e])) @ w_down[e]

    ys = lax.map(run, (xs, block_expert)).reshape(n_slots, D)
    out = jnp.zeros((T + 1, D), jnp.float32).at[slot_tok].add(ys.astype(jnp.float32) * slot_w[:, None])
    return out[:T].reshape(B, S, D).astype(h.dtype)

def encoder_layer(x, mem, l, p):
    B, S, _ = x.shape
    f32 = jnp.float32
    h = rms_norm(x, p['g_mix'][l])
    proj = h @ p['w_in'][l]
    widths = [HG_HEADS * HG_DK] * 3 + [HG_HEADS * HG_DV] * 2 + [DA_HEADS * 2 * DA_DK] * 2 + [DA_HEADS * DA_DV]
    points = np.cumsum(widths)[:-1].tolist()
    hq, hf_fwd, hf_bwd, hi, hg, dq, dk, dv = jnp.split(proj, points, axis=-1)

    lb = jnp.cumsum(jax.nn.softmax(p['hg_lb'].astype(f32), axis=0), axis=0)[l]

    def gates(fx):
        f = lb + (1.0 - lb) * jax.nn.sigmoid(fx.astype(f32))
        return jnp.log(f).reshape(B, S, HG_HEADS, HG_DK), (1.0 - f).reshape(B, S, HG_HEADS, HG_DK)

    q_hg = jax.nn.silu(hq.astype(f32)).reshape(B, S, HG_HEADS, HG_DK)
    i_hg = hi.astype(f32).reshape(B, S, HG_HEADS, HG_DV)
    lf_f, k_f = gates(hf_fwd)
    lf_b, k_b = gates(hf_bwd)
    o_fwd = hgrn2_chunk_scan(q_hg, k_f, i_hg, lf_f)
    o_bwd = jnp.flip(hgrn2_chunk_scan(jnp.flip(q_hg, 1), jnp.flip(k_b, 1), jnp.flip(i_hg, 1), jnp.flip(lf_b, 1)), 1)
    o_hg = head_rms(o_fwd + o_bwd, p['g_hg'][l].reshape(HG_HEADS, HG_DV)) * jax.nn.silu(hg.astype(f32)).reshape(B, S, HG_HEADS, HG_DV)

    lam_init = 0.8 - 0.6 * math.exp(-0.3 * l)
    lam = (jnp.exp(jnp.sum(p['lam_q1'][l].astype(f32) * p['lam_k1'][l].astype(f32)))
           - jnp.exp(jnp.sum(p['lam_q2'][l].astype(f32) * p['lam_k2'][l].astype(f32))) + lam_init)
    o_da = diff_attention(dq.reshape(B, S, DA_HEADS, 2, DA_DK), dk.reshape(B, S, DA_HEADS, 2, DA_DK),
                          dv.reshape(B, S, DA_HEADS, DA_DV), lam)
    o_da = head_rms(o_da, p['g_da'][l]) * (1.0 - lam_init)

    mix = jnp.concatenate([o_hg.reshape(B, S, HG_WIDTH), o_da.reshape(B, S, DA_WIDTH)], axis=-1).astype(x.dtype)
    x = x + mix @ p['w_out'][l]

    x = x + memory_cross_attention(rms_norm(x, p['g_ca'][l]), rms_norm(mem, p['g_mem'][l]),
                                   p['w_cq'][l], p['w_ckv'][l], p['w_co'][l])

    x = x + hier_moe(rms_norm(x, p['g_ffn'][l]), p['w_rg'][l], p['b_rg'][l], p['w_re'][l], p['b_re'][l],
                     p['w_gate'][l], p['w_up'][l], p['w_down'][l])
    return x

def encoder_trunk(x, mem, p):
    for l in range(DEPTH):
        x = encoder_layer(x, mem, l, p)
    return rms_norm(x, p['g_final'])

def setup_inputs(seed: int = 0) -> dict:
    key = jax.random.key(seed)
    ks = jax.random.split(key, 32)
    nrm = jax.random.normal
    f32 = jnp.float32

    def gain(k, shape):
        return 1.0 + 0.02 * nrm(k, shape, f32)

    return {
        'x_prompt': nrm(ks[0], (BATCH, SEQ, D_MODEL), f32),
        'x_sample': nrm(ks[1], (DEC_BATCH, DEC_SEQ, D_MODEL), f32),
        'mem_prompt': nrm(ks[2], (BATCH, N_MEM, D_MODEL), f32),
        'mem_sample': nrm(ks[3], (DEC_BATCH, N_MEM, D_MODEL), f32),
        'g_mix': gain(ks[4], (DEPTH, D_MODEL)),
        'w_in': nrm(ks[5], (DEPTH, D_MODEL, IN_COLS), f32) * D_MODEL ** -0.5,
        'hg_lb': 0.1 * nrm(ks[6], (DEPTH + 1, HG_HEADS * HG_DK), f32),
        'g_hg': gain(ks[7], (DEPTH, HG_HEADS * HG_DV)),
        'lam_q1': 0.1 * nrm(ks[8], (DEPTH, DA_DK), f32),
        'lam_k1': 0.1 * nrm(ks[9], (DEPTH, DA_DK), f32),
        'lam_q2': 0.1 * nrm(ks[10], (DEPTH, DA_DK), f32),
        'lam_k2': 0.1 * nrm(ks[11], (DEPTH, DA_DK), f32),
        'g_da': gain(ks[12], (DEPTH, DA_DV)),
        'w_out': nrm(ks[13], (DEPTH, MIX_WIDTH, D_MODEL), f32) * MIX_WIDTH ** -0.5,
        'g_ca': gain(ks[14], (DEPTH, D_MODEL)),
        'g_mem': gain(ks[15], (DEPTH, D_MODEL)),
        'w_cq': nrm(ks[16], (DEPTH, D_MODEL, D_MODEL), f32) * D_MODEL ** -0.5,
        'w_ckv': nrm(ks[17], (DEPTH, D_MODEL, 2 * D_MODEL), f32) * D_MODEL ** -0.5,
        'w_co': nrm(ks[18], (DEPTH, D_MODEL, D_MODEL), f32) * D_MODEL ** -0.5,
        'g_ffn': gain(ks[19], (DEPTH, D_MODEL)),
        'w_rg': nrm(ks[20], (DEPTH, D_MODEL, N_GROUPS), f32) * D_MODEL ** -0.5,
        'b_rg': 0.01 * nrm(ks[21], (DEPTH, N_GROUPS), f32),
        'w_re': nrm(ks[22], (DEPTH, D_MODEL, N_EXPERTS), f32) * D_MODEL ** -0.5,
        'b_re': 0.01 * nrm(ks[23], (DEPTH, N_EXPERTS), f32),
        'w_gate': nrm(ks[24], (DEPTH, N_EXPERTS, D_MODEL, D_EXPERT), f32) * D_MODEL ** -0.5,
        'w_up': nrm(ks[25], (DEPTH, N_EXPERTS, D_MODEL, D_EXPERT), f32) * D_MODEL ** -0.5,
        'w_down': nrm(ks[26], (DEPTH, N_EXPERTS, D_EXPERT, D_MODEL), f32) * D_EXPERT ** -0.5,
        'g_final': gain(ks[27], (D_MODEL,)),
    }

def reference(x_prompt, x_sample, mem_prompt, mem_sample, g_mix, w_in, hg_lb, g_hg, lam_q1, lam_k1, lam_q2, lam_k2,
              g_da, w_out, g_ca, g_mem, w_cq, w_ckv, w_co, g_ffn, w_rg, b_rg, w_re, b_re, w_gate, w_up, w_down, g_final):
    p = {'g_mix': g_mix, 'w_in': w_in, 'hg_lb': hg_lb, 'g_hg': g_hg, 'lam_q1': lam_q1, 'lam_k1': lam_k1,
         'lam_q2': lam_q2, 'lam_k2': lam_k2, 'g_da': g_da, 'w_out': w_out, 'g_ca': g_ca, 'g_mem': g_mem,
         'w_cq': w_cq, 'w_ckv': w_ckv, 'w_co': w_co, 'g_ffn': g_ffn, 'w_rg': w_rg, 'b_rg': b_rg, 'w_re': w_re,
         'b_re': b_re, 'w_gate': w_gate, 'w_up': w_up, 'w_down': w_down, 'g_final': g_final}
    y_prompt = encoder_trunk(x_prompt, mem_prompt, p)
    y_sample = encoder_trunk(x_sample, mem_sample, p)
    return (y_prompt, y_sample)


_drawn_inputs = setup_inputs


def setup_inputs(seed=0):
    import zlib

    import numpy as np

    out = dict(_drawn_inputs(seed))
    spreads = {}
    factors = {'hg_lb': 4.495,
     'g_hg': 3.741,
     'lam_k1': 5.238,
     'lam_q2': 5.681,
     'g_da': 3.013,
     'g_ca': 7.345,
     'g_mem': 6.88,
     'b_rg': 64.0,
     'b_re': 29.008,
     'g_final': 9.645,
     'g_ffn': 8.0}
    for name, (base, spread) in spreads.items():
        noise = np.random.default_rng([zlib.crc32(name.encode()), seed]).standard_normal(out[name].shape)
        drawn = base * np.exp(spread * noise) if base else spread * noise
        out[name] = __import__('jax').numpy.asarray(drawn.astype(out[name].dtype))
    for name, factor in factors.items():
        out[name] = (out[name] * factor).astype(out[name].dtype)
    return out
```

```python
import math
from contextlib import ExitStack

import concourse.bass as bass
from concourse import mybir

F32 = mybir.dt.float32
F32R = mybir.dt.float32r
I32 = mybir.dt.int32
U32 = mybir.dt.uint32
ALU = mybir.AluOpType
ACT = mybir.ActivationFunctionType
AX = mybir.AxisListType
ds = bass.ds

P = 128
D = 1024
KC = D // P
SEQ_P, SEQ_S, N_MEM = 1024, 256, 256
T = SEQ_P + SEQ_S
NT = T // P
NT_P = SEQ_P // P
EPS = 1e-6
HEADS = 4
HW = HEADS * P
DK = 64
DA_SCALE = DK ** -0.5
CA_DH = D // HEADS
CA_SCALE = CA_DH ** -0.5
N_GROUPS, EPG = 4, 8
N_EXP = N_GROUPS * EPG
D_EXP = 512
FC = D_EXP // P
MAX_BLOCKS = 2 * T // P + N_EXP
LAM_INIT = 0.8 - 0.6 * math.exp(-0.3 * 0)
ROW_Q, ROW_FF, ROW_FB, ROW_V, ROW_G, ROW_DQ, ROW_DK, ROW_DV = (HW * n for n in range(8))
TOKEN_GROUPS = [(0, 512), (512, 512), (1024, 256)]
PRIME = 2
ACT_SET = "natural_log_exp_and_others"


def free(n):
    return n + 1


def ready(n):
    return n + 1 + PRIME


def wait_apart(eng):
    eng.nop(nofuse=True)


class Mem:

    def __init__(self, nc, tag):
        self.nc, self.tag, self.stack, self.sems = nc, tag, ExitStack(), []

    def __enter__(self):
        return self

    def __exit__(self, *a):
        if self.sems and a[0] is None:
            self.nc.clear_and_free_semaphores(self.sems)
            self.nc.all_engine_barrier()
        return self.stack.__exit__(*a)

    def sb(self, name, shape, dt=F32):
        return self.stack.enter_context(self.nc.sbuf_tensor(f"{self.tag}_{name}", shape, dt))

    def ps(self, name, shape, dt=F32):
        return self.stack.enter_context(self.nc.psum_tensor(f"{self.tag}_{name}", shape, dt))

    def sem(self, name):
        self.sems.append(self.nc.alloc_semaphore(f"{self.tag}_{name}"))
        return self.sems[-1]


def product3(pe, out, lhs, rhs, first, last):
    pe.matmul(out, lhs[0], rhs[0], start=first, stop=False)
    pe.matmul(out, lhs[0], rhs[1], start=False, stop=False)
    return pe.matmul(out, lhs[1], rhs[0], start=False, stop=last)


def constants(nc, ident, eps):
    with Mem(nc, "const") as m:
        zero_done, done = m.sem("zero_done"), m.sem("done")
        with nc.Block() as block:
            @block.gpsimd
            def _(pool):
                pool.memset(ident[:], 0.0).then_inc(zero_done, 1)
                pool.wait_ge(zero_done, 1)
                pool.affine_select(out=ident[:], in_=ident[:], compare_op=ALU.not_equal, fill=1.0, base=0,
                                   pattern=[[-1, P]], channel_multiplier=1).then_inc(done, 1)
                pool.memset(eps[:], EPS).then_inc(done, 1)
                pool.wait_ge(done, 2)


def normed_transposed(nc, tag, sources, gain, ident, eps, high, low, rows_out=None):
    with Mem(nc, tag) as m:
        x = m.sb("x", [P, 2, D])
        xn = m.sb("xn", [P, 2, D])
        tmp = m.sb("tmp", [P, 2, D])
        junk = m.sb("junk", [P, D])
        g = m.sb("g", [P, KC])
        ss, lg, rstd = m.sb("ss", [P, 2]), m.sb("lg", [P, 2]), m.sb("rstd", [P, 2])
        xT = m.ps("xT", [P, 2, D])
        g_in = m.sem("g_in")
        x_in = [m.sem(f"x_in{u}") for u in range(2)]
        stored = [m.sem(f"stored{u}") for u in range(2)]
        rstd_done, xn_done, tr_done, tmp_done, high_done = (
            m.sem(s) for s in ("rstd_done", "xn_done", "tr_done", "tmp_done", "high_done"))
        pairs = sum(n for _, n in sources) // 2
        with nc.Block() as block:
            @block.sync
            def _(sp):
                with nc.allow_non_contiguous_dma(reason="a gain column of 1024 numbers"):
                    sp.dma_start(g[:], gain.rearrange("(k p) -> p k", p=P)).then_inc(g_in, 16)

                def load(i, rows, j):
                    for u in range(2):
                        sp.wait_ge(xn_done, free(2 * i + u))
                        sp.dma_start(x[:, u, :], rows[ds(j * (2 * P) + u * P, P), :]).then_inc(x_in[u], 16)

                at = 0
                for rows, tiles in sources:
                    if tiles > 2:
                        with sp.Fori(0, tiles // 2) as j:
                            load(j + at, rows, j)
                    else:
                        load(at, rows, 0)
                    at += tiles // 2

            @block.gpsimd
            def _(pool):
                if rows_out is None:
                    return
                with pool.Fori(0, pairs) as i:
                    for u in range(2):
                        pool.wait_ge(xn_done, ready(2 * i + u))
                        pool.dma_start(rows_out[ds(i * (2 * P) + u * P, P), :], xn[:, u, :]).then_inc(stored[u], 16)
                for u in range(2):
                    pool.wait_ge(stored[u], 16 * pairs)

            @block.scalar
            def _(act):
                act.preload_act_table_set(ACT_SET)
                act.sem_inc(rstd_done, PRIME)
                act.sem_inc(high_done, PRIME)
                with act.Fori(0, pairs) as i:
                    for u in range(2):
                        act.wait_ge(x_in[u], 16 * (i + 1))
                        act.activation(junk[:], x[:, u, :], ACT.Square, accum_out=ss[:, u:u + 1])
                        act.drain()
                    act.activation(lg[:], ss[:], ACT.Ln, scale=1.0 / D, bias=eps[:, 0:1])
                    act.drain()
                    act.activation(rstd[:], lg[:], ACT.Exp, scale=-0.5).then_inc(rstd_done, 2)
                    for u in range(2):
                        n = 2 * i + u
                        act.wait_ge(tmp_done, ready(n))
                        act.activation(high[:, :, ds(n * P, P)],
                                       tmp[:, u, :].rearrange("p (k t) -> p k t", k=KC),
                                       ACT.Copy).then_inc(high_done, 1)

            @block.vector
            def _(dve):
                dve.sem_inc(xn_done, PRIME)
                dve.sem_inc(tmp_done, PRIME)
                dve.wait_ge(g_in, 16)
                with dve.Fori(0, pairs) as i:
                    for u in range(2):
                        n = 2 * i + u
                        dve.wait_ge(rstd_done, 2 * i + 2 + PRIME)
                        dve.wait_ge(tr_done, free(n))
                        if rows_out is not None:
                            dve.wait_ge(stored[u], 16 * i)
                        dve.tensor_scalar(xn[:, u, :], x[:, u, :], rstd[:, u:u + 1], None,
                                          ALU.mult).then_inc(xn_done, 1)
                    for u in range(2):
                        n = 2 * i + u
                        dve.wait_ge(tr_done, ready(n))
                        dve.wait_ge(high_done, free(n))
                        dve.tensor_tensor(tmp[:, u, :].rearrange("p (k t) -> p k t", k=KC),
                                          xT[:, u, :].rearrange("p (k t) -> p k t", k=KC),
                                          g[:].unsqueeze(2).to_broadcast([P, KC, P]), ALU.mult).then_inc(tmp_done, 1)
                    for u in range(2):
                        n = 2 * i + u
                        dve.wait_ge(high_done, ready(n))
                        dve.tensor_tensor(low[:, :, ds(n * P, P)],
                                          tmp[:, u, :].rearrange("p (k t) -> p k t", k=KC),
                                          high[:, :, ds(n * P, P)].bitcast(F32), ALU.subtract)
                    dve.drain()

            @block.tensor
            def _(pe):
                pe.sem_inc(tr_done, PRIME)
                with pe.Fori(0, pairs) as i:
                    for u in range(2):
                        n = 2 * i + u
                        pe.wait_ge(xn_done, ready(n))
                        pe.wait_ge(tmp_done, free(n))
                        for k in range(KC):
                            last = pe.transpose(xT[:, u, k * P:(k + 1) * P], xn[:, u, k * P:(k + 1) * P], ident[:])
                        last.then_inc(tr_done, 1)


def project(nc, tag, weight, columns, high, low, groups, out_t):
    tokens = sum(n for _, n in groups)
    with Mem(nc, tag) as m:
        raw = m.sb("raw", [P, 2, KC, P])
        w_high = m.sb("w_high", [P, 2, KC, P], F32R)
        w_low = m.sb("w_low", [P, 2, KC, P], F32R)
        staged = m.sb("staged", [P, 2, tokens])
        acc = m.ps("acc", [P, 2, -(-tokens // 512) * 512])
        w_in = [m.sem(f"w_in{u}") for u in range(2)]
        stored = [m.sem(f"stored{u}") for u in range(2)]
        high_done, low_done, mm_done, staged_done = (
            m.sem(s) for s in ("high_done", "low_done", "mm_done", "staged_done"))
        pairs = columns // P // 2
        with nc.Block() as block:
            @block.sync
            def _(sp):
                with sp.Fori(0, pairs) as i:
                    for u in range(2):
                        sp.wait_ge(low_done, free(2 * i + u))
                        sp.dma_start(raw[:, u], weight[:, ds(i * (2 * P) + u * P, P)]
                                     .rearrange("(k p) n -> p k n", p=P)).then_inc(w_in[u], 16)

            @block.scalar
            def _(act):
                act.preload_act_table_set(ACT_SET)
                act.sem_inc(high_done, PRIME)
                act.sem_inc(staged_done, PRIME)

                def round_weight(i, u):
                    act.wait_ge(w_in[u], 16 * (i + 1))
                    act.wait_ge(mm_done, free(2 * i + u))
                    act.activation(w_high[:, u], raw[:, u], ACT.Copy).then_inc(high_done, 1)

                def stage(i, u):
                    act.wait_ge(mm_done, ready(2 * i + u))
                    act.wait_ge(stored[u], 16 * i)
                    act.activation(staged[:, u], acc[:, u, 0:tokens], ACT.Copy).then_inc(staged_done, 1)

                for u in range(2):
                    round_weight(0, u)
                with act.Fori(0, pairs - 1) as i:
                    for u in range(2):
                        stage(i, u)
                        round_weight(i + 1, u)
                for u in range(2):
                    stage(pairs - 1, u)

            @block.vector
            def _(dve):
                dve.sem_inc(low_done, PRIME)
                with dve.Fori(0, pairs) as i:
                    for u in range(2):
                        n = 2 * i + u
                        dve.wait_ge(high_done, ready(n))
                        dve.wait_ge(mm_done, free(n))
                        dve.tensor_tensor(w_low[:, u], raw[:, u], w_high[:, u].bitcast(F32),
                                          ALU.subtract).then_inc(low_done, 1)

            @block.tensor
            def _(pe):
                pe.sem_inc(mm_done, PRIME)
                with pe.Fori(0, pairs) as i:
                    for u in range(2):
                        n = 2 * i + u
                        pe.wait_ge(low_done, ready(n))
                        pe.wait_ge(staged_done, free(n))
                        for at, size in groups:
                            for k in range(KC):
                                last = product3(pe, acc[:, u, at:at + size], (w_high[:, u, k], w_low[:, u, k]),
                                                (high[:, k, at:at + size], low[:, k, at:at + size]),
                                                k == 0, k == KC - 1)
                        last.then_inc(mm_done, 1)

            @block.gpsimd
            def _(pool):
                with pool.Fori(0, pairs) as i:
                    for u in range(2):
                        pool.wait_ge(staged_done, ready(2 * i + u))
                        pool.dma_start(out_t[ds(i * (2 * P) + u * P, P), :], staged[:, u]).then_inc(stored[u], 16)
                for u in range(2):
                    pool.wait_ge(stored[u], 16 * pairs)


def lower_bound(nc, hg_lb, lb, one_minus_lb):
    with Mem(nc, "lb") as m:
        rows = m.sb("rows", [P, 2, HEADS])
        top = m.sb("top", [P, HEADS])
        e = m.sb("e", [P, 2, HEADS])
        total = m.sb("total", [P, HEADS])
        rows_in, shifted, exp_done = (m.sem(s) for s in ("rows_in", "shifted", "exp_done"))
        with nc.Block() as block:
            @block.sync
            def _(sp):
                with nc.allow_non_contiguous_dma(reason="a few columns of 128 numbers"):
                    for r in range(2):
                        sp.dma_start(rows[:, r], hg_lb[r].rearrange("(h p) -> p h", p=P)).then_inc(rows_in, 16)

            @block.vector
            def _(dve):
                dve.wait_ge(rows_in, 32)
                dve.tensor_tensor(top[:], rows[:, 0], rows[:, 1], ALU.max)
                dve.drain()
                dve.tensor_tensor(rows[:], rows[:], top[:].unsqueeze(1).to_broadcast([P, 2, HEADS]),
                                  ALU.subtract).then_inc(shifted, 1)
                dve.wait_ge(exp_done, 1)
                dve.tensor_tensor(total[:], e[:, 0], e[:, 1], ALU.add)
                dve.drain()
                dve.reciprocal(total[:], total[:])
                dve.drain()
                dve.tensor_tensor(lb[:], e[:, 0], total[:], ALU.mult)
                dve.drain()
                dve.tensor_scalar(one_minus_lb[:], lb[:], -1.0, 1.0, ALU.mult, ALU.add)

            @block.scalar
            def _(act):
                act.preload_act_table_set(ACT_SET)
                act.wait_ge(shifted, 1)
                act.activation(e[:], rows[:], ACT.Exp).then_inc(exp_done, 1)


LEVELS = (64, 32, 16)
CENTRE = LEVELS[-1] // 2 - 1


def hgrn(nc, tag, proj_t, row_f, forward, lb, one_minus_lb, ident, o_out):
    n_lev = len(LEVELS)
    base = LEVELS[-1]
    early, late = (0, 1) if forward else (1, 0)
    last_t = P - 1 if forward else 0

    def half_ref(half_width):
        return half_width - 1 if forward else 0

    with Mem(nc, tag) as m:
        x = m.sb("x", [P, 2, 3, HEADS, P])
        sig = m.sb("sig", [P, 2, 2, HW])
        q = m.sb("q", [P, 2, HW])
        k = m.sb("k", [P, 2, HW])
        f = m.sb("f", [P, 2, HW])
        lf = m.sb("lf", [P, 2, HEADS, P])
        b = m.sb("b", [P, 2, HEADS, P])
        diff = m.sb("diff", [P, 2, n_lev + 2, HW])
        decay = m.sb("decay", [P, 2, n_lev + 2, HW])
        uncentre = m.sb("uncentre", [P, 2, HW])
        from_start = m.sb("from_start", [P, 2, HW])
        q_dec = m.sb("q_dec", [P, 2, n_lev + 2, HW])
        k_dec = m.sb("k_dec", [P, 2, n_lev + 2, HW])
        v = m.sb("v", [P, 2, HW])
        k_tok = m.sb("k_tok", [P, HW])
        s_t = m.sb("s_t", [P, HW])
        state = m.sb("state", [P, HW])
        o = m.sb("o", [P, 2, HW])
        where = m.sb("where", [P, n_lev, HW])
        where_i = m.sb("where_i", [P, n_lev, HW], I32)
        v_ps, kt_ps, o_ps, st_ps = (m.ps(s, [P, HW]) for s in ("v_ps", "kt_ps", "o_ps", "st_ps"))
        s_ps = m.ps("s_ps", [P, n_lev + 1, HW])
        x_in = [m.sem(f"x_in{u}") for u in range(2)]
        o_stored = [m.sem(f"o_stored{u}") for u in range(2)]
        (ones_done, where_done, where_i_done, e_done, f_done, lf_done, diff_done, decay_done, base_done,
         levels_done, v_ready, v_done, scores_ready, s_done, kt_done, o_ready, o_done, state_done) = (
            m.sem(s) for s in (
                "ones_done", "where_done", "where_i_done", "e_done", "f_done", "lf_done", "diff_done",
                "decay_done", "base_done", "levels_done", "v_ready", "v_done", "scores_ready", "s_done",
                "kt_done", "o_ready", "o_done", "state_done"))

        def skewed(eng, front, back):
            front(0, 0)
            with eng.Fori(0, NT // 2 - 1) as i:
                for u in range(2):
                    front(i + u, 1 - u)
                    back(i, u)
            front(NT // 2 - 1, 1)
            for u in range(2):
                back(NT // 2 - 1, u)

        def token(i, u):
            return i * (2 * P) + u * P if forward else i * (-2 * P) + (NT - 1 - u) * P

        with nc.Block() as block:
            @block.sync
            def _(sp):
                def load(i, u):
                    sp.wait_ge(f_done, free(2 * i + u))
                    sp.wait_ge(v_ready, free(2 * i + u))
                    for j, row in enumerate((ROW_Q, row_f, ROW_V)):
                        sp.dma_start(x[:, u, j], proj_t[row:row + HW, ds(token(i, u), P)]
                                     .rearrange("(h p) t -> p h t", p=P)).then_inc(x_in[u], 16)

                def store(i, u):
                    sp.wait_ge(o_done, 2 * i + u + 1)
                    sp.dma_start(o_out[ds(token(i, u), P), :], o[:, u]).then_inc(o_stored[u], 16)

                for u in range(2):
                    load(0, u)
                with sp.Fori(0, NT // 2 - 1) as i:
                    for u in range(2):
                        store(i, u)
                        load(i + 1, u)
                for u in range(2):
                    store(NT // 2 - 1, u)
                for u in range(2):
                    sp.wait_ge(o_stored[u], 16 * (NT // 2))

            @block.gpsimd
            def _(pool):
                pool.memset(where[:], 1.0).then_inc(ones_done, 1)
                pool.memset(q_dec[:, :, 0:n_lev], 0.0).then_inc(ones_done, 1)
                pool.memset(k_dec[:, :, 0:n_lev], 0.0).then_inc(ones_done, 1)
                pool.wait_ge(ones_done, 3)
                count = 0
                for j, w in enumerate(LEVELS[1:] + (base // 2,)):
                    pair = 2 * w
                    view = where[:, j].rearrange("p (h m l) -> p h m l", h=HEADS, l=pair)
                    sides = [(0, 1, [[0, HEADS], [-pair, P // pair], [0, pair]]),
                             (pair - 1, -1, [[0, HEADS], [pair, P // pair], [0, pair]])]
                    if w == base // 2:
                        sides.append((0, -1, [[0, HEADS], [pair, P // pair], [1, pair]]) if forward else
                                     (0, 1, [[0, HEADS], [-pair, P // pair], [-1, pair]]))
                    for start, mult, pattern in sides:
                        pool.affine_select(out=view, in_=view, compare_op=ALU.is_ge, fill=0.0, base=start,
                                           pattern=pattern, channel_multiplier=mult).then_inc(where_done, 1)
                        count += 1
                        pool.wait_ge(where_done, count)
                pool.tensor_copy(where_i[:], where[:]).then_inc(where_i_done, 1)

                def levels(i, u):
                    n = 2 * i + u
                    pool.wait_ge(decay_done, n + 1)
                    for j, w in enumerate(LEVELS):
                        halves = lambda t: t.rearrange("p (g two l) -> p g two l", two=2, l=w)
                        e, qd, kd = (halves(t[:, u, j]) for t in (decay, q_dec, k_dec))
                        pool.tensor_tensor(qd[:, :, late], e[:, :, late], halves(q[:, u])[:, :, late], ALU.mult)
                        done = pool.tensor_tensor(kd[:, :, early], e[:, :, early], halves(k[:, u])[:, :, early],
                                                  ALU.mult)
                    done.then_inc(levels_done, 1)

                with pool.Fori(0, NT // 2) as i:
                    for u in range(2):
                        levels(i, u)

            @block.scalar
            def _(act):
                act.preload_act_table_set(ACT_SET)

                def front(i, u):
                    n = 2 * i + u
                    act.wait_ge(state_done, free(n))
                    act.wait_ge(x_in[u], 48 * (i + 1))
                    act.activation(sig[:, u], x[:, u, 0:2].rearrange("p a h t -> p a (h t)"), ACT.Exp,
                                   scale=-1.0).then_inc(e_done, 1)
                    act.wait_ge(v_ready, ready(n))
                    act.activation(v[:, u], v_ps[:], ACT.Copy).then_inc(v_done, 1)
                    act.wait_ge(f_done, ready(n))
                    act.activation(lf[:, u].rearrange("p h t -> p (h t)"), f[:, u], ACT.Ln).then_inc(lf_done, 1)
                    act.wait_ge(diff_done, n + 1)
                    act.activation(decay[:, u], diff[:, u], ACT.Exp)
                    act.activation(uncentre[:, u], diff[:, u, n_lev + 1], ACT.Exp, scale=-1.0)
                    act.activation(from_start[:, u], b[:, u].rearrange("p h t -> p (h t)"),
                                   ACT.Exp).then_inc(decay_done, 1)

                def back(i, u):
                    n = 2 * i + u
                    act.wait_ge(scores_ready, n + 1)
                    act.activation(k_tok[:], kt_ps[:], ACT.Copy).then_inc(kt_done, 1)
                    act.wait_ge(o_ready, n + 1)
                    act.wait_ge(o_stored[u], 16 * i)
                    act.activation(o[:, u], o_ps[:], ACT.Copy).then_inc(o_done, 1)

                skewed(act, front, back)

            @block.vector
            def _(dve):
                dve.sem_inc(f_done, PRIME)
                dve.sem_inc(state_done, PRIME)
                dve.memset(state[:], 0.0)
                dve.wait_ge(where_i_done, 1)
                dve.drain()

                def front(i, u):
                    n = 2 * i + u
                    dve.wait_ge(e_done, n + 1)
                    dve.tensor_scalar(sig[:, u], sig[:, u], 1.0, None, ALU.add)
                    dve.drain()
                    dve.reciprocal(sig[:, u], sig[:, u])
                    dve.drain()
                    dve.tensor_tensor(q[:, u], sig[:, u, 0], x[:, u, 0].rearrange("p h t -> p (h t)"), ALU.mult)
                    for h in range(HEADS):
                        cols = slice(h * P, (h + 1) * P)
                        done = dve.tensor_scalar(f[:, u, cols], sig[:, u, 1, cols], one_minus_lb[:, h:h + 1],
                                                 lb[:, h:h + 1], ALU.mult, ALU.add)
                    done.then_inc(f_done, 1)
                    dve.drain()
                    dve.tensor_scalar(k[:, u], f[:, u], -1.0, 1.0, ALU.mult, ALU.add)
                    dve.wait_ge(lf_done, n + 1)
                    for h in range(HEADS):
                        src, dst = lf[:, u, h], b[:, u, h]
                        if not forward:
                            src, dst = src[:, ::-1], dst[:, ::-1]
                        dve.tensor_tensor_scan(dst, src, src, 0.0, ALU.add, ALU.bypass)
                    dve.drain()
                    for j, w in enumerate(LEVELS):
                        bv = b[:, u].rearrange("p h (m two l) -> p (h m) two l", two=2, l=w)
                        dv = diff[:, u, j].rearrange("p (g two l) -> p g two l", two=2, l=w)
                        at = half_ref(w)
                        ref = bv[:, :, early, at:at + 1].to_broadcast([P, HW // (2 * w), w])
                        dve.tensor_tensor(dv[:, :, late], bv[:, :, late], ref, ALU.subtract)
                        dve.tensor_tensor(dv[:, :, early], ref, bv[:, :, early], ALU.subtract)
                    dve.tensor_tensor(diff[:, u, n_lev].rearrange("p (h t) -> p h t", h=HEADS),
                                      b[:, u, :, last_t:last_t + 1].to_broadcast([P, HEADS, P]), b[:, u],
                                      ALU.subtract)
                    bv = b[:, u].rearrange("p h (m l) -> p (h m) l", l=base)
                    dve.tensor_tensor(diff[:, u, n_lev + 1].rearrange("p (g l) -> p g l", l=base), bv,
                                      bv[:, :, CENTRE:CENTRE + 1].to_broadcast([P, HW // base, base]),
                                      ALU.subtract).then_inc(diff_done, 1)
                    dve.wait_ge(decay_done, n + 1)
                    dve.tensor_tensor(q_dec[:, u, n_lev], q[:, u], decay[:, u, n_lev + 1], ALU.mult)
                    dve.tensor_tensor(k_dec[:, u, n_lev], k[:, u], uncentre[:, u], ALU.mult)
                    dve.tensor_tensor(q_dec[:, u, n_lev + 1], q[:, u], from_start[:, u], ALU.mult)
                    dve.tensor_tensor(k_dec[:, u, n_lev + 1], k[:, u], decay[:, u, n_lev],
                                      ALU.mult).then_inc(base_done, 1)

                def back(i, u, anew=False):
                    n = 2 * i + u
                    dve.wait_ge(scores_ready, n + 1)
                    dve.tensor_copy(s_t[:], s_ps[:, 0])
                    for j in range(n_lev):
                        dve.drain()
                        done = dve.copy_predicated(s_t[:], where_i[:, j], s_ps[:, j + 1])
                    done.then_inc(s_done, 1)
                    dve.wait_ge(o_ready, n + 1)
                    if anew:
                        done = dve.memset(state[:], 0.0)
                    else:
                        for h in range(HEADS):
                            cols = slice(h * P, (h + 1) * P)
                            at = h * P + last_t
                            done = dve.scalar_tensor_tensor(state[:, cols], state[:, cols],
                                                            from_start[:, u, at:at + 1], st_ps[:, cols],
                                                            ALU.mult, ALU.add)
                    done.then_inc(state_done, 1)

                last = NT // 2 - 1
                new_after = NT_P - 1 if forward else NT - NT_P - 1
                out_at = new_after // 2

                def pair(i, u_anew=None, final=False):
                    for u in range(2):
                        if not (final and u == 1):
                            front(i + u, 1 - u)
                        back(i, u, u == u_anew)

                front(0, 0)
                if out_at > 0:
                    with dve.Fori(0, out_at) as i:
                        pair(i)
                pair(out_at, new_after % 2)
                if out_at + 1 < last:
                    with dve.Fori(out_at + 1, last) as i:
                        pair(i)
                pair(last, final=True)

            @block.tensor
            def _(pe):
                pe.sem_inc(v_ready, PRIME)
                pe.wait_ge(ones_done, 3)

                def front(i, u):
                    n = 2 * i + u
                    pe.wait_ge(x_in[u], 48 * (i + 1))
                    pe.wait_ge(v_done, n)
                    for h in range(HEADS):
                        done = pe.transpose(v_ps[:, h * P:(h + 1) * P], x[:, u, 2, h], ident[:])
                    done.then_inc(v_ready, 1)

                def back(i, u):
                    n = 2 * i + u
                    pe.wait_ge(base_done, n + 1)
                    pe.wait_ge(levels_done, n + 1)
                    pe.wait_ge(s_done, n)
                    for j in range(n_lev + 1):
                        for h in range(HEADS):
                            cols = slice(h * P, (h + 1) * P)
                            pe.matmul(s_ps[:, j, cols], k_dec[:, u, j, cols], q_dec[:, u, j, cols],
                                      start=True, stop=True)
                    pe.wait_ge(kt_done, n)
                    for h in range(HEADS):
                        cols = slice(h * P, (h + 1) * P)
                        done = pe.transpose(kt_ps[:, cols], k_dec[:, u, n_lev + 1, cols], ident[:])
                    done.then_inc(scores_ready, 1)
                    pe.wait_ge(v_done, n + 1)
                    pe.wait_ge(kt_done, n + 1)
                    pe.wait_ge(state_done, n + PRIME)
                    pe.wait_ge(s_done, n + 1)
                    pe.wait_ge(o_done, n)
                    for h in range(HEADS):
                        cols = slice(h * P, (h + 1) * P)
                        pe.matmul(st_ps[:, cols], k_tok[:, cols], v[:, u, cols], start=True, stop=True)
                    for h in range(HEADS):
                        cols = slice(h * P, (h + 1) * P)
                        pe.matmul(o_ps[:, cols], q_dec[:, u, n_lev + 1, cols], state[:, cols],
                                  start=True, stop=False)
                        done = pe.matmul(o_ps[:, cols], s_t[:, cols], v[:, u, cols], start=False, stop=True)
                    done.then_inc(o_ready, 1)

                skewed(pe, front, back)


def lambda_of(nc, q1, k1, q2, k2, lam):
    with Mem(nc, "lam") as m:
        vecs = m.sb("vecs", [DK, 4])
        prods = m.sb("prods", [DK, 2])
        ones = m.sb("ones", [DK, P])
        e = m.sb("e", [P, 2])
        sums = m.ps("sums", [P, 2])
        vecs_in, prods_done, sums_done, exp_done = (
            m.sem(s) for s in ("vecs_in", "prods_done", "sums_done", "exp_done"))
        with nc.Block() as block:
            @block.sync
            def _(sp):
                with nc.allow_non_contiguous_dma(reason="four columns of 64 numbers"):
                    for j, vec in enumerate((q1, q2, k1, k2)):
                        sp.dma_start(vecs[:, j:j + 1], vec.rearrange("(p a) -> p a", a=1)).then_inc(vecs_in, 16)

            @block.vector
            def _(dve):
                dve.memset(ones[:], 1.0)
                dve.wait_ge(vecs_in, 64)
                dve.tensor_tensor(prods[:], vecs[:, 0:2], vecs[:, 2:4], ALU.mult).then_inc(prods_done, 1)
                dve.wait_ge(exp_done, 1)
                dve.tensor_tensor(lam[:], e[:, 0:1], e[:, 1:2], ALU.subtract)
                dve.drain()
                dve.tensor_scalar(lam[:], lam[:], LAM_INIT, None, ALU.add)

            @block.tensor
            def _(pe):
                pe.wait_ge(prods_done, 1)
                pe.matmul(sums[:], ones[:], prods[:], start=True, stop=True).then_inc(sums_done, 1)

            @block.scalar
            def _(act):
                act.preload_act_table_set(ACT_SET)
                act.wait_ge(sums_done, 1)
                act.activation(e[:], sums[:], ACT.Exp).then_inc(exp_done, 1)


def diff_attention(nc, tag, proj_t, first, seq, g_da, lam, ident, eps, mix_out):
    nk = seq // P
    slopes = [2.0 ** (-8.0 * (h + 1) / HEADS) for h in range(HEADS)]
    width = 2 * seq - P
    banks = [(at, min(512, seq)) for at in range(0, seq, 512)]
    with Mem(nc, tag) as m:
        keys = m.sb("keys", [DK, 2, HEADS * seq])
        v_t = m.sb("v_t", [P, HEADS, seq])
        v = m.sb("v", [P, nk, HW])
        where = m.sb("where", [P, width])
        bias = m.sb("bias", [P, width])
        gain = m.sb("gain", [P, P])
        query = m.sb("query", [DK, 2, 2, P])
        scaled = m.sb("scaled", [DK, 2, 2, P])
        q_factor, slope, minus_slope = (m.sb(s, [P, HEADS]) for s in ("q_factor", "slope", "minus_slope"))
        score = m.sb("score", [P, 2, 2, seq])
        prob = m.sb("prob", [P, 2, 2, seq])
        attn_t = m.sb("attn_t", [P, seq])
        top = m.sb("top", [P, 2, 2])
        total = m.sb("total", [P, 2, 2])
        o_in = m.sb("o_in", [P, P])
        sq = m.sb("sq", [P, P])
        ss, rstd = m.sb("ss", [P, 1]), m.sb("rstd", [P, 1])
        o = m.sb("o", [P, 2, P])
        score_ps = m.ps("score_ps", [P, 2, max(512, seq)])
        attn_ps = m.ps("attn_ps", [P, max(512, seq)])
        o_ps = m.ps("o_ps", [P, 512])
        q_in = [m.sem(f"q_in{u}") for u in range(2)]
        stored = [m.sem(f"stored{u}") for u in range(2)]
        (loaded, slopes_done, where_done, q_done, v_ready, v_done, scores_ready, top_done, prob_done,
         attn_done, attn_t_ready, attn_t_done, o_ready, o_in_done, rstd_done, o_done) = (m.sem(s) for s in (
             "loaded", "slopes_done", "where_done", "q_done", "v_ready", "v_done", "scores_ready", "top_done",
             "prob_done", "attn_done", "attn_t_ready", "attn_t_done", "o_ready", "o_in_done", "rstd_done",
             "o_done"))
        per_buffer = HEADS * nk // 2

        def skewed(eng, front, back):
            def head(h, final=False):
                for t in range(nk):
                    if t + 1 < nk:
                        front(h, t + 1)
                    elif not final:
                        front(h + 1, 0)
                    back(h, t)

            front(0, 0)
            with eng.Fori(0, HEADS - 1) as h:
                head(h)
            head(HEADS - 1, final=True)

        def step(h, t):
            return h * nk + t

        def uses(h, t):
            return h * (nk // 2) + t // 2

        with nc.Block() as block:
            @block.sync
            def _(sp):
                for c in range(2):
                    sp.dma_start(keys[:, c].rearrange("p (h t) -> p h t", h=HEADS),
                                 proj_t[ROW_DK:ROW_DK + HW, first:first + seq]
                                 .rearrange("(h c p) t -> c p h t", c=2, p=DK)[c]).then_inc(loaded, 16)
                sp.dma_start(v_t[:], proj_t[ROW_DV:ROW_DV + HW, first:first + seq]
                             .rearrange("(h p) t -> p h t", p=P)).then_inc(loaded, 16)
                with nc.allow_non_contiguous_dma(reason="one row for all partitions"):
                    sp.dma_start(gain[:], g_da.rearrange("(a n) -> a n", a=1).to_broadcast([P, P])).then_inc(loaded, 16)

                def load(h, t):
                    u = t % 2
                    sp.wait_ge(q_done, free(step(h, t)))
                    sp.dma_start(query[:, u], proj_t[ds(h * P + ROW_DQ, P), first + t * P:first + (t + 1) * P]
                                 .rearrange("(c p) t -> p c t", p=DK)).then_inc(q_in[u], 16)

                with sp.Fori(0, HEADS) as h:
                    for t in range(nk):
                        load(h, t)

            @block.gpsimd
            def _(pool):
                pool.iota(where[:], [[-1, width]], base=seq - P, channel_multiplier=1,
                          allow_small_or_imprecise_dtypes=True).then_inc(where_done, 1)
                with pool.Fori(0, HEADS) as h:
                    for t in range(nk):
                        pool.wait_ge(o_done, step(h, t) + 1)
                        pool.dma_start(mix_out[first + t * P:first + (t + 1) * P, ds(h * P + HW, P)],
                                       o[:, t % 2]).then_inc(stored[t % 2], 16)
                for u in range(2):
                    pool.wait_ge(stored[u], 16 * per_buffer)

            @block.vector
            def _(dve):
                dve.sem_inc(attn_done, PRIME)
                dve.sem_inc(q_done, PRIME)
                for h in range(HEADS):
                    dve.memset(q_factor[:, h:h + 1], DA_SCALE / slopes[h])
                    dve.memset(slope[:, h:h + 1], slopes[h])
                    last = dve.memset(minus_slope[:, h:h + 1], -slopes[h])
                last.then_inc(slopes_done, 1)
                dve.wait_ge(where_done, 1)
                dve.scalar_tensor_tensor(bias[:], where[:], -1.0, where[:], ALU.mult, ALU.min)
                dve.wait_ge(loaded, 64)
                dve.tensor_scalar(gain[:], gain[:], 1.0 - LAM_INIT, None, ALU.mult)
                dve.drain()

                def scale_query(h, t):
                    u = t % 2
                    dve.wait_ge(q_in[u], uses(h, t) * 16 + 16)
                    dve.wait_ge(scores_ready, free(step(h, t)))
                    dve.tensor_scalar(scaled[:, u], query[:, u], q_factor[0:DK, ds(h, 1)], None,
                                      ALU.mult).then_inc(q_done, 1)

                def front(h, t):
                    n, u = step(h, t), t % 2
                    if t + 1 < nk:
                        scale_query(h, t + 1)
                    dve.wait_ge(scores_ready, ready(n))
                    wait_apart(dve)
                    col = seq - P - t * P
                    for c in range(2):
                        dve.tensor_tensor_reduce(out=score[:, u, c], in0=score_ps[:, c, 0:seq],
                                                 in1=bias[:, col:col + seq], scale=1.0, scalar=-3.0e38,
                                                 op0=ALU.add, op1=ALU.max, accum_out=top[:, u, c:c + 1])
                    dve.drain()
                    dve.tensor_scalar(top[:, u], top[:, u], minus_slope[:, ds(h, 1)], None,
                                      ALU.mult).then_inc(top_done, 1)

                def back(h, t):
                    n, u = step(h, t), t % 2
                    dve.wait_ge(prob_done, n + 1)
                    dve.reciprocal(total[:, u], total[:, u])
                    dve.drain()
                    dve.tensor_tensor(total[:, u, 1:2], total[:, u, 1:2], lam[:], ALU.mult)
                    dve.drain()
                    dve.tensor_scalar(prob[:, u, 1], prob[:, u, 1], total[:, u, 1:2], None, ALU.mult)
                    dve.drain()
                    dve.scalar_tensor_tensor(prob[:, u, 0], prob[:, u, 0], total[:, u, 0:1], prob[:, u, 1],
                                             ALU.mult, ALU.subtract).then_inc(attn_done, 1)
                    dve.wait_ge(o_ready, n + 1)
                    dve.tensor_copy(o_in[:], o_ps[:, 0:P]).then_inc(o_in_done, 1)
                    dve.wait_ge(rstd_done, n + 1)
                    dve.wait_ge(stored[u], uses(h, t) * 16)
                    dve.scalar_tensor_tensor(o[:, u], o_in[:], rstd[:, 0:1], gain[:], ALU.mult,
                                             ALU.mult).then_inc(o_done, 1)

                def front_of_head(h, t):
                    if t == 0:
                        scale_query(h, 0)
                    front(h, t)

                skewed(dve, front_of_head, back)

            @block.scalar
            def _(act):
                act.preload_act_table_set(ACT_SET)
                act.wait_ge(slopes_done, 1)
                for t in range(nk):
                    act.wait_ge(v_ready, t + 1)
                    act.activation(v[:, t], attn_ps[:, 0:HW], ACT.Copy).then_inc(v_done, 1)

                def front(h, t):
                    n, u = step(h, t), t % 2
                    act.wait_ge(top_done, n + 1)
                    act.wait_ge(attn_t_ready, free(n))
                    wait_apart(act)
                    for c in range(2):
                        done = act.activation(prob[:, u, c], score[:, u, c], ACT.Exp, scale=slope[:, ds(h, 1)],
                                              bias=top[:, u, c:c + 1], accum_out=total[:, u, c:c + 1])
                    done.then_inc(prob_done, 1)

                def back(h, t):
                    n = step(h, t)
                    act.wait_ge(attn_t_ready, ready(n))
                    act.activation(attn_t[:], attn_ps[:, 0:seq], ACT.Copy).then_inc(attn_t_done, 1)
                    act.wait_ge(o_in_done, n + 1)
                    act.activation(sq[:], o_in[:], ACT.Square, accum_out=ss[:])
                    act.drain()
                    act.activation(rstd[:], ss[:], ACT.Ln, scale=1.0 / P, bias=eps[:, 0:1])
                    act.drain()
                    act.activation(rstd[:], rstd[:], ACT.Exp, scale=-0.5).then_inc(rstd_done, 1)

                skewed(act, front, back)

            @block.tensor
            def _(pe):
                pe.sem_inc(scores_ready, PRIME)
                pe.sem_inc(attn_t_ready, PRIME)
                pe.wait_ge(loaded, 64)
                for t in range(nk):
                    pe.wait_ge(v_done, t)
                    for h in range(HEADS):
                        last = pe.transpose(attn_ps[:, h * P:(h + 1) * P], v_t[:, h, t * P:(t + 1) * P], ident[:])
                    last.then_inc(v_ready, 1)
                pe.wait_ge(v_done, nk)

                def front(h, t):
                    n, u = step(h, t), t % 2
                    pe.wait_ge(q_done, ready(n))
                    pe.wait_ge(top_done, n)
                    wait_apart(pe)
                    for c in range(2):
                        for at, size in banks:
                            last = pe.matmul(score_ps[:, c, at:at + size], scaled[:, u, c],
                                             keys[:, c, ds(h * seq + at, size)], start=True, stop=True)
                    last.then_inc(scores_ready, 1)

                def back(h, t):
                    n, u = step(h, t), t % 2
                    pe.wait_ge(attn_done, ready(n))
                    pe.wait_ge(attn_t_done, n)
                    for c in range(nk):
                        last = pe.transpose(attn_ps[:, c * P:(c + 1) * P], prob[:, u, 0, c * P:(c + 1) * P], ident[:])
                    last.then_inc(attn_t_ready, 1)
                    pe.wait_ge(attn_t_done, n + 1)
                    pe.wait_ge(o_in_done, n)
                    for c in range(nk):
                        last = pe.matmul(o_ps[:, 0:P], attn_t[:, c * P:(c + 1) * P], v[:, c, ds(h * P, P)],
                                         start=(c == 0), stop=(c == nk - 1))
                    last.then_inc(o_ready, 1)

                skewed(pe, front, back)


def split_weight(nc, tag, weight, high, low):
    with Mem(nc, tag) as m:
        raw = m.sb("raw", [P, 2, D])
        w_in = [m.sem(f"w_in{u}") for u in range(2)]
        high_done, low_done = m.sem("high_done"), m.sem("low_done")
        with nc.Block() as block:
            @block.sync
            def _(sp):
                for k in range(KC):
                    sp.wait_ge(low_done, free(k))
                    sp.dma_start(raw[:, k % 2], weight[k * P:(k + 1) * P, :]).then_inc(w_in[k % 2], 16)

            @block.scalar
            def _(act):
                act.preload_act_table_set(ACT_SET)
                for k in range(KC):
                    act.wait_ge(w_in[k % 2], 16 * (k // 2 + 1))
                    act.activation(high[:, k], raw[:, k % 2], ACT.Copy).then_inc(high_done, 1)

            @block.vector
            def _(dve):
                dve.sem_inc(low_done, PRIME)
                for k in range(KC):
                    dve.wait_ge(high_done, k + 1)
                    dve.tensor_tensor(low[:, k], raw[:, k % 2], high[:, k].bitcast(F32),
                                      ALU.subtract).then_inc(low_done, 1)


def tile_pairs(eng, body, sources):
    at = 0
    for rows, tiles in sources:
        if tiles > 2:
            with eng.Fori(0, tiles // 2) as j:
                body(j + at, rows, j)
        else:
            body(at, rows, 0)
        at += tiles // 2


def skewed_pairs(eng, front, back):
    last = NT // 2 - 1
    front(0, 0)
    with eng.Fori(0, last) as i:
        for u in range(2):
            front(i + u, 1 - u)
            back(i, u)
    front(last, 1)
    for u in range(2):
        back(last, u)


def mix_out(nc, tag, o_fwd, o_bwd, proj_t, mix, x_rows, g_hg, w_high, w_low, ident, eps, x1_out):
    with Mem(nc, tag) as m:
        of = m.sb("of", [P, 2, HW])
        ob = m.sb("ob", [P, 2, HW])
        gate_t = m.sb("gate_t", [P, 2, HEADS, P])
        mixed = m.sb("mixed", [P, 2, D])
        x = m.sb("x", [P, 2, D])
        gain = m.sb("gain", [P, HW])
        e = m.sb("e", [P, HW])
        sq = m.sb("sq", [P, HW])
        silu = m.sb("silu", [P, HW])
        ss, rstd = m.sb("ss", [P, HEADS]), m.sb("rstd", [P, HEADS])
        m_high, m_low = m.sb("m_high", [P, KC, P], F32R), m.sb("m_low", [P, KC, P], F32R)
        x1 = m.sb("x1", [P, 2, D])
        gate_ps = m.ps("gate_ps", [P, HW])
        mt_ps = m.ps("mt_ps", [P, D])
        out_ps = m.ps("out_ps", [P, 2, D])
        t_in = [m.sem(f"t_in{u}") for u in range(2)]
        stored = [m.sem(f"stored{u}") for u in range(2)]
        (gain_in, gate_ready, e_done, ss_done, rstd_done, mixed_done, mt_ready, high_done, low_done, out_ready,
         x1_done) = (m.sem(s) for s in ("gain_in", "gate_ready", "e_done", "ss_done", "rstd_done", "mixed_done",
                                        "mt_ready", "high_done", "low_done", "out_ready", "x1_done"))
        with nc.Block() as block:
            @block.sync
            def _(sp):
                with nc.allow_non_contiguous_dma(reason="one row for all partitions"):
                    sp.dma_start(gain[:], g_hg.rearrange("(a n) -> a n", a=1).to_broadcast([P, HW])).then_inc(gain_in, 16)

                def load(i, rows, j):
                    for u in range(2):
                        n = 2 * i + u
                        t = ds(i * (2 * P) + u * P, P)
                        sp.wait_ge(mt_ready, free(n))
                        sp.wait_ge(x1_done, free(n))
                        sp.dma_start(of[:, u], o_fwd[t, :]).then_inc(t_in[u], 16)
                        sp.dma_start(ob[:, u], o_bwd[t, :]).then_inc(t_in[u], 16)
                        sp.dma_start(gate_t[:, u], proj_t[ROW_G:ROW_G + HW, t]
                                     .rearrange("(h p) t -> p h t", p=P)).then_inc(t_in[u], 16)
                        sp.dma_start(mixed[:, u, HW:], mix[t, HW:]).then_inc(t_in[u], 16)
                        sp.dma_start(x[:, u], rows[ds(j * (2 * P) + u * P, P), :]).then_inc(t_in[u], 16)

                tile_pairs(sp, load, x_rows)

            @block.gpsimd
            def _(pool):
                with pool.Fori(0, NT // 2) as i:
                    for u in range(2):
                        pool.wait_ge(x1_done, ready(2 * i + u))
                        pool.dma_start(x1_out[ds(i * (2 * P) + u * P, P), :], x1[:, u]).then_inc(stored[u], 16)
                for u in range(2):
                    pool.wait_ge(stored[u], 16 * (NT // 2))

            @block.scalar
            def _(act):
                act.preload_act_table_set(ACT_SET)

                def front(i, u):
                    n = 2 * i + u
                    act.wait_ge(gate_ready, n + 1)
                    act.activation(e[:], gate_ps[:], ACT.Exp, scale=-1.0).then_inc(e_done, 1)
                    act.wait_ge(ss_done, n + 1)
                    act.activation(rstd[:], ss[:], ACT.Ln, scale=1.0 / P, bias=eps[:, 0:1])
                    act.drain()
                    act.activation(rstd[:], rstd[:], ACT.Exp, scale=-0.5).then_inc(rstd_done, 1)

                def back(i, u):
                    n = 2 * i + u
                    act.wait_ge(mt_ready, ready(n))
                    act.wait_ge(out_ready, n)
                    act.activation(m_high[:].rearrange("p k t -> p (k t)"), mt_ps[:], ACT.Copy).then_inc(high_done, 1)

                skewed_pairs(act, front, back)

            @block.vector
            def _(dve):
                dve.sem_inc(x1_done, PRIME)
                dve.wait_ge(gain_in, 16)

                def front(i, u):
                    n = 2 * i + u
                    dve.wait_ge(t_in[u], 80 * (i + 1))
                    dve.tensor_tensor(of[:, u], of[:, u], ob[:, u], ALU.add)
                    dve.drain()
                    dve.tensor_tensor(sq[:], of[:, u], of[:, u], ALU.mult)
                    dve.drain()
                    dve.tensor_reduce(ss[:], sq[:].rearrange("p (h c) -> p h c", h=HEADS), AX.X,
                                      ALU.add).then_inc(ss_done, 1)
                    dve.wait_ge(e_done, n + 1)
                    dve.tensor_scalar(silu[:], e[:], 1.0, None, ALU.add)
                    dve.drain()
                    dve.reciprocal(silu[:], silu[:])
                    dve.drain()
                    dve.tensor_tensor(silu[:], gate_ps[:], silu[:], ALU.mult)
                    dve.tensor_tensor(of[:, u], of[:, u], gain[:], ALU.mult)
                    dve.drain()
                    dve.tensor_tensor(silu[:], silu[:], of[:, u], ALU.mult)
                    dve.wait_ge(rstd_done, n + 1)
                    wait_apart(dve)
                    dve.drain()
                    heads = lambda t: t.rearrange("p (h c) -> p h c", h=HEADS)
                    dve.tensor_tensor(heads(mixed[:, u, 0:HW]), heads(silu[:]),
                                      rstd[:].unsqueeze(2).to_broadcast([P, HEADS, P]),
                                      ALU.mult).then_inc(mixed_done, 1)

                def back(i, u):
                    n = 2 * i + u
                    dve.wait_ge(high_done, n + 1)
                    dve.tensor_tensor(m_low[:].rearrange("p k t -> p (k t)"), mt_ps[:],
                                      m_high[:].rearrange("p k t -> p (k t)").bitcast(F32),
                                      ALU.subtract).then_inc(low_done, 1)
                    dve.wait_ge(out_ready, n + 1)
                    dve.wait_ge(stored[u], 16 * i)
                    dve.tensor_tensor(x1[:, u], out_ps[:, u], x[:, u], ALU.add).then_inc(x1_done, 1)

                skewed_pairs(dve, front, back)

            @block.tensor
            def _(pe):
                pe.sem_inc(mt_ready, PRIME)

                def front(i, u):
                    n = 2 * i + u
                    pe.wait_ge(t_in[u], 80 * (i + 1))
                    pe.wait_ge(mixed_done, n)
                    for h in range(HEADS):
                        last = pe.transpose(gate_ps[:, h * P:(h + 1) * P], gate_t[:, u, h], ident[:])
                    last.then_inc(gate_ready, 1)

                def back(i, u):
                    n = 2 * i + u
                    pe.wait_ge(mixed_done, n + 1)
                    for k in range(KC):
                        last = pe.transpose(mt_ps[:, k * P:(k + 1) * P], mixed[:, u, k * P:(k + 1) * P], ident[:])
                    last.then_inc(mt_ready, 1)
                    pe.wait_ge(low_done, n + 1)
                    pe.wait_ge(x1_done, free(n))
                    for half in (slice(0, 512), slice(512, D)):
                        for k in range(KC):
                            last = product3(pe, out_ps[:, u, half], (m_high[:, k], m_low[:, k]),
                                            (w_high[:, k, half], w_low[:, k, half]), k == 0, k == KC - 1)
                    last.then_inc(out_ready, 1)

                skewed_pairs(pe, front, back)


def cross_attention(nc, tag, q_t, kv_t, x1_rows, w_high, w_low, ident, x2_out):
    NM = 2 * N_MEM
    MC = N_MEM // P
    DC = CA_DH // P
    with Mem(nc, tag) as m:
        keys = m.sb("keys", [P, KC, NM])
        v_t = m.sb("v_t", [P, KC, NM])
        v = m.sb("v", [P, NM // P, D])
        q = m.sb("q", [P, 2, KC, P])
        x1 = m.sb("x1", [P, 2, D])
        top = m.sb("top", [P, 2, HEADS])
        total = m.sb("total", [P, 2, HEADS])
        prob = m.sb("prob", [P, 2, D])
        prob_t = m.sb("prob_t", [P, 2 * HEADS, P])
        o_high, o_low = m.sb("o_high", [P, KC, P], F32R), m.sb("o_low", [P, KC, P], F32R)
        x2 = m.sb("x2", [P, 2, D])
        score_ps, pt_ps, ot_ps, out_ps = (m.ps(s, [P, D]) for s in ("score_ps", "pt_ps", "ot_ps", "out_ps"))
        t_in = [m.sem(f"t_in{u}") for u in range(2)]
        stored = [m.sem(f"stored{u}") for u in range(2)]
        (loaded, v_ready, v_done, scores_ready, top_done, exp_done, prob_done, pt_ready, pt_done, ot_ready,
         high_done, low_done, out_ready, x2_done) = (m.sem(s) for s in (
             "loaded", "v_ready", "v_done", "scores_ready", "top_done", "exp_done", "prob_done", "pt_ready",
             "pt_done", "ot_ready", "high_done", "low_done", "out_ready", "x2_done"))

        def skewed_groups(eng, front, back):
            last = NT_P // 2 - 1
            front(0, 0, 0)
            with eng.Fori(0, last) as i:
                for u in range(2):
                    front(i + u, 1 - u, 0)
                    back(i, u, 0)
            front(last, 1, 0)
            back(last, 0, 0)
            front(last + 1, 0, 1)
            back(last, 1, 0)
            front(last + 1, 1, 1)
            for u in range(2):
                back(last + 1, u, 1)

        with nc.Block() as block:
            @block.sync
            def _(sp):
                for k in range(KC):
                    sp.dma_start(keys[:, k], kv_t[k * P:(k + 1) * P, :]).then_inc(loaded, 16)
                for k in range(KC):
                    sp.dma_start(v_t[:, k], kv_t[D + k * P:D + (k + 1) * P, :]).then_inc(loaded, 16)
                with sp.Fori(0, NT // 2) as i:
                    for u in range(2):
                        n = 2 * i + u
                        t = ds(i * (2 * P) + u * P, P)
                        sp.wait_ge(x2_done, free(n))
                        sp.dma_start(q[:, u], q_t[:, t].rearrange("(k p) t -> p k t", p=P)).then_inc(t_in[u], 16)
                        sp.dma_start(x1[:, u], x1_rows[t, :]).then_inc(t_in[u], 16)

            @block.gpsimd
            def _(pool):
                with pool.Fori(0, NT // 2) as i:
                    for u in range(2):
                        pool.wait_ge(x2_done, ready(2 * i + u))
                        pool.dma_start(x2_out[ds(i * (2 * P) + u * P, P), :], x2[:, u]).then_inc(stored[u], 16)
                for u in range(2):
                    pool.wait_ge(stored[u], 16 * (NT // 2))

            @block.scalar
            def _(act):
                act.preload_act_table_set(ACT_SET)
                for t in range(NM // P):
                    act.wait_ge(v_ready, t + 1)
                    act.activation(v[:, t], pt_ps[:], ACT.Copy).then_inc(v_done, 1)

                def front(i, u, group):
                    n = 2 * i + u
                    act.wait_ge(top_done, n + 1)
                    act.wait_ge(pt_ready, free(n))
                    for h in range(HEADS):
                        cols = slice(h * N_MEM, (h + 1) * N_MEM)
                        done = act.activation(prob[:, u, cols], score_ps[:, cols], ACT.Exp, scale=CA_SCALE,
                                              bias=top[:, u, h:h + 1], accum_out=total[:, u, h:h + 1])
                    done.then_inc(exp_done, 1)

                def back(i, u, group):
                    n = 2 * i + u
                    act.wait_ge(pt_ready, ready(n))
                    act.activation(prob_t[:].rearrange("p c t -> p (c t)"), pt_ps[:], ACT.Copy).then_inc(pt_done, 1)
                    act.wait_ge(ot_ready, n + 1)
                    act.activation(o_high[:].rearrange("p k t -> p (k t)"), ot_ps[:], ACT.Copy).then_inc(high_done, 1)

                skewed_groups(act, front, back)

            @block.vector
            def _(dve):
                dve.sem_inc(x2_done, PRIME)

                def front(i, u, group):
                    n = 2 * i + u
                    dve.wait_ge(scores_ready, n + 1)
                    dve.tensor_reduce(top[:, u], score_ps[:].rearrange("p (h c) -> p h c", h=HEADS), AX.X, ALU.max)
                    dve.drain()
                    dve.tensor_scalar(top[:, u], top[:, u], -CA_SCALE, None, ALU.mult).then_inc(top_done, 1)
                    dve.wait_ge(exp_done, n + 1)
                    dve.reciprocal(total[:, u], total[:, u])
                    dve.drain()
                    heads = prob[:, u].rearrange("p (h c) -> p h c", h=HEADS)
                    dve.tensor_tensor(heads, heads, total[:, u].unsqueeze(2).to_broadcast([P, HEADS, N_MEM]),
                                      ALU.mult).then_inc(prob_done, 1)

                def back(i, u, group):
                    n = 2 * i + u
                    dve.wait_ge(high_done, n + 1)
                    dve.tensor_tensor(o_low[:].rearrange("p k t -> p (k t)"), ot_ps[:],
                                      o_high[:].rearrange("p k t -> p (k t)").bitcast(F32),
                                      ALU.subtract).then_inc(low_done, 1)
                    dve.wait_ge(out_ready, n + 1)
                    dve.wait_ge(stored[u], 16 * i)
                    dve.tensor_tensor(x2[:, u], out_ps[:], x1[:, u], ALU.add).then_inc(x2_done, 1)

                skewed_groups(dve, front, back)

            @block.tensor
            def _(pe):
                pe.sem_inc(pt_ready, PRIME)
                pe.wait_ge(loaded, 16 * 2 * KC)
                for t in range(NM // P):
                    pe.wait_ge(v_done, t)
                    for k in range(KC):
                        last = pe.transpose(pt_ps[:, k * P:(k + 1) * P], v_t[:, k, t * P:(t + 1) * P], ident[:])
                    last.then_inc(v_ready, 1)
                pe.wait_ge(v_done, NM // P)

                def front(i, u, group):
                    n = 2 * i + u
                    pe.wait_ge(t_in[u], 32 * (i + 1))
                    pe.wait_ge(exp_done, n)
                    for h in range(HEADS):
                        for c in range(DC):
                            k = h * DC + c
                            last = pe.matmul(score_ps[:, h * N_MEM:(h + 1) * N_MEM], q[:, u, k],
                                             keys[:, k, group * N_MEM:(group + 1) * N_MEM],
                                             start=(c == 0), stop=(c == DC - 1))
                    last.then_inc(scores_ready, 1)

                def back(i, u, group):
                    n = 2 * i + u
                    pe.wait_ge(prob_done, n + 1)
                    pe.wait_ge(pt_done, n)
                    for c in range(2 * HEADS):
                        last = pe.transpose(pt_ps[:, c * P:(c + 1) * P], prob[:, u, c * P:(c + 1) * P], ident[:])
                    last.then_inc(pt_ready, 1)
                    pe.wait_ge(pt_done, n + 1)
                    pe.wait_ge(low_done, n)
                    for k in range(KC):
                        h = k // DC
                        for c in range(MC):
                            last = pe.matmul(ot_ps[:, k * P:(k + 1) * P], v[:, group * MC + c, k * P:(k + 1) * P],
                                             prob_t[:, h * MC + c], start=(c == 0), stop=(c == MC - 1))
                    last.then_inc(ot_ready, 1)
                    pe.wait_ge(low_done, n + 1)
                    pe.wait_ge(x2_done, n + PRIME)
                    for half in (slice(0, 512), slice(512, D)):
                        for k in range(KC):
                            last = product3(pe, out_ps[:, half], (o_high[:, k], o_low[:, k]),
                                            (w_high[:, k, half], w_low[:, k, half]), k == 0, k == KC - 1)
                    last.then_inc(out_ready, 1)

                skewed_groups(pe, front, back)


def router(nc, tag, h_high, h_low, w_rg, b_rg, w_re, b_re, ident, slots, dest_i, weight, expert_i, last_pair):
    NL = N_GROUPS + N_EXP
    NB = MAX_BLOCKS
    with Mem(nc, tag) as m:
        w = m.sb("w", [P, KC, P])
        w_high, w_low = m.sb("w_high", [P, KC, P], F32R), m.sb("w_low", [P, KC, P], F32R)
        logits_t = m.sb("logits_t", [P, T])
        bias = m.sb("bias", [P, NL])
        logits = m.sb("logits", [P, NT, NL])
        first_g = m.sb("first_g", [P, N_GROUPS])
        first_e = m.sb("first_e", [P, N_EXP])
        before = m.sb("before", [P, P])
        ones = m.sb("ones", [P, P])
        block_no = m.sb("block_no", [P, NB])
        entry = m.sb("entry", [P, 2, NT, 2], I32)
        unused = m.sb("unused", [P, NB, 2], I32)
        g_top, g_sum, e_top1, e_top2, e_diff, e_sum, pick = (
            m.sb(s, [P, NT]) for s in ("g_top", "g_sum", "e_top1", "e_top2", "e_diff", "e_sum", "pick"))
        g_one = m.sb("g_one", [P, NT, N_GROUPS])
        g_exp = m.sb("g_exp", [P, NT, N_GROUPS])
        masked = m.sb("masked", [P, NT, N_EXP])
        chosen = m.sb("chosen", [P, 2, NT, N_EXP])
        both = m.sb("both", [P, NT, N_EXP])
        place = m.sb("place", [P, NT, N_EXP])
        carry = m.sb("carry", [P, NT + 1, N_EXP])
        blocks = m.sb("blocks", [P, N_EXP])
        blocks_i = m.sb("blocks_i", [P, N_EXP], I32)
        block_end = m.sb("block_end", [P, N_EXP])
        start = m.sb("start", [P, N_EXP])
        dest = m.sb("dest", [P, 2, NT])
        past = m.sb("past", [P, NB, N_EXP])
        expert = m.sb("expert", [P, NB])
        logits_ps = m.ps("logits_ps", [P, 1536])
        tr_ps = m.ps("tr_ps", [P, 512])
        rank_ps = m.ps("rank_ps", [P, 512])
        sum_ps = m.ps("sum_ps", [P, 512])
        (loaded, cleared, tables, w_done, w_high_done, w_low_done, lt_ready, lt_done, tr_ready, g_shifted,
         g_exp_done, e_diff_done, e_exp_done, both_done, rank_ready, dest_done, table_cleared, scattered) = (
            m.sem(s) for s in (
                "loaded", "cleared", "tables", "w_done", "w_high_done", "w_low_done", "lt_ready", "lt_done",
                "tr_ready", "g_shifted", "g_exp_done", "e_diff_done", "e_exp_done", "both_done", "rank_ready",
                "dest_done", "table_cleared", "scattered"))
        with nc.Block() as block:
            @block.sync
            def _(sp):
                sp.wait_ge(w_done, 1)
                with nc.allow_non_contiguous_dma(reason="short rows of router weights"):
                    sp.dma_start(w[:, :, 0:N_GROUPS], w_rg.rearrange("(k p) n -> p k n", p=P)).then_inc(loaded, 16)
                    sp.dma_start(w[:, :, N_GROUPS:NL], w_re.rearrange("(k p) n -> p k n", p=P)).then_inc(loaded, 16)
                    sp.dma_start(bias[:, 0:N_GROUPS],
                                 b_rg.rearrange("(a n) -> a n", a=1).to_broadcast([P, N_GROUPS])).then_inc(loaded, 16)
                    sp.dma_start(bias[:, N_GROUPS:NL],
                                 b_re.rearrange("(a n) -> a n", a=1).to_broadcast([P, N_EXP])).then_inc(loaded, 16)
                sp.wait_ge(cleared, 3)
                sp.dma_start(slots.rearrange("(p b) a -> p b a", p=P), unused[:]).then_inc(table_cleared, 16)

            @block.gpsimd
            def _(pool):
                pool.memset(before[:], 1.0).then_inc(cleared, 1)
                pool.memset(unused[:, :, 0], 0).then_inc(cleared, 1)
                pool.memset(unused[:, :, 1], 2 * T).then_inc(cleared, 1)
                pool.memset(ones[:], 1.0).then_inc(tables, 1)
                pool.wait_ge(cleared, 3)
                pool.affine_select(out=before[:], in_=before[:], compare_op=ALU.is_gt, fill=0.0, base=0,
                                   pattern=[[1, P]], channel_multiplier=-1).then_inc(tables, 1)
                for table, step, base, width in ((first_g, -1, N_GROUPS, N_GROUPS), (first_e, -1, N_EXP, N_EXP),
                                                 (block_no, 1, 0, NB)):
                    pool.iota(table[:], [[step, width]], base=base, channel_multiplier=0,
                              allow_small_or_imprecise_dtypes=True).then_inc(tables, 1)
                pool.iota(entry[:, :, :, 0], [[0, 2], [P, NT]], base=0, channel_multiplier=1).then_inc(tables, 1)
                pool.iota(entry[:, :, :, 1], [[T, 2], [P, NT]], base=0, channel_multiplier=1).then_inc(tables, 1)
                pool.wait_ge(tables, 7)
                pool.wait_ge(dest_done, 1)
                pool.wait_ge(table_cleared, 16)
                for c in range(2):
                    for t in range(NT):
                        pool.indirect_dma_start(
                            out=slots, out_offset=bass.IndirectOffsetOnAxis(ap=dest_i[:, c, t:t + 1], axis=0),
                            in_=entry[:, c, t], in_offset=None).then_inc(scattered, 16)
                pool.wait_ge(scattered, 16 * 2 * NT)

            @block.scalar
            def _(act):
                act.preload_act_table_set(ACT_SET)
                act.wait_ge(loaded, 64)
                act.activation(w_high[:], w[:], ACT.Copy).then_inc(w_high_done, 1)
                act.wait_ge(g_shifted, 1)
                act.activation(g_exp[:], g_exp[:], ACT.Exp).then_inc(g_exp_done, 1)
                act.wait_ge(e_diff_done, 1)
                act.activation(e_diff[:], e_diff[:], ACT.Exp).then_inc(e_exp_done, 1)

            @block.vector
            def _(dve):
                def over(t, n):
                    return t.unsqueeze(2).to_broadcast([P, NT, n])

                def pick_first(values, top_of, order, one, n):
                    dve.tensor_reduce(top_of[:], values, AX.X, ALU.max)
                    dve.drain()
                    dve.tensor_tensor(one, values, over(top_of[:], n), ALU.is_equal)
                    dve.drain()
                    dve.tensor_tensor(one, one, order[:].unsqueeze(1).to_broadcast([P, NT, n]), ALU.mult)
                    dve.drain()
                    dve.tensor_reduce(pick[:], one, AX.X, ALU.max)
                    dve.drain()
                    dve.tensor_tensor(one, one, over(pick[:], n), ALU.is_equal)
                    dve.drain()

                dve.memset(w[:], 0.0).then_inc(w_done, 1)
                dve.memset(carry[:, 0], 0.0)
                dve.wait_ge(w_high_done, 1)
                dve.tensor_tensor(w_low[:], w[:], w_high[:].bitcast(F32), ALU.subtract).then_inc(w_low_done, 1)
                dve.wait_ge(lt_ready, 1)
                dve.tensor_copy(logits_t[:], logits_ps[:, 0:T]).then_inc(lt_done, 1)
                dve.wait_ge(tr_ready, 1)
                dve.wait_ge(tables, 7)
                dve.tensor_tensor(logits[:], tr_ps[:, 0:NT * NL].rearrange("p (t n) -> p t n", n=NL),
                                  bias[:].unsqueeze(1).to_broadcast([P, NT, NL]), ALU.add)
                dve.drain()
                pick_first(logits[:, :, 0:N_GROUPS], g_top, first_g, g_one[:], N_GROUPS)
                dve.tensor_tensor(g_exp[:], logits[:, :, 0:N_GROUPS], over(g_top[:], N_GROUPS),
                                  ALU.subtract).then_inc(g_shifted, 1)
                by_group = lambda t: t.rearrange("p t (g e) -> p (t g) e", g=N_GROUPS)
                sel = g_one[:].rearrange("p t g -> p (t g)").unsqueeze(2).to_broadcast([P, NT * N_GROUPS, EPG])
                for t in range(NT):
                    dve.tensor_tensor(masked[:, t].rearrange("p (g e) -> p g e", g=N_GROUPS),
                                      logits[:, t, N_GROUPS:].rearrange("p (g e) -> p g e", g=N_GROUPS),
                                      g_one[:, t].unsqueeze(2).to_broadcast([P, N_GROUPS, EPG]), ALU.mult)
                dve.drain()
                dve.tensor_scalar(g_one[:], g_one[:], -1.0, 1e30, ALU.add, ALU.mult)
                dve.drain()
                dve.tensor_tensor(by_group(masked[:]), by_group(masked[:]), sel, ALU.add)
                dve.drain()
                pick_first(masked[:], e_top1, first_e, chosen[:, 0], N_EXP)
                dve.scalar_tensor_tensor(masked[:], chosen[:, 0], -3e30, masked[:], ALU.mult, ALU.add)
                dve.drain()
                pick_first(masked[:], e_top2, first_e, chosen[:, 1], N_EXP)
                dve.tensor_tensor(e_diff[:], e_top2[:], e_top1[:], ALU.subtract).then_inc(e_diff_done, 1)
                dve.tensor_tensor(both[:], chosen[:, 0], chosen[:, 1], ALU.add).then_inc(both_done, 1)
                dve.wait_ge(g_exp_done, 1)
                dve.tensor_reduce(g_sum[:], g_exp[:], AX.X, ALU.add)
                dve.wait_ge(e_exp_done, 1)
                dve.tensor_scalar(e_sum[:], e_diff[:], 1.0, None, ALU.add)
                dve.drain()
                dve.tensor_tensor(e_sum[:], e_sum[:], g_sum[:], ALU.mult)
                dve.drain()
                dve.reciprocal(weight[:, 0], e_sum[:])
                dve.drain()
                dve.tensor_tensor(weight[:, 1], weight[:, 0], e_diff[:], ALU.mult)
                dve.wait_ge(rank_ready, 1)
                for t in range(NT):
                    dve.drain()
                    dve.tensor_tensor(carry[:, t + 1], carry[:, t], sum_ps[:, t * N_EXP:(t + 1) * N_EXP], ALU.add)
                dve.drain()
                dve.tensor_scalar(blocks[:], carry[:, NT], float(P - 1), None, ALU.add)
                dve.drain()
                dve.tensor_copy(blocks_i[:], blocks[:])
                dve.drain()
                dve.tensor_scalar(blocks_i[:], blocks_i[:], P.bit_length() - 1, None, ALU.arith_shift_right)
                dve.drain()
                dve.tensor_copy(blocks[:], blocks_i[:])
                dve.drain()
                dve.tensor_tensor_scan(block_end[:], blocks[:], blocks[:], 0.0, ALU.add, ALU.bypass)
                dve.drain()
                dve.tensor_tensor(start[:], block_end[:], blocks[:], ALU.subtract)
                dve.drain()
                dve.tensor_scalar(start[:], start[:], float(P), None, ALU.mult)
                dve.tensor_tensor(place[:], rank_ps[:, 0:NT * N_EXP].rearrange("p (t e) -> p t e", e=N_EXP),
                                  carry[:, 0:NT], ALU.add)
                dve.drain()
                dve.tensor_tensor(place[:], place[:], start[:].unsqueeze(1).to_broadcast([P, NT, N_EXP]), ALU.add)
                dve.drain()
                for c in range(2):
                    dve.tensor_tensor(chosen[:, c], chosen[:, c], place[:], ALU.mult)
                dve.drain()
                for c in range(2):
                    dve.tensor_reduce(dest[:, c], chosen[:, c], AX.X, ALU.add)
                dve.drain()
                dve.tensor_copy(dest_i[:], dest[:]).then_inc(dest_done, 1)
                dve.tensor_tensor(past[:], block_end[:].unsqueeze(1).to_broadcast([P, NB, N_EXP]),
                                  block_no[:].unsqueeze(2).to_broadcast([P, NB, N_EXP]), ALU.is_le)
                dve.drain()
                dve.tensor_reduce(expert[:], past[:], AX.X, ALU.add)
                dve.drain()
                dve.tensor_scalar(expert[:], expert[:], float(N_EXP - 1), None, ALU.min)
                dve.tensor_scalar(blocks[:, 0:1], block_end[:, N_EXP - 1:N_EXP], -1.0, None, ALU.add)
                dve.drain()
                dve.tensor_copy(expert_i[:], expert[:])
                dve.tensor_copy(last_pair[:], blocks[:, 0:1])
                dve.drain()
                dve.tensor_scalar(last_pair[:], last_pair[:], 1, None, ALU.arith_shift_right)

            @block.tensor
            def _(pe):
                pe.wait_ge(w_low_done, 1)
                for at, size in TOKEN_GROUPS:
                    for k in range(KC):
                        last = product3(pe, logits_ps[:, at:at + size], (w_high[:, k], w_low[:, k]),
                                        (h_high[:, k, at:at + size], h_low[:, k, at:at + size]), k == 0, k == KC - 1)
                last.then_inc(lt_ready, 1)
                pe.wait_ge(lt_done, 1)
                for t in range(NT):
                    last = pe.transpose(tr_ps[:, t * NL:(t + 1) * NL], logits_t[0:NL, t * P:(t + 1) * P],
                                        ident[0:NL, 0:NL])
                last.then_inc(tr_ready, 1)
                pe.wait_ge(both_done, 1)
                pe.wait_ge(tables, 7)
                rows = both[:].rearrange("p t e -> p (t e)")
                pe.matmul(rank_ps[:, 0:NT * N_EXP], before[:], rows, start=True, stop=True)
                pe.matmul(sum_ps[:, 0:NT * N_EXP], ones[:], rows, start=True, stop=True).then_inc(rank_ready, 1)


def experts(nc, tag, h_rows, slots, w_gate, w_up, w_down, g_ffn, expert_i, last_pair, ident, y_out):
    with Mem(nc, tag) as m:
        wg = m.sb("wg", [P, 2, KC, D_EXP])
        wu = m.sb("wu", [P, 2, KC, D_EXP])
        wd = m.sb("wd", [P, 2, FC, D])
        entry = [m.sb(f"entry{u}", [P, 2], I32) for u in range(2)]
        rows = m.sb("rows", [P, 2, D])
        x_t = m.sb("x_t", [P, 2, KC, P])
        g = m.sb("g", [P, KC])
        sig = m.sb("sig", [P, D_EXP])
        hidden = m.sb("hidden", [P, 2, D_EXP])
        hidden_t = m.sb("hidden_t", [P, FC, P])
        y = m.sb("y", [P, 2, D])
        tr_ps = m.ps("tr_ps", [P, D])
        gate_ps = m.ps("gate_ps", [P, 2, D_EXP])
        up_ps = m.ps("up_ps", [P, 2, D_EXP])
        y_ps = m.ps("y_ps", [P, D])
        g_in = m.sem("g_in")
        entry_in, row_in, wg_in, wu_in, wd_in, stored = (
            [m.sem(f"{s}{u}") for u in range(2)] for s in ("entry_in", "row_in", "wg_in", "wu_in", "wd_in", "stored"))
        (xt_ready, xt_done, gate_ready, up_ready, sig_done, hidden_done, ht_ready, ht_done, y_ready, y_done) = (
            m.sem(s) for s in ("xt_ready", "xt_done", "gate_ready", "up_ready", "sig_done", "hidden_done",
                               "ht_ready", "ht_done", "y_ready", "y_done"))

        def last_of(eng):
            return eng.value_load(last_pair[0:1, 0:1], min_val=2 * T // P // 2 - 1, max_val=MAX_BLOCKS // 2 - 1)

        def skewed(eng, front, back):
            last = last_of(eng)
            front(0, 0)
            with eng.Fori(0, last) as i:
                for u in range(2):
                    front(i + u, 1 - u)
                    back(i, u)
            front(last, 1)
            for u in range(2):
                back(last, u)
            return last

        with nc.Block() as block:
            @block.sync
            def _(sp):
                last = last_of(sp)
                with nc.allow_non_contiguous_dma(reason="a gain column of 1024 numbers"):
                    sp.dma_start(g[:], g_ffn.rearrange("(k p) -> p k", p=P)).then_inc(g_in, 16)
                with sp.Fori(0, last + 1) as i:
                    for u in range(2):
                        n = 2 * i + u
                        e = sp.value_load(expert_i[0:1, ds(n, 1)], min_val=0, max_val=N_EXP - 1)
                        sp.wait_ge(stored[u], i * 16)
                        with nc.allow_non_contiguous_dma(reason="two numbers to a partition"):
                            sp.dma_start(entry[u][:], slots[ds(n * P, P), :]).then_inc(entry_in[u], 16)
                        sp.wait_ge(up_ready, free(n))
                        sp.dma_start(wg[:, u], w_gate[ds(e * D, D), :]
                                     .rearrange("(k p) n -> p k n", p=P)).then_inc(wg_in[u], 16)
                        sp.dma_start(wu[:, u], w_up[ds(e * D, D), :]
                                     .rearrange("(k p) n -> p k n", p=P)).then_inc(wu_in[u], 16)
                        sp.wait_ge(y_ready, free(n))
                        sp.dma_start(wd[:, u], w_down[ds(e * D_EXP, D_EXP), :]
                                     .rearrange("(k p) n -> p k n", p=P)).then_inc(wd_in[u], 16)

            @block.gpsimd
            def _(pool):
                def front(i, u):
                    pool.wait_ge(entry_in[u], i * 16 + 16)
                    pool.wait_ge(xt_ready, free(2 * i + u))
                    wait_apart(pool)
                    pool.indirect_dma_start(out=rows[:, u], out_offset=None, in_=h_rows,
                                            in_offset=bass.IndirectOffsetOnAxis(ap=entry[u][:, 0:1], axis=0)
                                            ).then_inc(row_in[u], 16)

                def back(i, u):
                    n = 2 * i + u
                    pool.wait_ge(y_done, ready(n))
                    wait_apart(pool)
                    pool.indirect_dma_start(out=y_out, in_=y[:, u], in_offset=None,
                                            out_offset=bass.IndirectOffsetOnAxis(ap=entry[u][:, 1:2], axis=0),
                                            bounds_check=2 * T - 1, oob_is_err=False).then_inc(stored[u], 16)

                last = skewed(pool, front, back)
                for u in range(2):
                    pool.wait_ge(stored[u], last * 16 + 16)

            @block.scalar
            def _(act):
                act.preload_act_table_set(ACT_SET)
                act.sem_inc(y_done, PRIME)
                act.sem_inc(ht_done, PRIME)

                def front(i, u):
                    n = 2 * i + u
                    act.wait_ge(gate_ready, ready(n))
                    act.activation(sig[:], gate_ps[:, u], ACT.Exp, scale=-1.0).then_inc(sig_done, 1)

                def back(i, u):
                    n = 2 * i + u
                    act.wait_ge(ht_ready, n + 1)
                    act.activation(hidden_t[:].rearrange("p k t -> p (k t)"), tr_ps[:, 0:D_EXP],
                                   ACT.Copy).then_inc(ht_done, 1)
                    act.wait_ge(y_ready, ready(n))
                    act.wait_ge(stored[u], i * 16)
                    act.activation(y[:, u], y_ps[:], ACT.Copy).then_inc(y_done, 1)

                skewed(act, front, back)

            @block.vector
            def _(dve):
                dve.sem_inc(hidden_done, PRIME)
                dve.wait_ge(g_in, 16)

                def front(i, u):
                    n = 2 * i + u
                    dve.wait_ge(xt_ready, ready(n))
                    dve.tensor_tensor(x_t[:, u], tr_ps[:].rearrange("p (k t) -> p k t", k=KC),
                                      g[:].unsqueeze(2).to_broadcast([P, KC, P]), ALU.mult).then_inc(xt_done, 1)
                    dve.wait_ge(sig_done, n + 1)
                    dve.tensor_scalar(hidden[:, u], sig[:], 1.0, None, ALU.add)
                    dve.drain()
                    dve.reciprocal(hidden[:, u], hidden[:, u])
                    dve.drain()
                    dve.tensor_tensor(hidden[:, u], gate_ps[:, u], hidden[:, u], ALU.mult)
                    dve.drain()
                    dve.wait_ge(up_ready, ready(n))
                    dve.tensor_tensor(hidden[:, u], up_ps[:, u], hidden[:, u], ALU.mult).then_inc(hidden_done, 1)

                def back(i, u):
                    pass

                skewed(dve, front, back)

            @block.tensor
            def _(pe):
                for s in (xt_ready, gate_ready, up_ready, y_ready):
                    pe.sem_inc(s, PRIME)

                def front(i, u):
                    n = 2 * i + u
                    pe.wait_ge(row_in[u], i * 16 + 16)
                    pe.wait_ge(ht_done, free(n))
                    for k in range(KC):
                        last = pe.transpose(tr_ps[:, k * P:(k + 1) * P], rows[:, u, k * P:(k + 1) * P], ident[:])
                    last.then_inc(xt_ready, 1)
                    pe.wait_ge(xt_done, n + 1)
                    pe.wait_ge(hidden_done, free(n))
                    for loaded, w, out, done in ((wg_in, wg, gate_ps, gate_ready), (wu_in, wu, up_ps, up_ready)):
                        pe.wait_ge(loaded[u], i * 16 + 16)
                        for k in range(KC):
                            last = pe.matmul(out[:, u], x_t[:, u, k], w[:, u, k], start=(k == 0), stop=(k == KC - 1))
                        last.then_inc(done, 1)

                def back(i, u):
                    n = 2 * i + u
                    pe.wait_ge(hidden_done, ready(n))
                    for k in range(FC):
                        last = pe.transpose(tr_ps[:, k * P:(k + 1) * P], hidden[:, u, k * P:(k + 1) * P], ident[:])
                    last.then_inc(ht_ready, 1)
                    pe.wait_ge(ht_done, ready(n))
                    pe.wait_ge(y_done, n + PRIME)
                    pe.wait_ge(wd_in[u], i * 16 + 16)
                    for half in (slice(0, 512), slice(512, D)):
                        for k in range(FC):
                            last = pe.matmul(y_ps[:, half], hidden_t[:, k], wd[:, u, k, half],
                                             start=(k == 0), stop=(k == FC - 1))
                    last.then_inc(y_ready, 1)

                skewed(pe, front, back)


def combine(nc, tag, x2_rows, y_rows, weight, g_final, eps, outputs):
    with Mem(nc, tag) as m:
        x = m.sb("x", [P, 2, D])
        y = m.sb("y", [P, 2, 2, D])
        gain = m.sb("gain", [P, D])
        junk = m.sb("junk", [P, D])
        ss, rstd = m.sb("ss", [P, 1]), m.sb("rstd", [P, 1])
        out = m.sb("out", [P, 2, D])
        gain_in = m.sem("gain_in")
        x_in, stored = ([m.sem(f"{s}{u}") for u in range(2)] for s in ("x_in", "stored"))
        sum_done, rstd_done, out_done = m.sem("sum_done"), m.sem("rstd_done"), m.sem("out_done")
        with nc.Block() as block:
            @block.sync
            def _(sp):
                with nc.allow_non_contiguous_dma(reason="one row for all partitions"):
                    sp.dma_start(gain[:], g_final.rearrange("(a n) -> a n", a=1).to_broadcast([P, D])).then_inc(gain_in, 16)
                with sp.Fori(0, NT // 2) as i:
                    for u in range(2):
                        sp.wait_ge(out_done, free(2 * i + u))
                        t = i * (2 * P) + u * P
                        sp.dma_start(x[:, u], x2_rows[ds(t, P), :]).then_inc(x_in[u], 16)
                        for c in range(2):
                            sp.dma_start(y[:, u, c], y_rows[ds(t + c * T, P), :]).then_inc(x_in[u], 16)

            @block.vector
            def _(dve):
                dve.sem_inc(out_done, PRIME)
                dve.wait_ge(gain_in, 16)
                with dve.Fori(0, NT // 2) as i:
                    for u in range(2):
                        n = 2 * i + u
                        dve.wait_ge(x_in[u], i * 48 + 48)
                        dve.scalar_tensor_tensor(x[:, u], y[:, u, 0], weight[:, 0, ds(n, 1)], x[:, u],
                                                 ALU.mult, ALU.add)
                        dve.drain()
                        dve.scalar_tensor_tensor(x[:, u], y[:, u, 1], weight[:, 1, ds(n, 1)], x[:, u],
                                                 ALU.mult, ALU.add).then_inc(sum_done, 1)
                        dve.wait_ge(rstd_done, n + 1)
                        dve.wait_ge(stored[u], i * 16)
                        dve.scalar_tensor_tensor(out[:, u], x[:, u], rstd[:], gain[:], ALU.mult,
                                                 ALU.mult).then_inc(out_done, 1)

            @block.scalar
            def _(act):
                act.preload_act_table_set(ACT_SET)

                def body(i, rows, j):
                    for u in range(2):
                        n = 2 * i + u
                        act.wait_ge(sum_done, n + 1)
                        act.activation(junk[:], x[:, u], ACT.Square, accum_out=ss[:])
                        act.drain()
                        act.activation(rstd[:], ss[:], ACT.Ln, scale=1.0 / D, bias=eps[:, 0:1])
                        act.drain()
                        act.activation(rstd[:], rstd[:], ACT.Exp, scale=-0.5).then_inc(rstd_done, 1)
                        act.wait_ge(out_done, ready(n))
                        act.dma_start(rows[ds(j * (2 * P) + u * P, P), :], out[:, u]).then_inc(stored[u], 16)

                tile_pairs(act, body, outputs)
                for u in range(2):
                    act.wait_ge(stored[u], 16 * (NT // 2))


def encoder(nc, x_prompt, x_sample, mem_prompt, mem_sample, g_mix, w_in, hg_lb, g_hg, lam_q1, lam_k1, lam_q2,
            lam_k2, g_da, w_out, g_ca, g_mem, w_cq, w_ckv, w_co, g_ffn, w_rg, b_rg, w_re, b_re, w_gate, w_up,
            w_down, g_final, y_prompt, y_sample):
    def scratch(name, shape, dt=F32):
        return nc.dram_tensor(name, shape, dt, kind="Internal").ap()

    proj_t = scratch("proj_t", [w_in.shape[2], T])
    o_fwd, o_bwd = scratch("o_fwd", [T, HW]), scratch("o_bwd", [T, HW])
    mix = scratch("mix", [T, 2 * HW])
    x1, x2, h3 = scratch("x1", [T, D]), scratch("x2", [T, D]), scratch("h3", [T, D])
    kv_t = scratch("kv_t", [2 * D, 2 * N_MEM])
    q_t = scratch("q_t", [D, T])
    slots = scratch("slots", [MAX_BLOCKS * P, 2], I32)
    y_rows = scratch("y_rows", [2 * T, D])
    x_rows = [(x_prompt[0], NT_P), (x_sample[0], NT - NT_P)]

    with Mem(nc, "kept") as kept:
        ident, eps = kept.sb("ident", [P, P]), kept.sb("eps", [P, 1])
        lb, one_minus_lb = kept.sb("lb", [P, HEADS]), kept.sb("one_minus_lb", [P, HEADS])
        lam = kept.sb("lam", [P, 1])
        constants(nc, ident, eps)
        lower_bound(nc, hg_lb, lb, one_minus_lb)
        lambda_of(nc, lam_q1[0], lam_k1[0], lam_q2[0], lam_k2[0], lam)

        with Mem(nc, "mem") as m:
            high, low = m.sb("high", [P, KC, 2 * N_MEM], F32R), m.sb("low", [P, KC, 2 * N_MEM], F32R)
            normed_transposed(nc, "norm_mem", [(mem_prompt[0], N_MEM // P), (mem_sample[0], N_MEM // P)], g_mem[0],
                              ident, eps, high, low)
            project(nc, "proj_kv", w_ckv[0], 2 * D, high, low, [(0, 2 * N_MEM)], kv_t)
        with Mem(nc, "in") as m:
            high, low = m.sb("high", [P, KC, T], F32R), m.sb("low", [P, KC, T], F32R)
            normed_transposed(nc, "norm_mix", x_rows, g_mix[0], ident, eps, high, low)
            project(nc, "proj_in", w_in[0], w_in.shape[2], high, low, TOKEN_GROUPS, proj_t)

        hgrn(nc, "hg_fwd", proj_t, ROW_FF, True, lb, one_minus_lb, ident, o_fwd)
        hgrn(nc, "hg_bwd", proj_t, ROW_FB, False, lb, one_minus_lb, ident, o_bwd)
        diff_attention(nc, "da_prompt", proj_t, 0, SEQ_P, g_da[0], lam, ident, eps, mix)
        diff_attention(nc, "da_sample", proj_t, SEQ_P, SEQ_S, g_da[0], lam, ident, eps, mix)

        with Mem(nc, "out") as m:
            w_high, w_low = m.sb("w_high", [P, KC, D], F32R), m.sb("w_low", [P, KC, D], F32R)
            split_weight(nc, "split_out", w_out[0], w_high, w_low)
            mix_out(nc, "mix_out", o_fwd, o_bwd, proj_t, mix, x_rows, g_hg[0], w_high, w_low, ident, eps, x1)
        with Mem(nc, "cq") as m:
            high, low = m.sb("high", [P, KC, T], F32R), m.sb("low", [P, KC, T], F32R)
            normed_transposed(nc, "norm_ca", [(x1, NT)], g_ca[0], ident, eps, high, low)
            project(nc, "proj_q", w_cq[0], D, high, low, TOKEN_GROUPS, q_t)
        with Mem(nc, "co") as m:
            w_high, w_low = m.sb("w_high", [P, KC, D], F32R), m.sb("w_low", [P, KC, D], F32R)
            split_weight(nc, "split_co", w_co[0], w_high, w_low)
            cross_attention(nc, "cross", q_t, kv_t, x1, w_high, w_low, ident, x2)

        dest_i, weight = kept.sb("dest_i", [P, 2, NT], I32), kept.sb("weight", [P, 2, NT])
        expert_i, last_pair = kept.sb("expert_i", [P, MAX_BLOCKS], I32), kept.sb("last_pair", [P, 1], I32)
        with Mem(nc, "moe") as m:
            high, low = m.sb("high", [P, KC, T], F32R), m.sb("low", [P, KC, T], F32R)
            normed_transposed(nc, "norm_ffn", [(x2, NT)], g_ffn[0], ident, eps, high, low, rows_out=h3)
            router(nc, "router", high, low, w_rg[0], b_rg[0], w_re[0], b_re[0], ident, slots, dest_i, weight,
                   expert_i, last_pair)
        experts(nc, "experts", h3, slots, w_gate[0].rearrange("e k n -> (e k) n"),
                w_up[0].rearrange("e k n -> (e k) n"), w_down[0].rearrange("e k n -> (e k) n"), g_ffn[0],
                expert_i, last_pair, ident, y_rows)
        combine(nc, "combine", x2, y_rows, weight, g_final, eps,
                [(y_prompt[0], NT_P), (y_sample[0], NT - NT_P)])


_INS = ["x_prompt", "x_sample", "mem_prompt", "mem_sample", "g_mix", "w_in", "hg_lb", "g_hg", "lam_q1", "lam_k1",
        "lam_q2", "lam_k2", "g_da", "w_out", "g_ca", "g_mem", "w_cq", "w_ckv", "w_co", "g_ffn", "w_rg", "b_rg",
        "w_re", "b_re", "w_gate", "w_up", "w_down", "g_final"]
_OUTS = [((1, SEQ_P, D), "float32"), ((1, SEQ_S, D), "float32")]


def kernel(**inputs):
    import numpy as _np
    import concourse.bacc as _bacc
    from concourse import mybir as _mybir
    from concourse.bass_utils import run_bass_kernel_spmd as _run

    nc = _bacc.Bacc("TRN2", target_bir_lowering=False, num_devices=1)
    arrays, args = {}, []
    for name in _INS:
        a = _np.ascontiguousarray(inputs[name])
        arrays[f"in_{name}_dram"] = a
        args.append(nc.dram_tensor(f"in_{name}_dram", a.shape, _mybir.dt.from_np(a.dtype), kind="ExternalInput").ap())
    for i, (shape, dtype) in enumerate(_OUTS):
        dt = _mybir.dt.from_np(_np.dtype(dtype))
        args.append(nc.dram_tensor(f"out_{i}_dram", shape, dt, kind="ExternalOutput").ap())
    encoder(nc, *args)
    r = _run(nc, [arrays], core_ids=[0])
    got = tuple(r.results[0][f"out_{i}_dram"] for i in range(len(_OUTS)))
    return got
```

```python
import math
from contextlib import ExitStack

import concourse.bass as bass
from concourse import mybir

F32 = mybir.dt.float32
F32R = mybir.dt.float32r
I32 = mybir.dt.int32
U32 = mybir.dt.uint32
ALU = mybir.AluOpType
ACT = mybir.ActivationFunctionType
AX = mybir.AxisListType
ds = bass.ds

P = 128
D = 1024
KC = D // P
SEQ_P, SEQ_S, N_MEM = 1024, 256, 256
T = SEQ_P + SEQ_S
NT = T // P
NT_P = SEQ_P // P
EPS = 1e-6
HEADS = 4
HW = HEADS * P
DK = 64
DA_SCALE = DK ** -0.5
CA_DH = D // HEADS
CA_SCALE = CA_DH ** -0.5
N_GROUPS, EPG = 4, 8
N_EXP = N_GROUPS * EPG
D_EXP = 512
FC = D_EXP // P
MAX_BLOCKS = 2 * T // P + N_EXP
LAM_INIT = 0.8 - 0.6 * math.exp(-0.3 * 0)
ROW_Q, ROW_FF, ROW_FB, ROW_V, ROW_G, ROW_DQ, ROW_DK, ROW_DV = (HW * n for n in range(8))
TOKEN_GROUPS = [(0, 512), (512, 512), (1024, 256)]
PRIME = 2
ACT_SET = "natural_log_exp_and_others"


def free(n):
    return n + 1


def ready(n):
    return n + 1 + PRIME


def wait_apart(eng):
    eng.nop(nofuse=True)


class Mem:

    def __init__(self, nc, tag):
        self.nc, self.tag, self.stack, self.sems = nc, tag, ExitStack(), []

    def __enter__(self):
        return self

    def __exit__(self, *a):
        if self.sems and a[0] is None:
            self.nc.clear_and_free_semaphores(self.sems)
            self.nc.all_engine_barrier()
        return self.stack.__exit__(*a)

    def sb(self, name, shape, dt=F32):
        return self.stack.enter_context(self.nc.sbuf_tensor(f"{self.tag}_{name}", shape, dt))

    def ps(self, name, shape, dt=F32):
        return self.stack.enter_context(self.nc.psum_tensor(f"{self.tag}_{name}", shape, dt))

    def sem(self, name):
        self.sems.append(self.nc.alloc_semaphore(f"{self.tag}_{name}"))
        return self.sems[-1]


def product3(pe, out, lhs, rhs, first, last):
    pe.matmul(out, lhs[0], rhs[0], start=first, stop=False)
    pe.matmul(out, lhs[0], rhs[1], start=False, stop=False)
    return pe.matmul(out, lhs[1], rhs[0], start=False, stop=last)


def constants(nc, ident, eps):
    with Mem(nc, "const") as m:
        zero_done, done = m.sem("zero_done"), m.sem("done")
        with nc.Block() as block:
            @block.gpsimd
            def _(pool):
                pool.memset(ident[:], 0.0).then_inc(zero_done, 1)
                pool.wait_ge(zero_done, 1)
                pool.affine_select(out=ident[:], in_=ident[:], compare_op=ALU.not_equal, fill=1.0, base=0,
                                   pattern=[[-1, P]], channel_multiplier=1).then_inc(done, 1)
                pool.memset(eps[:], EPS).then_inc(done, 1)
                pool.wait_ge(done, 2)


def normed_transposed(nc, tag, sources, gain, ident, eps, high, low, rows_out=None):
    with Mem(nc, tag) as m:
        x = m.sb("x", [P, 2, D])
        xn = m.sb("xn", [P, 2, D])
        tmp = m.sb("tmp", [P, 2, D])
        junk = m.sb("junk", [P, D])
        g = m.sb("g", [P, KC])
        ss, lg, rstd = m.sb("ss", [P, 2]), m.sb("lg", [P, 2]), m.sb("rstd", [P, 2])
        xT = m.ps("xT", [P, 2, D])
        g_in = m.sem("g_in")
        x_in = [m.sem(f"x_in{u}") for u in range(2)]
        stored = [m.sem(f"stored{u}") for u in range(2)]
        rstd_done, xn_done, tr_done, tmp_done, high_done = (
            m.sem(s) for s in ("rstd_done", "xn_done", "tr_done", "tmp_done", "high_done"))
        pairs = sum(n for _, n in sources) // 2
        with nc.Block() as block:
            @block.sync
            def _(sp):
                with nc.allow_non_contiguous_dma(reason="a gain column of 1024 numbers"):
                    sp.dma_start(g[:], gain.rearrange("(k p) -> p k", p=P)).then_inc(g_in, 16)

                def load(i, rows, j):
                    for u in range(2):
                        sp.wait_ge(xn_done, free(2 * i + u))
                        sp.dma_start(x[:, u, :], rows[ds(j * (2 * P) + u * P, P), :]).then_inc(x_in[u], 16)

                at = 0
                for rows, tiles in sources:
                    if tiles > 2:
                        with sp.Fori(0, tiles // 2) as j:
                            load(j + at, rows, j)
                    else:
                        load(at, rows, 0)
                    at += tiles // 2

            @block.gpsimd
            def _(pool):
                if rows_out is None:
                    return
                with pool.Fori(0, pairs) as i:
                    for u in range(2):
                        pool.wait_ge(xn_done, ready(2 * i + u))
                        pool.dma_start(rows_out[ds(i * (2 * P) + u * P, P), :], xn[:, u, :]).then_inc(stored[u], 16)
                for u in range(2):
                    pool.wait_ge(stored[u], 16 * pairs)

            @block.scalar
            def _(act):
                act.preload_act_table_set(ACT_SET)
                act.sem_inc(rstd_done, PRIME)
                act.sem_inc(high_done, PRIME)
                with act.Fori(0, pairs) as i:
                    for u in range(2):
                        act.wait_ge(x_in[u], 16 * (i + 1))
                        act.activation(junk[:], x[:, u, :], ACT.Square, accum_out=ss[:, u:u + 1])
                        act.drain()
                    act.activation(lg[:], ss[:], ACT.Ln, scale=1.0 / D, bias=eps[:, 0:1])
                    act.drain()
                    act.activation(rstd[:], lg[:], ACT.Exp, scale=-0.5).then_inc(rstd_done, 2)
                    for u in range(2):
                        n = 2 * i + u
                        act.wait_ge(tmp_done, ready(n))
                        act.activation(high[:, :, ds(n * P, P)],
                                       tmp[:, u, :].rearrange("p (k t) -> p k t", k=KC),
                                       ACT.Copy).then_inc(high_done, 1)

            @block.vector
            def _(dve):
                dve.sem_inc(xn_done, PRIME)
                dve.sem_inc(tmp_done, PRIME)
                dve.wait_ge(g_in, 16)
                with dve.Fori(0, pairs) as i:
                    for u in range(2):
                        n = 2 * i + u
                        dve.wait_ge(rstd_done, 2 * i + 2 + PRIME)
                        dve.wait_ge(tr_done, free(n))
                        if rows_out is not None:
                            dve.wait_ge(stored[u], 16 * i)
                        dve.tensor_scalar(xn[:, u, :], x[:, u, :], rstd[:, u:u + 1], None,
                                          ALU.mult).then_inc(xn_done, 1)
                    for u in range(2):
                        n = 2 * i + u
                        dve.wait_ge(tr_done, ready(n))
                        dve.wait_ge(high_done, free(n))
                        dve.tensor_tensor(tmp[:, u, :].rearrange("p (k t) -> p k t", k=KC),
                                          xT[:, u, :].rearrange("p (k t) -> p k t", k=KC),
                                          g[:].unsqueeze(2).to_broadcast([P, KC, P]), ALU.mult).then_inc(tmp_done, 1)
                    for u in range(2):
                        n = 2 * i + u
                        dve.wait_ge(high_done, ready(n))
                        dve.tensor_tensor(low[:, :, ds(n * P, P)],
                                          tmp[:, u, :].rearrange("p (k t) -> p k t", k=KC),
                                          high[:, :, ds(n * P, P)].bitcast(F32), ALU.subtract)
                    dve.drain()

            @block.tensor
            def _(pe):
                pe.sem_inc(tr_done, PRIME)
                with pe.Fori(0, pairs) as i:
                    for u in range(2):
                        n = 2 * i + u
                        pe.wait_ge(xn_done, ready(n))
                        pe.wait_ge(tmp_done, free(n))
                        for k in range(KC):
                            last = pe.transpose(xT[:, u, k * P:(k + 1) * P], xn[:, u, k * P:(k + 1) * P], ident[:])
                        last.then_inc(tr_done, 1)


def project(nc, tag, weight, columns, high, low, groups, out_t):
    tokens = sum(n for _, n in groups)
    with Mem(nc, tag) as m:
        raw = m.sb("raw", [P, 2, KC, P])
        w_high = m.sb("w_high", [P, 2, KC, P], F32R)
        w_low = m.sb("w_low", [P, 2, KC, P], F32R)
        staged = m.sb("staged", [P, 2, tokens])
        acc = m.ps("acc", [P, 2, -(-tokens // 512) * 512])
        w_in = [m.sem(f"w_in{u}") for u in range(2)]
        stored = [m.sem(f"stored{u}") for u in range(2)]
        high_done, low_done, mm_done, staged_done = (
            m.sem(s) for s in ("high_done", "low_done", "mm_done", "staged_done"))
        pairs = columns // P // 2
        with nc.Block() as block:
            @block.sync
            def _(sp):
                with sp.Fori(0, pairs) as i:
                    for u in range(2):
                        sp.wait_ge(low_done, free(2 * i + u))
                        sp.dma_start(raw[:, u], weight[:, ds(i * (2 * P) + u * P, P)]
                                     .rearrange("(k p) n -> p k n", p=P)).then_inc(w_in[u], 16)

            @block.scalar
            def _(act):
                act.preload_act_table_set(ACT_SET)
                act.sem_inc(high_done, PRIME)
                act.sem_inc(staged_done, PRIME)

                def round_weight(i, u):
                    act.wait_ge(w_in[u], 16 * (i + 1))
                    act.wait_ge(mm_done, free(2 * i + u))
                    act.activation(w_high[:, u], raw[:, u], ACT.Copy).then_inc(high_done, 1)

                def stage(i, u):
                    act.wait_ge(mm_done, ready(2 * i + u))
                    act.wait_ge(stored[u], 16 * i)
                    act.activation(staged[:, u], acc[:, u, 0:tokens], ACT.Copy).then_inc(staged_done, 1)

                for u in range(2):
                    round_weight(0, u)
                with act.Fori(0, pairs - 1) as i:
                    for u in range(2):
                        stage(i, u)
                        round_weight(i + 1, u)
                for u in range(2):
                    stage(pairs - 1, u)

            @block.vector
            def _(dve):
                dve.sem_inc(low_done, PRIME)
                with dve.Fori(0, pairs) as i:
                    for u in range(2):
                        n = 2 * i + u
                        dve.wait_ge(high_done, ready(n))
                        dve.wait_ge(mm_done, free(n))
                        dve.tensor_tensor(w_low[:, u], raw[:, u], w_high[:, u].bitcast(F32),
                                          ALU.subtract).then_inc(low_done, 1)

            @block.tensor
            def _(pe):
                pe.sem_inc(mm_done, PRIME)
                with pe.Fori(0, pairs) as i:
                    for u in range(2):
                        n = 2 * i + u
                        pe.wait_ge(low_done, ready(n))
                        pe.wait_ge(staged_done, free(n))
                        for at, size in groups:
                            for k in range(KC):
                                last = product3(pe, acc[:, u, at:at + size], (w_high[:, u, k], w_low[:, u, k]),
                                                (high[:, k, at:at + size], low[:, k, at:at + size]),
                                                k == 0, k == KC - 1)
                        last.then_inc(mm_done, 1)

            @block.gpsimd
            def _(pool):
                with pool.Fori(0, pairs) as i:
                    for u in range(2):
                        pool.wait_ge(staged_done, ready(2 * i + u))
                        pool.dma_start(out_t[ds(i * (2 * P) + u * P, P), :], staged[:, u]).then_inc(stored[u], 16)
                for u in range(2):
                    pool.wait_ge(stored[u], 16 * pairs)


def lower_bound(nc, hg_lb, lb, one_minus_lb):
    with Mem(nc, "lb") as m:
        rows = m.sb("rows", [P, 2, HEADS])
        top = m.sb("top", [P, HEADS])
        e = m.sb("e", [P, 2, HEADS])
        total = m.sb("total", [P, HEADS])
        rows_in, shifted, exp_done = (m.sem(s) for s in ("rows_in", "shifted", "exp_done"))
        with nc.Block() as block:
            @block.sync
            def _(sp):
                with nc.allow_non_contiguous_dma(reason="a few columns of 128 numbers"):
                    for r in range(2):
                        sp.dma_start(rows[:, r], hg_lb[r].rearrange("(h p) -> p h", p=P)).then_inc(rows_in, 16)

            @block.vector
            def _(dve):
                dve.wait_ge(rows_in, 32)
                dve.tensor_tensor(top[:], rows[:, 0], rows[:, 1], ALU.max)
                dve.drain()
                dve.tensor_tensor(rows[:], rows[:], top[:].unsqueeze(1).to_broadcast([P, 2, HEADS]),
                                  ALU.subtract).then_inc(shifted, 1)
                dve.wait_ge(exp_done, 1)
                dve.tensor_tensor(total[:], e[:, 0], e[:, 1], ALU.add)
                dve.drain()
                dve.reciprocal(total[:], total[:])
                dve.drain()
                dve.tensor_tensor(lb[:], e[:, 0], total[:], ALU.mult)
                dve.drain()
                dve.tensor_scalar(one_minus_lb[:], lb[:], -1.0, 1.0, ALU.mult, ALU.add)

            @block.scalar
            def _(act):
                act.preload_act_table_set(ACT_SET)
                act.wait_ge(shifted, 1)
                act.activation(e[:], rows[:], ACT.Exp).then_inc(exp_done, 1)


LEVELS = (64, 32, 16)
CENTRE = LEVELS[-1] // 2 - 1


def hgrn(nc, tag, proj_t, lb, one_minus_lb, ident, o_fwd, o_bwd):
    n_lev = len(LEVELS)
    base = LEVELS[-1]
    early, late = (0, 1), (1, 0)
    last_t = (P - 1, 0)
    anew_after = (NT_P - 1, NT - NT_P - 1)
    outputs = (o_fwd, o_bwd)
    with Mem(nc, tag) as m:
        x = m.sb("x", [P, 2, 2, HEADS, P])
        v_t = m.sb("v_t", [P, 2, HEADS, P])
        sig = m.sb("sig", [P, 2, 2 * HW])
        q = m.sb("q", [P, 2, HW])
        k = m.sb("k", [P, 2, HW])
        f = m.sb("f", [P, 2, HW])
        lf = m.sb("lf", [P, 2, HEADS, P])
        b = m.sb("b", [P, 2, HEADS, P])
        diff = m.sb("diff", [P, 2, n_lev + 2, HW])
        decay = m.sb("decay", [P, 2, n_lev + 2, HW])
        uncentre = m.sb("uncentre", [P, 2, HW])
        from_start = m.sb("from_start", [P, 2, HW])
        whole = m.sb("whole", [P, 2, HEADS])
        q_dec = m.sb("q_dec", [P, 2, n_lev + 2, HW])
        k_dec = m.sb("k_dec", [P, 2, n_lev + 2, HW])
        v = m.sb("v", [P, 2, HW])
        k_tok = m.sb("k_tok", [P, HW])
        s_t = m.sb("s_t", [P, HW])
        state = m.sb("state", [P, 2, HW])
        o = m.sb("o", [P, 2, HW])
        one = m.sb("one", [P, 1])
        where = m.sb("where", [P, n_lev + 1, HW])
        where_i = m.sb("where_i", [P, n_lev + 1, HW], I32)
        v_ps, kt_ps, o_ps, st_ps = (m.ps(s, [P, HW]) for s in ("v_ps", "kt_ps", "o_ps", "st_ps"))
        s_ps = m.ps("s_ps", [P, n_lev + 1, HW])
        x_in = [m.sem(f"x_in{u}") for u in range(2)]
        v_in = [m.sem(f"v_in{u}") for u in range(2)]
        o_stored = [m.sem(f"o_stored{u}") for u in range(2)]
        (ones_done, where_done, where_i_done, clamp_done, sig_done, f_done, lf_done, diff_done, decay_done,
         base_done, levels_done, v_ready, v_done, scores_ready, s_done, kt_done, o_ready, o_done, state_done) = (
            m.sem(s) for s in (
                "ones_done", "where_done", "where_i_done", "clamp_done", "sig_done", "f_done", "lf_done",
                "diff_done", "decay_done", "base_done", "levels_done", "v_ready", "v_done", "scores_ready",
                "s_done", "kt_done", "o_ready", "o_done", "state_done"))

        def skewed(eng, *parts, unrolled=()):
            lead_max = max(lead for lead, _ in parts)
            looped = NT - (lead_max + 1) // 2

            def pair(i, us=(0, 1), pairs_left=NT):
                for u in us:
                    for lead, part in parts:
                        if 0 <= u + lead < 2 * pairs_left:
                            part(i + (u + lead) // 2, (u + lead) % 2)

            for n in range(-lead_max, 0):
                pair(0, (n,))
            at = 0
            for stop in unrolled + (looped,):
                if at < stop:
                    with eng.Fori(at, stop) as i:
                        pair(i)
                if stop < looped:
                    pair(stop)
                at = stop + 1
            for i in range(looped, NT):
                pair(i, pairs_left=NT - i)

        def token(i, u):
            return i * P if u == 0 else i * -P + (NT - 1) * P

        with nc.Block() as block:
            @block.sync
            def _(sp):
                def load_gates(i, u):
                    sp.wait_ge(f_done, free(2 * i + u))
                    for j, row in enumerate((ROW_Q, (ROW_FF, ROW_FB)[u])):
                        sp.dma_start(x[:, u, j], proj_t[row:row + HW, ds(token(i, u), P)]
                                     .rearrange("(h p) t -> p h t", p=P)).then_inc(x_in[u], 16)

                def load_v(i, u):
                    sp.wait_ge(v_ready, free(2 * i + u))
                    sp.dma_start(v_t[:, u], proj_t[ROW_V:ROW_V + HW, ds(token(i, u), P)]
                                 .rearrange("(h p) t -> p h t", p=P)).then_inc(v_in[u], 16)

                def store(i, u):
                    sp.wait_ge(o_done, 2 * i + u + 1)
                    sp.dma_start(outputs[u][ds(token(i, u), P), :], o[:, u]).then_inc(o_stored[u], 16)

                skewed(sp, (2, load_v), (5, load_gates), (0, store))
                for u in range(2):
                    sp.wait_ge(o_stored[u], 16 * NT)

            @block.gpsimd
            def _(pool):
                pool.sem_inc(levels_done, PRIME)
                pool.memset(where[:], 1.0).then_inc(ones_done, 1)
                pool.memset(q_dec[:, :, 0:n_lev], 0.0).then_inc(ones_done, 1)
                pool.memset(k_dec[:, :, 0:n_lev], 0.0).then_inc(ones_done, 1)
                pool.wait_ge(ones_done, 3)
                count = 0
                for j, w in enumerate(LEVELS[1:] + (base // 2, base // 2)):
                    pair = 2 * w
                    view = where[:, j].rearrange("p (h m l) -> p h m l", h=HEADS, l=pair)
                    sides = [(0, 1, [[0, HEADS], [-pair, P // pair], [0, pair]]),
                             (pair - 1, -1, [[0, HEADS], [pair, P // pair], [0, pair]])]
                    if j == n_lev - 1:
                        sides.append((0, -1, [[0, HEADS], [pair, P // pair], [1, pair]]))
                    if j == n_lev:
                        sides.append((0, 1, [[0, HEADS], [-pair, P // pair], [-1, pair]]))
                    for start, mult, pattern in sides:
                        pool.affine_select(out=view, in_=view, compare_op=ALU.is_ge, fill=0.0, base=start,
                                           pattern=pattern, channel_multiplier=mult).then_inc(where_done, 1)
                        count += 1
                        pool.wait_ge(where_done, count)
                pool.tensor_copy(where_i[:], where[:]).then_inc(where_i_done, 1)

                def levels(i, u):
                    n = 2 * i + u
                    pool.wait_ge(decay_done, n + 1)
                    pool.wait_ge(scores_ready, free(n))
                    pool.tensor_tensor(q_dec[:, u, n_lev], q[:, u], decay[:, u, n_lev + 1], ALU.mult)
                    for j, w in enumerate(LEVELS):
                        halves = lambda t: t.rearrange("p (g two l) -> p g two l", two=2, l=w)
                        e, qd, kd = (halves(t[:, u, j]) for t in (decay, q_dec, k_dec))
                        pool.tensor_tensor(qd[:, :, late[u]], e[:, :, late[u]], halves(q[:, u])[:, :, late[u]],
                                           ALU.mult)
                        pool.tensor_tensor(kd[:, :, early[u]], e[:, :, early[u]],
                                           halves(k[:, u])[:, :, early[u]], ALU.mult)
                    pool.wait_ge(o_ready, free(n))
                    pool.tensor_tensor(q_dec[:, u, n_lev + 1], q[:, u], from_start[:, u],
                                       ALU.mult).then_inc(levels_done, 1)

                skewed(pool, (2, levels))

            @block.scalar
            def _(act):
                act.preload_act_table_set(ACT_SET)
                act.wait_ge(where_i_done, 1)

                def key_tokens(i, u):
                    act.wait_ge(scores_ready, ready(2 * i + u))
                    act.activation(k_tok[:], kt_ps[:], ACT.Copy).then_inc(kt_done, 1)

                def log_f(i, u):
                    n = 2 * i + u
                    act.wait_ge(f_done, ready(n))
                    act.activation(lf[:, u].rearrange("p h t -> p (h t)"), f[:, u], ACT.Ln).then_inc(lf_done, 1)

                def decays(i, u):
                    n = 2 * i + u
                    act.wait_ge(diff_done, n + 1)
                    act.wait_ge(levels_done, free(n))
                    act.wait_ge(base_done, free(n))
                    act.activation(decay[:, u], diff[:, u], ACT.Exp)
                    act.activation(uncentre[:, u], diff[:, u, n_lev + 1], ACT.Exp, scale=-1.0)
                    act.activation(from_start[:, u], b[:, u].rearrange("p h t -> p (h t)"),
                                   ACT.Exp).then_inc(decay_done, 1)

                def copy_v(i, u):
                    act.wait_ge(v_ready, ready(2 * i + u))
                    act.activation(v[:, u], v_ps[:], ACT.Copy).then_inc(v_done, 1)

                def sigmoid(i, u):
                    n = 2 * i + u
                    act.wait_ge(clamp_done, n + 1)
                    act.activation(sig[:, u], sig[:, u], ACT.Exp, scale=-1.0)
                    act.drain()
                    act.activation(sig[:, u], sig[:, u], ACT.Ln, bias=one[:, 0:1])
                    act.drain()
                    act.activation(sig[:, u], sig[:, u], ACT.Exp, scale=-1.0).then_inc(sig_done, 1)

                def copy_out(i, u):
                    act.wait_ge(o_ready, ready(2 * i + u))
                    act.wait_ge(o_stored[u], 16 * i)
                    act.activation(o[:, u], o_ps[:], ACT.Copy).then_inc(o_done, 1)

                skewed(act, (0, key_tokens), (3, log_f), (2, decays), (1, copy_v), (4, sigmoid), (0, copy_out))

            @block.vector
            def _(dve):
                dve.sem_inc(f_done, PRIME)
                dve.sem_inc(state_done, PRIME)
                dve.sem_inc(base_done, PRIME)
                dve.memset(state[:], 0.0)
                dve.memset(one[:], 1.0)
                dve.wait_ge(where_i_done, 1)
                dve.drain()

                def clamp(i, u):
                    n = 2 * i + u
                    dve.wait_ge(x_in[u], 32 * (i + 1))
                    dve.tensor_scalar(sig[:, u], x[:, u].rearrange("p a h t -> p (a h t)"), -44.0, None,
                                      ALU.max).then_inc(clamp_done, 1)

                def gates(i, u):
                    n = 2 * i + u
                    dve.drain()
                    dve.wait_ge(sig_done, n + 1)
                    dve.wait_ge(levels_done, free(n))
                    dve.tensor_tensor(q[:, u], sig[:, u, 0:HW], x[:, u, 0].rearrange("p h t -> p (h t)"), ALU.mult)
                    for h in range(HEADS):
                        cols = slice(h * P, (h + 1) * P)
                        done = dve.tensor_scalar(f[:, u, cols], sig[:, u, HW + h * P:HW + (h + 1) * P],
                                                 one_minus_lb[:, h:h + 1], lb[:, h:h + 1], ALU.mult, ALU.add)
                    done.then_inc(f_done, 1)
                    dve.drain()
                    dve.tensor_scalar(k[:, u], f[:, u], -1.0, 1.0, ALU.mult, ALU.add)

                def differences(i, u):
                    n = 2 * i + u
                    dve.wait_ge(lf_done, n + 1)
                    for h in range(HEADS):
                        src, dst = lf[:, u, h], b[:, u, h]
                        if u == 1:
                            src, dst = src[:, ::-1], dst[:, ::-1]
                        dve.tensor_tensor_scan(dst, src, src, 0.0, ALU.add, ALU.bypass)
                    dve.drain()
                    for j, w in enumerate(LEVELS):
                        bv = b[:, u].rearrange("p h (m two l) -> p (h m) two l", two=2, l=w)
                        dv = diff[:, u, j].rearrange("p (g two l) -> p g two l", two=2, l=w)
                        at = (w - 1, 0)[u]
                        ref = bv[:, :, early[u], at:at + 1].to_broadcast([P, HW // (2 * w), w])
                        dve.tensor_tensor(dv[:, :, late[u]], bv[:, :, late[u]], ref, ALU.subtract)
                        dve.tensor_tensor(dv[:, :, early[u]], ref, bv[:, :, early[u]], ALU.subtract)
                    dve.tensor_tensor(diff[:, u, n_lev].rearrange("p (h t) -> p h t", h=HEADS),
                                      b[:, u, :, last_t[u]:last_t[u] + 1].to_broadcast([P, HEADS, P]), b[:, u],
                                      ALU.subtract)
                    bv = b[:, u].rearrange("p h (m l) -> p (h m) l", l=base)
                    dve.tensor_tensor(diff[:, u, n_lev + 1].rearrange("p (g l) -> p g l", l=base), bv,
                                      bv[:, :, CENTRE:CENTRE + 1].to_broadcast([P, HW // base, base]),
                                      ALU.subtract).then_inc(diff_done, 1)

                def base_and_state(i, u):
                    n = 2 * i + u
                    dve.drain()
                    dve.wait_ge(decay_done, n + 1)
                    dve.tensor_tensor(k_dec[:, u, n_lev], k[:, u], uncentre[:, u], ALU.mult)
                    dve.tensor_copy(whole[:, u].unsqueeze(2),
                                    from_start[:, u].rearrange("p (h t) -> p h t", h=HEADS)[:, :, last_t[u]:last_t[u] + 1])
                    dve.tensor_tensor(k_dec[:, u, n_lev + 1], k[:, u], decay[:, u, n_lev],
                                      ALU.mult).then_inc(base_done, 1)

                def mask(i, u):
                    dve.wait_ge(scores_ready, ready(2 * i + u))
                    dve.tensor_copy(s_t[:], s_ps[:, 0])
                    for j in range(n_lev):
                        dve.drain()
                        held = where_i[:, j + u if j == n_lev - 1 else j]
                        done = dve.copy_predicated(s_t[:], held, s_ps[:, j + 1])
                    done.then_inc(s_done, 1)

                def carry(i, u):
                    dve.wait_ge(o_ready, ready(2 * i + u))
                    if isinstance(i, int) and i == anew_after[u]:
                        done = dve.memset(state[:, u], 0.0)
                    else:
                        for h in range(HEADS):
                            cols = slice(h * P, (h + 1) * P)
                            done = dve.scalar_tensor_tensor(state[:, u, cols], state[:, u, cols],
                                                            whole[:, u, h:h + 1], st_ps[:, cols],
                                                            ALU.mult, ALU.add)
                    done.then_inc(state_done, 1)

                skewed(dve, (0, mask), (3, differences), (0, carry), (2, base_and_state), (4, gates), (5, clamp),
                       unrolled=(anew_after[1],))

            @block.tensor
            def _(pe):
                pe.sem_inc(v_ready, PRIME)
                pe.sem_inc(scores_ready, PRIME)
                pe.sem_inc(o_ready, PRIME)
                pe.wait_ge(ones_done, 3)

                def transpose_v(i, u):
                    n = 2 * i + u
                    pe.wait_ge(v_in[u], 16 * (i + 1))
                    pe.wait_ge(v_done, n)
                    for h in range(HEADS):
                        done = pe.transpose(v_ps[:, h * P:(h + 1) * P], v_t[:, u, h], ident[:])
                    done.then_inc(v_ready, 1)

                def scores(i, u):
                    n = 2 * i + u
                    pe.wait_ge(base_done, ready(n))
                    pe.wait_ge(levels_done, ready(n))
                    pe.wait_ge(s_done, n)
                    pe.wait_ge(kt_done, n)
                    for h in range(HEADS):
                        cols = slice(h * P, (h + 1) * P)
                        pe.transpose(kt_ps[:, cols], k_dec[:, u, n_lev + 1, cols], ident[:])
                    for j in range(n_lev + 1):
                        for h in range(HEADS):
                            cols = slice(h * P, (h + 1) * P)
                            done = pe.matmul(s_ps[:, j, cols], k_dec[:, u, j, cols], q_dec[:, u, j, cols],
                                             start=True, stop=True)
                    done.then_inc(scores_ready, 1)

                def output(i, u):
                    n = 2 * i + u
                    pe.wait_ge(v_done, n + 1)
                    pe.wait_ge(kt_done, n + 1)
                    pe.wait_ge(state_done, n + PRIME)
                    pe.wait_ge(o_done, n)
                    for h in range(HEADS):
                        cols = slice(h * P, (h + 1) * P)
                        pe.matmul(st_ps[:, cols], k_tok[:, cols], v[:, u, cols], start=True, stop=True)
                    pe.wait_ge(s_done, n + 1)
                    for h in range(HEADS):
                        cols = slice(h * P, (h + 1) * P)
                        pe.matmul(o_ps[:, cols], q_dec[:, u, n_lev + 1, cols], state[:, u, cols],
                                  start=True, stop=False)
                        done = pe.matmul(o_ps[:, cols], s_t[:, cols], v[:, u, cols], start=False, stop=True)
                    done.then_inc(o_ready, 1)

                skewed(pe, (1, transpose_v), (0, output), (1, scores))


def lambda_of(nc, q1, k1, q2, k2, lam):
    with Mem(nc, "lam") as m:
        vecs = m.sb("vecs", [DK, 4])
        prods = m.sb("prods", [DK, 2])
        ones = m.sb("ones", [DK, P])
        e = m.sb("e", [P, 2])
        sums = m.ps("sums", [P, 2])
        vecs_in, prods_done, sums_done, exp_done = (
            m.sem(s) for s in ("vecs_in", "prods_done", "sums_done", "exp_done"))
        with nc.Block() as block:
            @block.sync
            def _(sp):
                with nc.allow_non_contiguous_dma(reason="four columns of 64 numbers"):
                    for j, vec in enumerate((q1, q2, k1, k2)):
                        sp.dma_start(vecs[:, j:j + 1], vec.rearrange("(p a) -> p a", a=1)).then_inc(vecs_in, 16)

            @block.vector
            def _(dve):
                dve.memset(ones[:], 1.0)
                dve.wait_ge(vecs_in, 64)
                dve.tensor_tensor(prods[:], vecs[:, 0:2], vecs[:, 2:4], ALU.mult).then_inc(prods_done, 1)
                dve.wait_ge(exp_done, 1)
                dve.tensor_tensor(lam[:], e[:, 0:1], e[:, 1:2], ALU.subtract)
                dve.drain()
                dve.tensor_scalar(lam[:], lam[:], LAM_INIT, None, ALU.add)

            @block.tensor
            def _(pe):
                pe.wait_ge(prods_done, 1)
                pe.matmul(sums[:], ones[:], prods[:], start=True, stop=True).then_inc(sums_done, 1)

            @block.scalar
            def _(act):
                act.preload_act_table_set(ACT_SET)
                act.wait_ge(sums_done, 1)
                act.activation(e[:], sums[:], ACT.Exp).then_inc(exp_done, 1)


def diff_attention(nc, tag, proj_t, first, seq, g_da, lam, ident, eps, mix_out):
    nk = seq // P
    slopes = [2.0 ** (-8.0 * (h + 1) / HEADS) for h in range(HEADS)]
    width = 2 * seq - P
    banks = [(at, min(512, seq)) for at in range(0, seq, 512)]
    with Mem(nc, tag) as m:
        keys = m.sb("keys", [DK, 2, HEADS * seq])
        v_t = m.sb("v_t", [P, HEADS, seq])
        v = m.sb("v", [P, nk, HW])
        where = m.sb("where", [P, width])
        bias = m.sb("bias", [P, width])
        gain = m.sb("gain", [P, P])
        query = m.sb("query", [DK, 2, HEADS * seq])
        scaled = m.sb("scaled", [DK, 2, 2, P])
        q_factor, slope, minus_slope = (m.sb(s, [P, HEADS]) for s in ("q_factor", "slope", "minus_slope"))
        score = m.sb("score", [P, 2, 2, seq])
        prob = m.sb("prob", [P, 2, 2, seq])
        attn_t = m.sb("attn_t", [P, seq])
        top = m.sb("top", [P, 2, 2])
        total = m.sb("total", [P, 2, 2])
        o_in = m.sb("o_in", [P, 2, P])
        sq = m.sb("sq", [P, P])
        ss, rstd = m.sb("ss", [P, 1]), m.sb("rstd", [P, 1])
        o = m.sb("o", [P, 2, P])
        score_ps = m.ps("score_ps", [P, 2, max(512, seq)])
        attn_ps = m.ps("attn_ps", [P, max(512, seq)])
        o_ps = m.ps("o_ps", [P, 2, 512])
        stored = [m.sem(f"stored{u}") for u in range(2)]
        (loaded, slopes_done, where_done, q_done, v_ready, v_done, scores_ready, top_done, prob_done,
         attn_done, attn_t_ready, attn_t_done, o_ready, rstd_done, o_done) = (m.sem(s) for s in (
             "loaded", "slopes_done", "where_done", "q_done", "v_ready", "v_done", "scores_ready", "top_done",
             "prob_done", "attn_done", "attn_t_ready", "attn_t_done", "o_ready", "rstd_done",
             "o_done"))
        score_read = [m.sem(f"score_read{c}") for c in range(2)]
        per_buffer = HEADS * nk // 2

        def skewed(eng, *parts):
            lead_max = max(lead for lead, _ in parts)

            def slot(h, t, heads_left):
                for lead, part in parts:
                    if 0 <= t + lead < nk * heads_left:
                        part(h + (t + lead) // nk, (t + lead) % nk)

            for t in range(-lead_max, 0):
                slot(0, t, HEADS)
            looped = HEADS - 1 if nk > lead_max else 0
            if looped:
                with eng.Fori(0, looped) as h:
                    for t in range(nk):
                        slot(h, t, 2)
            for h in range(looped, HEADS):
                for t in range(nk):
                    slot(h, t, HEADS - h)

        def step(h, t):
            return h * nk + t

        def uses(h, t):
            return h * (nk // 2) + t // 2

        with nc.Block() as block:
            @block.sync
            def _(sp):
                for heads, row in ((query, ROW_DQ), (keys, ROW_DK)):
                    for c in range(2):
                        sp.dma_start(heads[:, c].rearrange("p (h t) -> p h t", h=HEADS),
                                     proj_t[row:row + HW, first:first + seq]
                                     .rearrange("(h c p) t -> c p h t", c=2, p=DK)[c]).then_inc(loaded, 16)
                sp.dma_start(v_t[:], proj_t[ROW_DV:ROW_DV + HW, first:first + seq]
                             .rearrange("(h p) t -> p h t", p=P)).then_inc(loaded, 16)
                with nc.allow_non_contiguous_dma(reason="one row for all partitions"):
                    sp.dma_start(gain[:], g_da.rearrange("(a n) -> a n", a=1).to_broadcast([P, P])).then_inc(loaded, 16)

            @block.gpsimd
            def _(pool):
                pool.iota(where[:], [[-1, width]], base=seq - P, channel_multiplier=1,
                          allow_small_or_imprecise_dtypes=True).then_inc(where_done, 1)
                with pool.Fori(0, HEADS) as h:
                    for t in range(nk):
                        pool.wait_ge(o_done, step(h, t) + 1)
                        pool.dma_start(mix_out[first + t * P:first + (t + 1) * P, ds(h * P + HW, P)],
                                       o[:, t % 2]).then_inc(stored[t % 2], 16)
                for u in range(2):
                    pool.wait_ge(stored[u], 16 * per_buffer)

            @block.vector
            def _(dve):
                for h in range(HEADS):
                    dve.memset(q_factor[:, h:h + 1], DA_SCALE / slopes[h])
                    dve.memset(slope[:, h:h + 1], slopes[h])
                    last = dve.memset(minus_slope[:, h:h + 1], -slopes[h])
                last.then_inc(slopes_done, 1)
                dve.wait_ge(where_done, 1)
                dve.scalar_tensor_tensor(bias[:], where[:], -1.0, where[:], ALU.mult, ALU.min)
                dve.wait_ge(loaded, 96)
                dve.tensor_scalar(gain[:], gain[:], 1.0 - LAM_INIT, None, ALU.mult)
                dve.drain()

                def scale_query(h, t):
                    n, u = step(h, t), t % 2
                    dve.wait_ge(scores_ready, 2 * n + 2)
                    wait_apart(dve)
                    dve.tensor_scalar(scaled[:, u], query[:, :, ds(h * seq + t * P, P)], q_factor[0:DK, ds(h, 1)],
                                      None, ALU.mult).then_inc(q_done, 1)

                def find_top(h, t):
                    n, u = step(h, t), t % 2
                    col = seq - P - t * P
                    for c in range(2):
                        dve.wait_ge(scores_ready, 2 * n + c + 1 + 2 * PRIME)
                        wait_apart(dve)
                        dve.tensor_tensor_reduce(out=score[:, u, c], in0=score_ps[:, c, 0:seq],
                                                 in1=bias[:, col:col + seq], scale=1.0, scalar=-3.0e38,
                                                 op0=ALU.add, op1=ALU.max,
                                                 accum_out=top[:, u, c:c + 1]).then_inc(score_read[c], 1)
                    dve.drain()
                    dve.tensor_scalar(top[:, u], top[:, u], minus_slope[:, ds(h, 1)], None,
                                      ALU.mult).then_inc(top_done, 1)

                def attention(h, t):
                    n, u = step(h, t), t % 2
                    dve.wait_ge(prob_done, n + 1)
                    dve.reciprocal(total[:, u], total[:, u])
                    dve.drain()
                    dve.tensor_tensor(total[:, u, 1:2], total[:, u, 1:2], lam[:], ALU.mult)
                    dve.drain()
                    dve.tensor_scalar(prob[:, u, 1], prob[:, u, 1], total[:, u, 1:2], None, ALU.mult)
                    dve.drain()
                    dve.scalar_tensor_tensor(prob[:, u, 0], prob[:, u, 0], total[:, u, 0:1], prob[:, u, 1],
                                             ALU.mult, ALU.subtract).then_inc(attn_done, 1)

                def head_norm(h, t):
                    n, u = step(h, t), t % 2
                    dve.wait_ge(rstd_done, ready(n))
                    dve.wait_ge(stored[u], uses(h, t) * 16)
                    dve.scalar_tensor_tensor(o[:, u], o_in[:, u], rstd[:, 0:1], gain[:], ALU.mult,
                                             ALU.mult).then_inc(o_done, 1)

                skewed(dve, (3, scale_query), (1, attention), (3, find_top), (0, head_norm))

            @block.scalar
            def _(act):
                act.preload_act_table_set(ACT_SET)
                act.sem_inc(rstd_done, PRIME)
                act.wait_ge(slopes_done, 1)
                for t in range(nk):
                    act.wait_ge(v_ready, t + 1)
                    act.activation(v[:, t], attn_ps[:, 0:HW], ACT.Copy).then_inc(v_done, 1)

                def exps(h, t):
                    n, u = step(h, t), t % 2
                    act.wait_ge(top_done, n + 1)
                    act.wait_ge(attn_t_ready, free(n))
                    wait_apart(act)
                    for c in range(2):
                        done = act.activation(prob[:, u, c], score[:, u, c], ACT.Exp, scale=slope[:, ds(h, 1)],
                                              bias=top[:, u, c:c + 1], accum_out=total[:, u, c:c + 1])
                    done.then_inc(prob_done, 1)

                def copy_attention(h, t):
                    n = step(h, t)
                    act.wait_ge(attn_t_ready, ready(n))
                    act.wait_ge(o_ready, n)
                    act.activation(attn_t[:], attn_ps[:, 0:seq], ACT.Copy).then_inc(attn_t_done, 1)

                def head_rstd(h, t):
                    n, u = step(h, t), t % 2
                    act.wait_ge(o_ready, n + 1)
                    act.wait_ge(o_done, n)
                    act.activation(o_in[:, u], o_ps[:, u, 0:P], ACT.Copy)
                    act.activation(sq[:], o_ps[:, u, 0:P], ACT.Square, accum_out=ss[:])
                    act.drain()
                    act.activation(rstd[:], ss[:], ACT.Ln, scale=1.0 / P, bias=eps[:, 0:1])
                    act.drain()
                    act.activation(rstd[:], rstd[:], ACT.Exp, scale=-0.5).then_inc(rstd_done, 1)

                skewed(act, (2, exps), (0, head_rstd), (1, copy_attention))

            @block.tensor
            def _(pe):
                pe.sem_inc(scores_ready, 2 * PRIME)
                pe.sem_inc(attn_t_ready, PRIME)
                pe.wait_ge(loaded, 96)
                for t in range(nk):
                    pe.wait_ge(v_done, t)
                    for h in range(HEADS):
                        last = pe.transpose(attn_ps[:, h * P:(h + 1) * P], v_t[:, h, t * P:(t + 1) * P], ident[:])
                    last.then_inc(v_ready, 1)
                pe.wait_ge(v_done, nk)

                def scores(h, t):
                    n, u = step(h, t), t % 2
                    pe.wait_ge(q_done, n + 1)
                    for c in range(2):
                        pe.wait_ge(score_read[c], n)
                        wait_apart(pe)
                        for at, size in banks:
                            last = pe.matmul(score_ps[:, c, at:at + size], scaled[:, u, c],
                                             keys[:, c, ds(h * seq + at, size)], start=True, stop=True)
                        last.then_inc(scores_ready, 1)

                def transposes(h, t):
                    n, u = step(h, t), t % 2
                    pe.wait_ge(attn_done, n + 1)
                    pe.wait_ge(attn_t_done, n)
                    for c in range(nk):
                        last = pe.transpose(attn_ps[:, c * P:(c + 1) * P], prob[:, u, 0, c * P:(c + 1) * P], ident[:])
                    last.then_inc(attn_t_ready, 1)

                def output(h, t):
                    n, u = step(h, t), t % 2
                    pe.wait_ge(attn_t_done, n + 1)
                    pe.wait_ge(rstd_done, free(n))
                    for c in range(nk):
                        last = pe.matmul(o_ps[:, u, 0:P], attn_t[:, c * P:(c + 1) * P], v[:, c, ds(h * P, P)],
                                         start=(c == 0), stop=(c == nk - 1))
                    last.then_inc(o_ready, 1)

                skewed(pe, (0, output), (3, scores), (1, transposes))


def split_weight(nc, tag, weight, high, low):
    with Mem(nc, tag) as m:
        raw = m.sb("raw", [P, 2, D])
        w_in = [m.sem(f"w_in{u}") for u in range(2)]
        high_done, low_done = m.sem("high_done"), m.sem("low_done")
        with nc.Block() as block:
            @block.sync
            def _(sp):
                for k in range(KC):
                    sp.wait_ge(low_done, free(k))
                    sp.dma_start(raw[:, k % 2], weight[k * P:(k + 1) * P, :]).then_inc(w_in[k % 2], 16)

            @block.scalar
            def _(act):
                act.preload_act_table_set(ACT_SET)
                for k in range(KC):
                    act.wait_ge(w_in[k % 2], 16 * (k // 2 + 1))
                    act.activation(high[:, k], raw[:, k % 2], ACT.Copy).then_inc(high_done, 1)

            @block.vector
            def _(dve):
                dve.sem_inc(low_done, PRIME)
                for k in range(KC):
                    dve.wait_ge(high_done, k + 1)
                    dve.tensor_tensor(low[:, k], raw[:, k % 2], high[:, k].bitcast(F32),
                                      ALU.subtract).then_inc(low_done, 1)


def tile_pairs(eng, body, sources):
    at = 0
    for rows, tiles in sources:
        if tiles > 2:
            with eng.Fori(0, tiles // 2) as j:
                body(j + at, rows, j)
        else:
            body(at, rows, 0)
        at += tiles // 2


def skewed_pairs(eng, front, back):
    last = NT // 2 - 1
    front(0, 0)
    with eng.Fori(0, last) as i:
        for u in range(2):
            front(i + u, 1 - u)
            back(i, u)
    front(last, 1)
    for u in range(2):
        back(last, u)


def mix_out(nc, tag, o_fwd, o_bwd, proj_t, mix, x_rows, g_hg, w_high, w_low, ident, eps, x1_out):
    with Mem(nc, tag) as m:
        of = m.sb("of", [P, 2, HW])
        ob = m.sb("ob", [P, 2, HW])
        gate_t = m.sb("gate_t", [P, 2, HEADS, P])
        mixed = m.sb("mixed", [P, 2, D])
        x = m.sb("x", [P, 2, D])
        gain = m.sb("gain", [P, HW])
        e = m.sb("e", [P, HW])
        sq = m.sb("sq", [P, HW])
        silu = m.sb("silu", [P, HW])
        ss, rstd = m.sb("ss", [P, HEADS]), m.sb("rstd", [P, HEADS])
        m_high, m_low = m.sb("m_high", [P, KC, P], F32R), m.sb("m_low", [P, KC, P], F32R)
        x1 = m.sb("x1", [P, 2, D])
        gate_ps = m.ps("gate_ps", [P, HW])
        mt_ps = m.ps("mt_ps", [P, D])
        out_ps = m.ps("out_ps", [P, 2, D])
        t_in = [m.sem(f"t_in{u}") for u in range(2)]
        stored = [m.sem(f"stored{u}") for u in range(2)]
        (gain_in, gate_ready, e_done, ss_done, rstd_done, mixed_done, mt_ready, high_done, low_done, out_ready,
         x1_done) = (m.sem(s) for s in ("gain_in", "gate_ready", "e_done", "ss_done", "rstd_done", "mixed_done",
                                        "mt_ready", "high_done", "low_done", "out_ready", "x1_done"))
        with nc.Block() as block:
            @block.sync
            def _(sp):
                with nc.allow_non_contiguous_dma(reason="one row for all partitions"):
                    sp.dma_start(gain[:], g_hg.rearrange("(a n) -> a n", a=1).to_broadcast([P, HW])).then_inc(gain_in, 16)

                def load(i, rows, j):
                    for u in range(2):
                        n = 2 * i + u
                        t = ds(i * (2 * P) + u * P, P)
                        sp.wait_ge(mt_ready, free(n))
                        sp.wait_ge(x1_done, free(n))
                        sp.dma_start(of[:, u], o_fwd[t, :]).then_inc(t_in[u], 16)
                        sp.dma_start(ob[:, u], o_bwd[t, :]).then_inc(t_in[u], 16)
                        sp.dma_start(gate_t[:, u], proj_t[ROW_G:ROW_G + HW, t]
                                     .rearrange("(h p) t -> p h t", p=P)).then_inc(t_in[u], 16)
                        sp.dma_start(mixed[:, u, HW:], mix[t, HW:]).then_inc(t_in[u], 16)
                        sp.dma_start(x[:, u], rows[ds(j * (2 * P) + u * P, P), :]).then_inc(t_in[u], 16)

                tile_pairs(sp, load, x_rows)

            @block.gpsimd
            def _(pool):
                with pool.Fori(0, NT // 2) as i:
                    for u in range(2):
                        pool.wait_ge(x1_done, ready(2 * i + u))
                        pool.dma_start(x1_out[ds(i * (2 * P) + u * P, P), :], x1[:, u]).then_inc(stored[u], 16)
                for u in range(2):
                    pool.wait_ge(stored[u], 16 * (NT // 2))

            @block.scalar
            def _(act):
                act.preload_act_table_set(ACT_SET)

                def front(i, u):
                    n = 2 * i + u
                    act.wait_ge(gate_ready, n + 1)
                    act.activation(e[:], gate_ps[:], ACT.Exp, scale=-1.0).then_inc(e_done, 1)
                    act.wait_ge(ss_done, n + 1)
                    act.activation(rstd[:], ss[:], ACT.Ln, scale=1.0 / P, bias=eps[:, 0:1])
                    act.drain()
                    act.activation(rstd[:], rstd[:], ACT.Exp, scale=-0.5).then_inc(rstd_done, 1)

                def back(i, u):
                    n = 2 * i + u
                    act.wait_ge(mt_ready, ready(n))
                    act.wait_ge(out_ready, n)
                    act.activation(m_high[:].rearrange("p k t -> p (k t)"), mt_ps[:], ACT.Copy).then_inc(high_done, 1)

                skewed_pairs(act, front, back)

            @block.vector
            def _(dve):
                dve.sem_inc(x1_done, PRIME)
                dve.wait_ge(gain_in, 16)

                def front(i, u):
                    n = 2 * i + u
                    dve.wait_ge(t_in[u], 80 * (i + 1))
                    dve.tensor_tensor(of[:, u], of[:, u], ob[:, u], ALU.add)
                    dve.drain()
                    dve.tensor_tensor(sq[:], of[:, u], of[:, u], ALU.mult)
                    dve.drain()
                    dve.tensor_reduce(ss[:], sq[:].rearrange("p (h c) -> p h c", h=HEADS), AX.X,
                                      ALU.add).then_inc(ss_done, 1)
                    dve.wait_ge(e_done, n + 1)
                    dve.tensor_scalar(silu[:], e[:], 1.0, None, ALU.add)
                    dve.drain()
                    dve.reciprocal(silu[:], silu[:])
                    dve.drain()
                    dve.tensor_tensor(silu[:], gate_ps[:], silu[:], ALU.mult)
                    dve.tensor_tensor(of[:, u], of[:, u], gain[:], ALU.mult)
                    dve.drain()
                    dve.tensor_tensor(silu[:], silu[:], of[:, u], ALU.mult)
                    dve.wait_ge(rstd_done, n + 1)
                    wait_apart(dve)
                    dve.drain()
                    heads = lambda t: t.rearrange("p (h c) -> p h c", h=HEADS)
                    dve.tensor_tensor(heads(mixed[:, u, 0:HW]), heads(silu[:]),
                                      rstd[:].unsqueeze(2).to_broadcast([P, HEADS, P]),
                                      ALU.mult).then_inc(mixed_done, 1)

                def back(i, u):
                    n = 2 * i + u
                    dve.wait_ge(high_done, n + 1)
                    dve.tensor_tensor(m_low[:].rearrange("p k t -> p (k t)"), mt_ps[:],
                                      m_high[:].rearrange("p k t -> p (k t)").bitcast(F32),
                                      ALU.subtract).then_inc(low_done, 1)
                    dve.wait_ge(out_ready, n + 1)
                    dve.wait_ge(stored[u], 16 * i)
                    dve.tensor_tensor(x1[:, u], out_ps[:, u], x[:, u], ALU.add).then_inc(x1_done, 1)

                skewed_pairs(dve, front, back)

            @block.tensor
            def _(pe):
                pe.sem_inc(mt_ready, PRIME)

                def front(i, u):
                    n = 2 * i + u
                    pe.wait_ge(t_in[u], 80 * (i + 1))
                    pe.wait_ge(mixed_done, n)
                    for h in range(HEADS):
                        last = pe.transpose(gate_ps[:, h * P:(h + 1) * P], gate_t[:, u, h], ident[:])
                    last.then_inc(gate_ready, 1)

                def back(i, u):
                    n = 2 * i + u
                    pe.wait_ge(mixed_done, n + 1)
                    for k in range(KC):
                        last = pe.transpose(mt_ps[:, k * P:(k + 1) * P], mixed[:, u, k * P:(k + 1) * P], ident[:])
                    last.then_inc(mt_ready, 1)
                    pe.wait_ge(low_done, n + 1)
                    pe.wait_ge(x1_done, free(n))
                    for half in (slice(0, 512), slice(512, D)):
                        for k in range(KC):
                            last = product3(pe, out_ps[:, u, half], (m_high[:, k], m_low[:, k]),
                                            (w_high[:, k, half], w_low[:, k, half]), k == 0, k == KC - 1)
                    last.then_inc(out_ready, 1)

                skewed_pairs(pe, front, back)


def cross_attention(nc, tag, q_t, kv_t, x1_rows, w_high, w_low, ident, x2_out):
    NM = 2 * N_MEM
    MC = N_MEM // P
    DC = CA_DH // P
    with Mem(nc, tag) as m:
        keys = m.sb("keys", [P, KC, NM])
        v_t = m.sb("v_t", [P, KC, NM])
        v = m.sb("v", [P, NM // P, D])
        q = m.sb("q", [P, 2, KC, P])
        x1 = m.sb("x1", [P, 2, D])
        top = m.sb("top", [P, 2, HEADS])
        total = m.sb("total", [P, 2, HEADS])
        prob = m.sb("prob", [P, 2, D])
        prob_t = m.sb("prob_t", [P, 2 * HEADS, P])
        o_high, o_low = m.sb("o_high", [P, KC, P], F32R), m.sb("o_low", [P, KC, P], F32R)
        x2 = m.sb("x2", [P, 2, D])
        score_ps, pt_ps, ot_ps, out_ps = (m.ps(s, [P, D]) for s in ("score_ps", "pt_ps", "ot_ps", "out_ps"))
        t_in = [m.sem(f"t_in{u}") for u in range(2)]
        stored = [m.sem(f"stored{u}") for u in range(2)]
        (loaded, v_ready, v_done, scores_ready, top_done, exp_done, prob_done, pt_ready, pt_done, ot_ready,
         high_done, low_done, out_ready, x2_done) = (m.sem(s) for s in (
             "loaded", "v_ready", "v_done", "scores_ready", "top_done", "exp_done", "prob_done", "pt_ready",
             "pt_done", "ot_ready", "high_done", "low_done", "out_ready", "x2_done"))

        def skewed_groups(eng, front, back):
            last = NT_P // 2 - 1
            front(0, 0, 0)
            with eng.Fori(0, last) as i:
                for u in range(2):
                    front(i + u, 1 - u, 0)
                    back(i, u, 0)
            front(last, 1, 0)
            back(last, 0, 0)
            front(last + 1, 0, 1)
            back(last, 1, 0)
            front(last + 1, 1, 1)
            for u in range(2):
                back(last + 1, u, 1)

        with nc.Block() as block:
            @block.sync
            def _(sp):
                for k in range(KC):
                    sp.dma_start(keys[:, k], kv_t[k * P:(k + 1) * P, :]).then_inc(loaded, 16)
                for k in range(KC):
                    sp.dma_start(v_t[:, k], kv_t[D + k * P:D + (k + 1) * P, :]).then_inc(loaded, 16)
                with sp.Fori(0, NT // 2) as i:
                    for u in range(2):
                        n = 2 * i + u
                        t = ds(i * (2 * P) + u * P, P)
                        sp.wait_ge(x2_done, free(n))
                        sp.dma_start(q[:, u], q_t[:, t].rearrange("(k p) t -> p k t", p=P)).then_inc(t_in[u], 16)
                        sp.dma_start(x1[:, u], x1_rows[t, :]).then_inc(t_in[u], 16)

            @block.gpsimd
            def _(pool):
                with pool.Fori(0, NT // 2) as i:
                    for u in range(2):
                        pool.wait_ge(x2_done, ready(2 * i + u))
                        pool.dma_start(x2_out[ds(i * (2 * P) + u * P, P), :], x2[:, u]).then_inc(stored[u], 16)
                for u in range(2):
                    pool.wait_ge(stored[u], 16 * (NT // 2))

            @block.scalar
            def _(act):
                act.preload_act_table_set(ACT_SET)
                for t in range(NM // P):
                    act.wait_ge(v_ready, t + 1)
                    act.activation(v[:, t], pt_ps[:], ACT.Copy).then_inc(v_done, 1)

                def front(i, u, group):
                    n = 2 * i + u
                    act.wait_ge(top_done, n + 1)
                    act.wait_ge(pt_ready, free(n))
                    for h in range(HEADS):
                        cols = slice(h * N_MEM, (h + 1) * N_MEM)
                        done = act.activation(prob[:, u, cols], score_ps[:, cols], ACT.Exp, scale=CA_SCALE,
                                              bias=top[:, u, h:h + 1], accum_out=total[:, u, h:h + 1])
                    done.then_inc(exp_done, 1)

                def back(i, u, group):
                    n = 2 * i + u
                    act.wait_ge(pt_ready, ready(n))
                    act.activation(prob_t[:].rearrange("p c t -> p (c t)"), pt_ps[:], ACT.Copy).then_inc(pt_done, 1)
                    act.wait_ge(ot_ready, n + 1)
                    act.activation(o_high[:].rearrange("p k t -> p (k t)"), ot_ps[:], ACT.Copy).then_inc(high_done, 1)

                skewed_groups(act, front, back)

            @block.vector
            def _(dve):
                dve.sem_inc(x2_done, PRIME)

                def front(i, u, group):
                    n = 2 * i + u
                    dve.wait_ge(scores_ready, n + 1)
                    dve.tensor_reduce(top[:, u], score_ps[:].rearrange("p (h c) -> p h c", h=HEADS), AX.X, ALU.max)
                    dve.drain()
                    dve.tensor_scalar(top[:, u], top[:, u], -CA_SCALE, None, ALU.mult).then_inc(top_done, 1)
                    dve.wait_ge(exp_done, n + 1)
                    dve.reciprocal(total[:, u], total[:, u])
                    dve.drain()
                    heads = prob[:, u].rearrange("p (h c) -> p h c", h=HEADS)
                    dve.tensor_tensor(heads, heads, total[:, u].unsqueeze(2).to_broadcast([P, HEADS, N_MEM]),
                                      ALU.mult).then_inc(prob_done, 1)

                def back(i, u, group):
                    n = 2 * i + u
                    dve.wait_ge(high_done, n + 1)
                    dve.tensor_tensor(o_low[:].rearrange("p k t -> p (k t)"), ot_ps[:],
                                      o_high[:].rearrange("p k t -> p (k t)").bitcast(F32),
                                      ALU.subtract).then_inc(low_done, 1)
                    dve.wait_ge(out_ready, n + 1)
                    dve.wait_ge(stored[u], 16 * i)
                    dve.tensor_tensor(x2[:, u], out_ps[:], x1[:, u], ALU.add).then_inc(x2_done, 1)

                skewed_groups(dve, front, back)

            @block.tensor
            def _(pe):
                pe.sem_inc(pt_ready, PRIME)
                pe.wait_ge(loaded, 16 * 2 * KC)
                for t in range(NM // P):
                    pe.wait_ge(v_done, t)
                    for k in range(KC):
                        last = pe.transpose(pt_ps[:, k * P:(k + 1) * P], v_t[:, k, t * P:(t + 1) * P], ident[:])
                    last.then_inc(v_ready, 1)
                pe.wait_ge(v_done, NM // P)

                def front(i, u, group):
                    n = 2 * i + u
                    pe.wait_ge(t_in[u], 32 * (i + 1))
                    pe.wait_ge(exp_done, n)
                    for h in range(HEADS):
                        for c in range(DC):
                            k = h * DC + c
                            last = pe.matmul(score_ps[:, h * N_MEM:(h + 1) * N_MEM], q[:, u, k],
                                             keys[:, k, group * N_MEM:(group + 1) * N_MEM],
                                             start=(c == 0), stop=(c == DC - 1))
                    last.then_inc(scores_ready, 1)

                def back(i, u, group):
                    n = 2 * i + u
                    pe.wait_ge(prob_done, n + 1)
                    pe.wait_ge(pt_done, n)
                    for c in range(2 * HEADS):
                        last = pe.transpose(pt_ps[:, c * P:(c + 1) * P], prob[:, u, c * P:(c + 1) * P], ident[:])
                    last.then_inc(pt_ready, 1)
                    pe.wait_ge(pt_done, n + 1)
                    pe.wait_ge(low_done, n)
                    for k in range(KC):
                        h = k // DC
                        for c in range(MC):
                            last = pe.matmul(ot_ps[:, k * P:(k + 1) * P], v[:, group * MC + c, k * P:(k + 1) * P],
                                             prob_t[:, h * MC + c], start=(c == 0), stop=(c == MC - 1))
                    last.then_inc(ot_ready, 1)
                    pe.wait_ge(low_done, n + 1)
                    pe.wait_ge(x2_done, n + PRIME)
                    for half in (slice(0, 512), slice(512, D)):
                        for k in range(KC):
                            last = product3(pe, out_ps[:, half], (o_high[:, k], o_low[:, k]),
                                            (w_high[:, k, half], w_low[:, k, half]), k == 0, k == KC - 1)
                    last.then_inc(out_ready, 1)

                skewed_groups(pe, front, back)


def router(nc, tag, h_high, h_low, w_rg, b_rg, w_re, b_re, ident, slots, slot_i, weight, expert_i, last_pair):
    NL = N_GROUPS + N_EXP
    NB = MAX_BLOCKS
    with Mem(nc, tag) as m:
        w = m.sb("w", [P, KC, P])
        w_high, w_low = m.sb("w_high", [P, KC, P], F32R), m.sb("w_low", [P, KC, P], F32R)
        logits_t = m.sb("logits_t", [P, T])
        bias = m.sb("bias", [P, NL])
        logits = m.sb("logits", [P, NT, NL])
        first_g = m.sb("first_g", [P, N_GROUPS])
        first_e = m.sb("first_e", [P, N_EXP])
        before = m.sb("before", [P, P])
        ones = m.sb("ones", [P, P])
        block_no = m.sb("block_no", [P, NB])
        entry = m.sb("entry", [P, 2, NT, 2], I32)
        unused = m.sb("unused", [P, NB, 2], I32)
        g_top, g_sum, e_top1, e_top2, e_diff, e_sum, pick = (
            m.sb(s, [P, NT]) for s in ("g_top", "g_sum", "e_top1", "e_top2", "e_diff", "e_sum", "pick"))
        g_one = m.sb("g_one", [P, NT, N_GROUPS])
        g_exp = m.sb("g_exp", [P, NT, N_GROUPS])
        masked = m.sb("masked", [P, NT, N_EXP])
        chosen = m.sb("chosen", [P, 2, NT, N_EXP])
        both = m.sb("both", [P, NT, N_EXP])
        place = m.sb("place", [P, NT, N_EXP])
        carry = m.sb("carry", [P, NT + 1, N_EXP])
        blocks = m.sb("blocks", [P, N_EXP])
        blocks_i = m.sb("blocks_i", [P, N_EXP], I32)
        block_end = m.sb("block_end", [P, N_EXP])
        start = m.sb("start", [P, N_EXP])
        dest = m.sb("dest", [P, 2, NT])
        dest_i = m.sb("dest_i", [P, 2, NT], I32)
        table_i = m.sb("table_i", [NB, P, 2], I32)
        table = m.sb("table", [NB, 2, P])
        past = m.sb("past", [P, NB, N_EXP])
        expert = m.sb("expert", [P, NB])
        logits_ps = m.ps("logits_ps", [P, 1536])
        tr_ps = m.ps("tr_ps", [P, 512])
        rank_ps = m.ps("rank_ps", [P, 512])
        sum_ps = m.ps("sum_ps", [P, 512])
        (loaded, cleared, tables, w_done, w_high_done, w_low_done, lt_ready, lt_done, tr_ready, g_shifted,
         g_exp_done, e_diff_done, e_exp_done, both_done, rank_ready, dest_done, table_cleared, scattered, table_in, table_done, table_ready) = (
            m.sem(s) for s in (
                "loaded", "cleared", "tables", "w_done", "w_high_done", "w_low_done", "lt_ready", "lt_done",
                "tr_ready", "g_shifted", "g_exp_done", "e_diff_done", "e_exp_done", "both_done", "rank_ready",
                "dest_done", "table_cleared", "scattered", "table_in", "table_done", "table_ready"))
        with nc.Block() as block:
            @block.sync
            def _(sp):
                sp.wait_ge(w_done, 1)
                with nc.allow_non_contiguous_dma(reason="short rows of router weights"):
                    sp.dma_start(w[:, :, 0:N_GROUPS], w_rg.rearrange("(k p) n -> p k n", p=P)).then_inc(loaded, 16)
                    sp.dma_start(w[:, :, N_GROUPS:NL], w_re.rearrange("(k p) n -> p k n", p=P)).then_inc(loaded, 16)
                    sp.dma_start(bias[:, 0:N_GROUPS],
                                 b_rg.rearrange("(a n) -> a n", a=1).to_broadcast([P, N_GROUPS])).then_inc(loaded, 16)
                    sp.dma_start(bias[:, N_GROUPS:NL],
                                 b_re.rearrange("(a n) -> a n", a=1).to_broadcast([P, N_EXP])).then_inc(loaded, 16)
                sp.wait_ge(cleared, 3)
                sp.dma_start(slots.rearrange("(p b) a -> p b a", p=P), unused[:]).then_inc(table_cleared, 16)
                sp.wait_ge(scattered, 16 * 2 * NT)
                sp.dma_start(table_i[:], slots.rearrange("(b p) a -> b p a", p=P)).then_inc(table_in, 16)

            @block.gpsimd
            def _(pool):
                pool.memset(before[:], 1.0).then_inc(cleared, 1)
                pool.memset(unused[:, :, 0], 0).then_inc(cleared, 1)
                pool.memset(unused[:, :, 1], 2 * T).then_inc(cleared, 1)
                pool.memset(ones[:], 1.0).then_inc(tables, 1)
                pool.wait_ge(cleared, 3)
                pool.affine_select(out=before[:], in_=before[:], compare_op=ALU.is_gt, fill=0.0, base=0,
                                   pattern=[[1, P]], channel_multiplier=-1).then_inc(tables, 1)
                for table, step, base, width in ((first_g, -1, N_GROUPS, N_GROUPS), (first_e, -1, N_EXP, N_EXP),
                                                 (block_no, 1, 0, NB)):
                    pool.iota(table[:], [[step, width]], base=base, channel_multiplier=0,
                              allow_small_or_imprecise_dtypes=True).then_inc(tables, 1)
                pool.iota(entry[:, :, :, 0], [[0, 2], [P, NT]], base=0, channel_multiplier=1).then_inc(tables, 1)
                pool.iota(entry[:, :, :, 1], [[T, 2], [P, NT]], base=0, channel_multiplier=1).then_inc(tables, 1)
                pool.wait_ge(tables, 7)
                pool.wait_ge(dest_done, 1)
                pool.wait_ge(table_cleared, 16)
                for c in range(2):
                    for t in range(NT):
                        pool.indirect_dma_start(
                            out=slots, out_offset=bass.IndirectOffsetOnAxis(ap=dest_i[:, c, t:t + 1], axis=0),
                            in_=entry[:, c, t], in_offset=None).then_inc(scattered, 16)
                pool.wait_ge(scattered, 16 * 2 * NT)

            @block.scalar
            def _(act):
                act.preload_act_table_set(ACT_SET)
                act.wait_ge(loaded, 64)
                act.activation(w_high[:], w[:], ACT.Copy).then_inc(w_high_done, 1)
                act.wait_ge(g_shifted, 1)
                act.activation(g_exp[:], g_exp[:], ACT.Exp).then_inc(g_exp_done, 1)
                act.wait_ge(e_diff_done, 1)
                act.activation(e_diff[:], e_diff[:], ACT.Exp).then_inc(e_exp_done, 1)

            @block.vector
            def _(dve):
                def over(t, n):
                    return t.unsqueeze(2).to_broadcast([P, NT, n])

                def pick_first(values, top_of, order, one, n):
                    dve.tensor_reduce(top_of[:], values, AX.X, ALU.max)
                    dve.drain()
                    dve.tensor_tensor(one, values, over(top_of[:], n), ALU.is_equal)
                    dve.drain()
                    dve.tensor_tensor(one, one, order[:].unsqueeze(1).to_broadcast([P, NT, n]), ALU.mult)
                    dve.drain()
                    dve.tensor_reduce(pick[:], one, AX.X, ALU.max)
                    dve.drain()
                    dve.tensor_tensor(one, one, over(pick[:], n), ALU.is_equal)
                    dve.drain()

                dve.memset(w[:], 0.0).then_inc(w_done, 1)
                dve.memset(carry[:, 0], 0.0)
                dve.wait_ge(w_high_done, 1)
                dve.tensor_tensor(w_low[:], w[:], w_high[:].bitcast(F32), ALU.subtract).then_inc(w_low_done, 1)
                dve.wait_ge(lt_ready, 1)
                dve.tensor_copy(logits_t[:], logits_ps[:, 0:T]).then_inc(lt_done, 1)
                dve.wait_ge(tr_ready, 1)
                dve.wait_ge(tables, 7)
                dve.tensor_tensor(logits[:], tr_ps[:, 0:NT * NL].rearrange("p (t n) -> p t n", n=NL),
                                  bias[:].unsqueeze(1).to_broadcast([P, NT, NL]), ALU.add)
                dve.drain()
                pick_first(logits[:, :, 0:N_GROUPS], g_top, first_g, g_one[:], N_GROUPS)
                dve.tensor_tensor(g_exp[:], logits[:, :, 0:N_GROUPS], over(g_top[:], N_GROUPS),
                                  ALU.subtract).then_inc(g_shifted, 1)
                by_group = lambda t: t.rearrange("p t (g e) -> p (t g) e", g=N_GROUPS)
                sel = g_one[:].rearrange("p t g -> p (t g)").unsqueeze(2).to_broadcast([P, NT * N_GROUPS, EPG])
                for t in range(NT):
                    dve.tensor_tensor(masked[:, t].rearrange("p (g e) -> p g e", g=N_GROUPS),
                                      logits[:, t, N_GROUPS:].rearrange("p (g e) -> p g e", g=N_GROUPS),
                                      g_one[:, t].unsqueeze(2).to_broadcast([P, N_GROUPS, EPG]), ALU.mult)
                dve.drain()
                dve.tensor_scalar(g_one[:], g_one[:], -1.0, 1e30, ALU.add, ALU.mult)
                dve.drain()
                dve.tensor_tensor(by_group(masked[:]), by_group(masked[:]), sel, ALU.add)
                dve.drain()
                pick_first(masked[:], e_top1, first_e, chosen[:, 0], N_EXP)
                dve.scalar_tensor_tensor(masked[:], chosen[:, 0], -3e30, masked[:], ALU.mult, ALU.add)
                dve.drain()
                pick_first(masked[:], e_top2, first_e, chosen[:, 1], N_EXP)
                dve.tensor_tensor(e_diff[:], e_top2[:], e_top1[:], ALU.subtract).then_inc(e_diff_done, 1)
                dve.tensor_tensor(both[:], chosen[:, 0], chosen[:, 1], ALU.add).then_inc(both_done, 1)
                dve.wait_ge(g_exp_done, 1)
                dve.tensor_reduce(g_sum[:], g_exp[:], AX.X, ALU.add)
                dve.wait_ge(e_exp_done, 1)
                dve.tensor_scalar(e_sum[:], e_diff[:], 1.0, None, ALU.add)
                dve.drain()
                dve.tensor_tensor(e_sum[:], e_sum[:], g_sum[:], ALU.mult)
                dve.drain()
                dve.reciprocal(weight[:, 0], e_sum[:])
                dve.drain()
                dve.tensor_tensor(weight[:, 1], weight[:, 0], e_diff[:], ALU.mult)
                dve.wait_ge(rank_ready, 1)
                for t in range(NT):
                    dve.drain()
                    dve.tensor_tensor(carry[:, t + 1], carry[:, t], sum_ps[:, t * N_EXP:(t + 1) * N_EXP], ALU.add)
                dve.drain()
                dve.tensor_scalar(blocks[:], carry[:, NT], float(P - 1), None, ALU.add)
                dve.drain()
                dve.tensor_copy(blocks_i[:], blocks[:])
                dve.drain()
                dve.tensor_scalar(blocks_i[:], blocks_i[:], P.bit_length() - 1, None, ALU.arith_shift_right)
                dve.drain()
                dve.tensor_copy(blocks[:], blocks_i[:])
                dve.drain()
                dve.tensor_tensor_scan(block_end[:], blocks[:], blocks[:], 0.0, ALU.add, ALU.bypass)
                dve.drain()
                dve.tensor_tensor(start[:], block_end[:], blocks[:], ALU.subtract)
                dve.drain()
                dve.tensor_scalar(start[:], start[:], float(P), None, ALU.mult)
                dve.tensor_tensor(place[:], rank_ps[:, 0:NT * N_EXP].rearrange("p (t e) -> p t e", e=N_EXP),
                                  carry[:, 0:NT], ALU.add)
                dve.drain()
                dve.tensor_tensor(place[:], place[:], start[:].unsqueeze(1).to_broadcast([P, NT, N_EXP]), ALU.add)
                dve.drain()
                for c in range(2):
                    dve.tensor_tensor(chosen[:, c], chosen[:, c], place[:], ALU.mult)
                dve.drain()
                for c in range(2):
                    dve.tensor_reduce(dest[:, c], chosen[:, c], AX.X, ALU.add)
                dve.drain()
                dve.tensor_copy(dest_i[:], dest[:]).then_inc(dest_done, 1)
                dve.tensor_tensor(past[:], block_end[:].unsqueeze(1).to_broadcast([P, NB, N_EXP]),
                                  block_no[:].unsqueeze(2).to_broadcast([P, NB, N_EXP]), ALU.is_le)
                dve.drain()
                dve.tensor_reduce(expert[:], past[:], AX.X, ALU.add)
                dve.drain()
                dve.tensor_scalar(expert[:], expert[:], float(N_EXP - 1), None, ALU.min)
                dve.tensor_scalar(blocks[:, 0:1], block_end[:, N_EXP - 1:N_EXP], -1.0, None, ALU.add)
                dve.drain()
                dve.tensor_copy(expert_i[:], expert[:])
                dve.tensor_copy(last_pair[:], blocks[:, 0:1])
                dve.drain()
                dve.tensor_scalar(last_pair[:], last_pair[:], 1, None, ALU.arith_shift_right)
                dve.wait_ge(table_in, 16)
                dve.tensor_copy(table[:], table_i[:].rearrange("b p a -> b a p")).then_inc(table_done, 1)
                dve.wait_ge(table_ready, 1)
                dve.tensor_copy(slot_i[:], tr_ps[:, 0:2 * NB].rearrange("p (a b) -> p a b", a=2))

            @block.tensor
            def _(pe):
                pe.wait_ge(w_low_done, 1)
                for at, size in TOKEN_GROUPS:
                    for k in range(KC):
                        last = product3(pe, logits_ps[:, at:at + size], (w_high[:, k], w_low[:, k]),
                                        (h_high[:, k, at:at + size], h_low[:, k, at:at + size]), k == 0, k == KC - 1)
                last.then_inc(lt_ready, 1)
                pe.wait_ge(lt_done, 1)
                for t in range(NT):
                    last = pe.transpose(tr_ps[:, t * NL:(t + 1) * NL], logits_t[0:NL, t * P:(t + 1) * P],
                                        ident[0:NL, 0:NL])
                last.then_inc(tr_ready, 1)
                pe.wait_ge(both_done, 1)
                pe.wait_ge(tables, 7)
                rows = both[:].rearrange("p t e -> p (t e)")
                pe.matmul(rank_ps[:, 0:NT * N_EXP], before[:], rows, start=True, stop=True)
                pe.matmul(sum_ps[:, 0:NT * N_EXP], ones[:], rows, start=True, stop=True).then_inc(rank_ready, 1)
                pe.wait_ge(table_done, 1)
                for a in range(2):
                    last = pe.transpose(tr_ps[:, a * NB:(a + 1) * NB], table[:, a], ident[0:NB, 0:NB])
                last.then_inc(table_ready, 1)


def experts(nc, tag, h_rows, slot_i, w_gate, w_up, w_down, g_ffn, expert_i, last_pair, ident, y_out):
    with Mem(nc, tag) as m:
        wg = m.sb("wg", [P, 2, KC, D_EXP])
        wu = m.sb("wu", [P, 2, KC, D_EXP])
        wd = m.sb("wd", [P, 2, FC, D])
        token = [m.sb(f"token{u}", [P, 1], I32) for u in range(2)]
        result = [m.sb(f"result{u}", [P, 1], I32) for u in range(2)]
        rows = m.sb("rows", [P, 2, D])
        x_t = m.sb("x_t", [P, 2, KC, P])
        g = m.sb("g", [P, KC])
        sig = m.sb("sig", [P, D_EXP])
        hidden = m.sb("hidden", [P, 2, D_EXP])
        hidden_t = m.sb("hidden_t", [P, FC, P])
        y = m.sb("y", [P, 2, D])
        tr_ps = m.ps("tr_ps", [P, D])
        gate_ps = m.ps("gate_ps", [P, 2, D_EXP])
        up_ps = m.ps("up_ps", [P, 2, D_EXP])
        y_ps = m.ps("y_ps", [P, D])
        g_in = m.sem("g_in")
        row_in, wg_in, wu_in, wd_in, stored = (
            [m.sem(f"{s}{u}") for u in range(2)] for s in ("row_in", "wg_in", "wu_in", "wd_in", "stored"))
        token_done, result_done = m.sem("token_done"), m.sem("result_done")
        (xt_ready, xt_done, gate_ready, up_ready, sig_done, hidden_done, ht_ready, ht_done, y_ready, y_done) = (
            m.sem(s) for s in ("xt_ready", "xt_done", "gate_ready", "up_ready", "sig_done", "hidden_done",
                               "ht_ready", "ht_done", "y_ready", "y_done"))

        def last_of(eng):
            return eng.value_load(last_pair[0:1, 0:1], min_val=2 * T // P // 2 - 1, max_val=MAX_BLOCKS // 2 - 1)

        def skewed(eng, front, back):
            last = last_of(eng)
            front(0, 0)
            with eng.Fori(0, last) as i:
                for u in range(2):
                    front(i + u, 1 - u)
                    back(i, u)
            front(last, 1)
            for u in range(2):
                back(last, u)
            return last

        with nc.Block() as block:
            @block.sync
            def _(sp):
                last = last_of(sp)
                with nc.allow_non_contiguous_dma(reason="a gain column of 1024 numbers"):
                    sp.dma_start(g[:], g_ffn.rearrange("(k p) -> p k", p=P)).then_inc(g_in, 16)
                with sp.Fori(0, last + 1) as i:
                    for u in range(2):
                        n = 2 * i + u
                        e = sp.value_load(expert_i[0:1, ds(n, 1)], min_val=0, max_val=N_EXP - 1)
                        sp.wait_ge(up_ready, free(n))
                        sp.dma_start(wg[:, u], w_gate[ds(e * D, D), :]
                                     .rearrange("(k p) n -> p k n", p=P)).then_inc(wg_in[u], 16)
                        sp.dma_start(wu[:, u], w_up[ds(e * D, D), :]
                                     .rearrange("(k p) n -> p k n", p=P)).then_inc(wu_in[u], 16)
                        sp.wait_ge(y_ready, free(n))
                        sp.dma_start(wd[:, u], w_down[ds(e * D_EXP, D_EXP), :]
                                     .rearrange("(k p) n -> p k n", p=P)).then_inc(wd_in[u], 16)

            @block.gpsimd
            def _(pool):
                def gather(i, u):
                    n = 2 * i + u
                    pool.wait_ge(xt_ready, free(n))
                    wait_apart(pool)
                    pool.tensor_copy(token[u][:], slot_i[:, 0, ds(n, 1)]).then_inc(token_done, 1)
                    pool.wait_ge(token_done, n + 1)
                    wait_apart(pool)
                    pool.indirect_dma_start(out=rows[:, u], out_offset=None, in_=h_rows,
                                            in_offset=bass.IndirectOffsetOnAxis(ap=token[u][:], axis=0)
                                            ).then_inc(row_in[u], 16)

                def scatter(i, u):
                    n = 2 * i + u
                    pool.wait_ge(y_done, ready(n))
                    wait_apart(pool)
                    pool.tensor_copy(result[u][:], slot_i[:, 1, ds(n, 1)]).then_inc(result_done, 1)
                    pool.wait_ge(result_done, n + 1)
                    wait_apart(pool)
                    pool.indirect_dma_start(out=y_out, in_=y[:, u], in_offset=None,
                                            out_offset=bass.IndirectOffsetOnAxis(ap=result[u][:], axis=0),
                                            bounds_check=2 * T - 1, oob_is_err=False).then_inc(stored[u], 16)

                last = last_of(pool)
                for u in range(2):
                    gather(0, u)
                with pool.Fori(0, last) as i:
                    for u in range(2):
                        gather(i + 1, u)
                        scatter(i, u)
                for u in range(2):
                    scatter(last, u)
                for u in range(2):
                    pool.wait_ge(stored[u], last * 16 + 16)

            @block.scalar
            def _(act):
                act.preload_act_table_set(ACT_SET)
                act.sem_inc(y_done, PRIME)
                act.sem_inc(ht_done, PRIME)

                def front(i, u):
                    n = 2 * i + u
                    act.wait_ge(gate_ready, ready(n))
                    act.activation(sig[:], gate_ps[:, u], ACT.Exp, scale=-1.0).then_inc(sig_done, 1)

                def back(i, u):
                    n = 2 * i + u
                    act.wait_ge(ht_ready, n + 1)
                    act.activation(hidden_t[:].rearrange("p k t -> p (k t)"), tr_ps[:, 0:D_EXP],
                                   ACT.Copy).then_inc(ht_done, 1)
                    act.wait_ge(y_ready, ready(n))
                    act.wait_ge(stored[u], i * 16)
                    act.activation(y[:, u], y_ps[:], ACT.Copy).then_inc(y_done, 1)

                skewed(act, front, back)

            @block.vector
            def _(dve):
                dve.sem_inc(hidden_done, PRIME)
                dve.wait_ge(g_in, 16)

                def front(i, u):
                    n = 2 * i + u
                    dve.wait_ge(xt_ready, ready(n))
                    dve.tensor_tensor(x_t[:, u], tr_ps[:].rearrange("p (k t) -> p k t", k=KC),
                                      g[:].unsqueeze(2).to_broadcast([P, KC, P]), ALU.mult).then_inc(xt_done, 1)
                    dve.wait_ge(sig_done, n + 1)
                    dve.tensor_scalar(hidden[:, u], sig[:], 1.0, None, ALU.add)
                    dve.drain()
                    dve.reciprocal(hidden[:, u], hidden[:, u])
                    dve.drain()
                    dve.tensor_tensor(hidden[:, u], gate_ps[:, u], hidden[:, u], ALU.mult)
                    dve.drain()
                    dve.wait_ge(up_ready, ready(n))
                    dve.tensor_tensor(hidden[:, u], up_ps[:, u], hidden[:, u], ALU.mult).then_inc(hidden_done, 1)

                def back(i, u):
                    pass

                skewed(dve, front, back)

            @block.tensor
            def _(pe):
                for s in (xt_ready, gate_ready, up_ready, y_ready):
                    pe.sem_inc(s, PRIME)

                def front(i, u):
                    n = 2 * i + u
                    pe.wait_ge(row_in[u], i * 16 + 16)
                    pe.wait_ge(ht_done, free(n))
                    for k in range(KC):
                        last = pe.transpose(tr_ps[:, k * P:(k + 1) * P], rows[:, u, k * P:(k + 1) * P], ident[:])
                    last.then_inc(xt_ready, 1)
                    pe.wait_ge(xt_done, n + 1)
                    pe.wait_ge(hidden_done, free(n))
                    for loaded, w, out, done in ((wg_in, wg, gate_ps, gate_ready), (wu_in, wu, up_ps, up_ready)):
                        pe.wait_ge(loaded[u], i * 16 + 16)
                        for k in range(KC):
                            last = pe.matmul(out[:, u], x_t[:, u, k], w[:, u, k], start=(k == 0), stop=(k == KC - 1))
                        last.then_inc(done, 1)

                def back(i, u):
                    n = 2 * i + u
                    pe.wait_ge(hidden_done, ready(n))
                    for k in range(FC):
                        last = pe.transpose(tr_ps[:, k * P:(k + 1) * P], hidden[:, u, k * P:(k + 1) * P], ident[:])
                    last.then_inc(ht_ready, 1)
                    pe.wait_ge(ht_done, ready(n))
                    pe.wait_ge(y_done, n + PRIME)
                    pe.wait_ge(wd_in[u], i * 16 + 16)
                    for half in (slice(0, 512), slice(512, D)):
                        for k in range(FC):
                            last = pe.matmul(y_ps[:, half], hidden_t[:, k], wd[:, u, k, half],
                                             start=(k == 0), stop=(k == FC - 1))
                    last.then_inc(y_ready, 1)

                skewed(pe, front, back)


def combine(nc, tag, x2_rows, y_rows, weight, g_final, eps, outputs):
    with Mem(nc, tag) as m:
        x = m.sb("x", [P, 2, D])
        y = m.sb("y", [P, 2, 2, D])
        gain = m.sb("gain", [P, D])
        junk = m.sb("junk", [P, D])
        ss, rstd = m.sb("ss", [P, 1]), m.sb("rstd", [P, 1])
        out = m.sb("out", [P, 2, D])
        gain_in = m.sem("gain_in")
        x_in, stored = ([m.sem(f"{s}{u}") for u in range(2)] for s in ("x_in", "stored"))
        sum_done, rstd_done, out_done = m.sem("sum_done"), m.sem("rstd_done"), m.sem("out_done")
        with nc.Block() as block:
            @block.sync
            def _(sp):
                with nc.allow_non_contiguous_dma(reason="one row for all partitions"):
                    sp.dma_start(gain[:], g_final.rearrange("(a n) -> a n", a=1).to_broadcast([P, D])).then_inc(gain_in, 16)
                with sp.Fori(0, NT // 2) as i:
                    for u in range(2):
                        sp.wait_ge(out_done, free(2 * i + u))
                        t = i * (2 * P) + u * P
                        sp.dma_start(x[:, u], x2_rows[ds(t, P), :]).then_inc(x_in[u], 16)
                        for c in range(2):
                            sp.dma_start(y[:, u, c], y_rows[ds(t + c * T, P), :]).then_inc(x_in[u], 16)

            @block.vector
            def _(dve):
                dve.sem_inc(out_done, PRIME)
                dve.wait_ge(gain_in, 16)
                with dve.Fori(0, NT // 2) as i:
                    for u in range(2):
                        n = 2 * i + u
                        dve.wait_ge(x_in[u], i * 48 + 48)
                        dve.scalar_tensor_tensor(x[:, u], y[:, u, 0], weight[:, 0, ds(n, 1)], x[:, u],
                                                 ALU.mult, ALU.add)
                        dve.drain()
                        dve.scalar_tensor_tensor(x[:, u], y[:, u, 1], weight[:, 1, ds(n, 1)], x[:, u],
                                                 ALU.mult, ALU.add).then_inc(sum_done, 1)
                        dve.wait_ge(rstd_done, n + 1)
                        dve.wait_ge(stored[u], i * 16)
                        dve.scalar_tensor_tensor(out[:, u], x[:, u], rstd[:], gain[:], ALU.mult,
                                                 ALU.mult).then_inc(out_done, 1)

            @block.scalar
            def _(act):
                act.preload_act_table_set(ACT_SET)

                def body(i, rows, j):
                    for u in range(2):
                        n = 2 * i + u
                        act.wait_ge(sum_done, n + 1)
                        act.activation(junk[:], x[:, u], ACT.Square, accum_out=ss[:])
                        act.drain()
                        act.activation(rstd[:], ss[:], ACT.Ln, scale=1.0 / D, bias=eps[:, 0:1])
                        act.drain()
                        act.activation(rstd[:], rstd[:], ACT.Exp, scale=-0.5).then_inc(rstd_done, 1)
                        act.wait_ge(out_done, ready(n))
                        act.dma_start(rows[ds(j * (2 * P) + u * P, P), :], out[:, u]).then_inc(stored[u], 16)

                tile_pairs(act, body, outputs)
                for u in range(2):
                    act.wait_ge(stored[u], 16 * (NT // 2))


def encoder(nc, x_prompt, x_sample, mem_prompt, mem_sample, g_mix, w_in, hg_lb, g_hg, lam_q1, lam_k1, lam_q2,
            lam_k2, g_da, w_out, g_ca, g_mem, w_cq, w_ckv, w_co, g_ffn, w_rg, b_rg, w_re, b_re, w_gate, w_up,
            w_down, g_final, y_prompt, y_sample):
    def scratch(name, shape, dt=F32):
        return nc.dram_tensor(name, shape, dt, kind="Internal").ap()

    proj_t = scratch("proj_t", [w_in.shape[2], T])
    o_fwd, o_bwd = scratch("o_fwd", [T, HW]), scratch("o_bwd", [T, HW])
    mix = scratch("mix", [T, 2 * HW])
    x1, x2, h3 = scratch("x1", [T, D]), scratch("x2", [T, D]), scratch("h3", [T, D])
    kv_t = scratch("kv_t", [2 * D, 2 * N_MEM])
    q_t = scratch("q_t", [D, T])
    slots = scratch("slots", [MAX_BLOCKS * P, 2], I32)
    y_rows = scratch("y_rows", [2 * T, D])
    x_rows = [(x_prompt[0], NT_P), (x_sample[0], NT - NT_P)]

    with Mem(nc, "kept") as kept:
        ident, eps = kept.sb("ident", [P, P]), kept.sb("eps", [P, 1])
        lb, one_minus_lb = kept.sb("lb", [P, HEADS]), kept.sb("one_minus_lb", [P, HEADS])
        lam = kept.sb("lam", [P, 1])
        constants(nc, ident, eps)
        lower_bound(nc, hg_lb, lb, one_minus_lb)
        lambda_of(nc, lam_q1[0], lam_k1[0], lam_q2[0], lam_k2[0], lam)

        with Mem(nc, "mem") as m:
            high, low = m.sb("high", [P, KC, 2 * N_MEM], F32R), m.sb("low", [P, KC, 2 * N_MEM], F32R)
            normed_transposed(nc, "norm_mem", [(mem_prompt[0], N_MEM // P), (mem_sample[0], N_MEM // P)], g_mem[0],
                              ident, eps, high, low)
            project(nc, "proj_kv", w_ckv[0], 2 * D, high, low, [(0, 2 * N_MEM)], kv_t)
        with Mem(nc, "in") as m:
            high, low = m.sb("high", [P, KC, T], F32R), m.sb("low", [P, KC, T], F32R)
            normed_transposed(nc, "norm_mix", x_rows, g_mix[0], ident, eps, high, low)
            project(nc, "proj_in", w_in[0], w_in.shape[2], high, low, TOKEN_GROUPS, proj_t)

        hgrn(nc, "hgrn", proj_t, lb, one_minus_lb, ident, o_fwd, o_bwd)
        diff_attention(nc, "da_prompt", proj_t, 0, SEQ_P, g_da[0], lam, ident, eps, mix)
        diff_attention(nc, "da_sample", proj_t, SEQ_P, SEQ_S, g_da[0], lam, ident, eps, mix)

        with Mem(nc, "out") as m:
            w_high, w_low = m.sb("w_high", [P, KC, D], F32R), m.sb("w_low", [P, KC, D], F32R)
            split_weight(nc, "split_out", w_out[0], w_high, w_low)
            mix_out(nc, "mix_out", o_fwd, o_bwd, proj_t, mix, x_rows, g_hg[0], w_high, w_low, ident, eps, x1)
        with Mem(nc, "cq") as m:
            high, low = m.sb("high", [P, KC, T], F32R), m.sb("low", [P, KC, T], F32R)
            normed_transposed(nc, "norm_ca", [(x1, NT)], g_ca[0], ident, eps, high, low)
            project(nc, "proj_q", w_cq[0], D, high, low, TOKEN_GROUPS, q_t)
        with Mem(nc, "co") as m:
            w_high, w_low = m.sb("w_high", [P, KC, D], F32R), m.sb("w_low", [P, KC, D], F32R)
            split_weight(nc, "split_co", w_co[0], w_high, w_low)
            cross_attention(nc, "cross", q_t, kv_t, x1, w_high, w_low, ident, x2)

        slot_i, weight = kept.sb("slot_i", [P, 2, MAX_BLOCKS], I32), kept.sb("weight", [P, 2, NT])
        expert_i, last_pair = kept.sb("expert_i", [P, MAX_BLOCKS], I32), kept.sb("last_pair", [P, 1], I32)
        with Mem(nc, "moe") as m:
            high, low = m.sb("high", [P, KC, T], F32R), m.sb("low", [P, KC, T], F32R)
            normed_transposed(nc, "norm_ffn", [(x2, NT)], g_ffn[0], ident, eps, high, low, rows_out=h3)
            router(nc, "router", high, low, w_rg[0], b_rg[0], w_re[0], b_re[0], ident, slots, slot_i, weight,
                   expert_i, last_pair)
        experts(nc, "experts", h3, slot_i, w_gate[0].rearrange("e k n -> (e k) n"),
                w_up[0].rearrange("e k n -> (e k) n"), w_down[0].rearrange("e k n -> (e k) n"), g_ffn[0],
                expert_i, last_pair, ident, y_rows)
        combine(nc, "combine", x2, y_rows, weight, g_final, eps,
                [(y_prompt[0], NT_P), (y_sample[0], NT - NT_P)])


_INS = ["x_prompt", "x_sample", "mem_prompt", "mem_sample", "g_mix", "w_in", "hg_lb", "g_hg", "lam_q1", "lam_k1",
        "lam_q2", "lam_k2", "g_da", "w_out", "g_ca", "g_mem", "w_cq", "w_ckv", "w_co", "g_ffn", "w_rg", "b_rg",
        "w_re", "b_re", "w_gate", "w_up", "w_down", "g_final"]
_OUTS = [((1, SEQ_P, D), "float32"), ((1, SEQ_S, D), "float32")]


def kernel(**inputs):
    import numpy as _np
    import concourse.bacc as _bacc
    from concourse import mybir as _mybir
    from concourse.bass_utils import run_bass_kernel_spmd as _run

    nc = _bacc.Bacc("TRN2", target_bir_lowering=False, num_devices=1)
    arrays, args = {}, []
    for name in _INS:
        a = _np.ascontiguousarray(inputs[name])
        arrays[f"in_{name}_dram"] = a
        args.append(nc.dram_tensor(f"in_{name}_dram", a.shape, _mybir.dt.from_np(a.dtype), kind="ExternalInput").ap())
    for i, (shape, dtype) in enumerate(_OUTS):
        dt = _mybir.dt.from_np(_np.dtype(dtype))
        args.append(nc.dram_tensor(f"out_{i}_dram", shape, dt, kind="ExternalOutput").ap())
    encoder(nc, *args)
    r = _run(nc, [arrays], core_ids=[0])
    got = tuple(r.results[0][f"out_{i}_dram"] for i in range(len(_OUTS)))
    return got
```

```python
import math
from contextlib import ExitStack

import concourse.bass as bass
from concourse import mybir

F32 = mybir.dt.float32
F32R = mybir.dt.float32r
I32 = mybir.dt.int32
U32 = mybir.dt.uint32
ALU = mybir.AluOpType
ACT = mybir.ActivationFunctionType
AX = mybir.AxisListType
ds = bass.ds

P = 128
D = 1024
KC = D // P
SEQ_P, SEQ_S, N_MEM = 1024, 256, 256
T = SEQ_P + SEQ_S
NT = T // P
NT_P = SEQ_P // P
EPS = 1e-6
HEADS = 4
HW = HEADS * P
DK = 64
DA_SCALE = DK ** -0.5
CA_DH = D // HEADS
CA_SCALE = CA_DH ** -0.5
N_GROUPS, EPG = 4, 8
N_EXP = N_GROUPS * EPG
D_EXP = 512
FC = D_EXP // P
MAX_BLOCKS = 2 * T // P + N_EXP
LAM_INIT = 0.8 - 0.6 * math.exp(-0.3 * 0)
ROW_Q, ROW_FF, ROW_FB, ROW_V, ROW_G, ROW_DQ, ROW_DK, ROW_DV = (HW * n for n in range(8))
TOKEN_GROUPS = [(0, 512), (512, 512), (1024, 256)]
PRIME = 2
ACT_SET = "natural_log_exp_and_others"


def free(n):
    return n + 1


def ready(n):
    return n + 1 + PRIME


def wait_apart(eng):
    eng.nop(nofuse=True)


class Mem:

    def __init__(self, nc, tag):
        self.nc, self.tag, self.stack, self.sems = nc, tag, ExitStack(), []

    def __enter__(self):
        return self

    def __exit__(self, *a):
        if self.sems and a[0] is None:
            self.nc.clear_and_free_semaphores(self.sems)
            self.nc.all_engine_barrier()
        return self.stack.__exit__(*a)

    def sb(self, name, shape, dt=F32):
        return self.stack.enter_context(self.nc.sbuf_tensor(f"{self.tag}_{name}", shape, dt))

    def ps(self, name, shape, dt=F32):
        return self.stack.enter_context(self.nc.psum_tensor(f"{self.tag}_{name}", shape, dt))

    def sem(self, name):
        self.sems.append(self.nc.alloc_semaphore(f"{self.tag}_{name}"))
        return self.sems[-1]


def product3(pe, out, lhs, rhs, first, last):
    pe.matmul(out, lhs[0], rhs[0], start=first, stop=False)
    pe.matmul(out, lhs[0], rhs[1], start=False, stop=False)
    return pe.matmul(out, lhs[1], rhs[0], start=False, stop=last)


def skewed_pairs(eng, pairs, *parts, apart=(), looped=None, worked_in=(0, None)):
    lead_max = max(lead for lead, _ in parts)
    in_range = pairs - (lead_max + 1) // 2
    looped = in_range if looped is None else min(looped, in_range)

    def pair(i, us=(0, 1), pairs_left=pairs):
        for u in us:
            for lead, part in parts:
                if 0 <= u + lead < 2 * pairs_left:
                    part(i + (u + lead) // 2, (u + lead) % 2)

    for n in range(-lead_max, 0):
        if n == worked_in[0]:
            worked_in[1]()
        pair(0, (n,))
    at = 0
    for stop in apart + (looped,):
        if at < stop:
            with eng.Fori(at, stop) as i:
                pair(i)
        if stop < looped:
            pair(stop)
        at = stop + 1
    for i in range(looped, pairs):
        pair(i, pairs_left=pairs - i)


def rows_of(sources, i, u):
    rows, tiles = sources[0]
    if isinstance(i, int) and 2 * i >= tiles:
        i -= tiles // 2
        rows = sources[1][0]
    return rows[ds(i * (2 * P) + u * P, P), :]


def constants(nc, ident, eps):
    with Mem(nc, "const") as m:
        zero_done, done = m.sem("zero_done"), m.sem("done")
        with nc.Block() as block:
            @block.gpsimd
            def _(pool):
                pool.memset(ident[:], 0.0).then_inc(zero_done, 1)
                pool.wait_ge(zero_done, 1)
                pool.affine_select(out=ident[:], in_=ident[:], compare_op=ALU.not_equal, fill=1.0, base=0,
                                   pattern=[[-1, P]], channel_multiplier=1).then_inc(done, 1)
                pool.memset(eps[:], EPS).then_inc(done, 1)
                pool.wait_ge(done, 2)


def normed_transposed(nc, tag, sources, gain, ident, eps, high, low, rows_out=None):
    with Mem(nc, tag) as m:
        x = m.sb("x", [P, 2, D])
        xn = m.sb("xn", [P, 2, D])
        junk = m.sb("junk", [P, D])
        g = m.sb("g", [P, D])
        ss, rstd = m.sb("ss", [P, 2]), m.sb("rstd", [P, 2])
        xT = m.ps("xT", [P, 2, D])
        g_in = m.sem("g_in")
        x_in = [m.sem(f"x_in{u}") for u in range(2)]
        stored = [m.sem(f"stored{u}") for u in range(2)]
        rstd_done, xn_done, tr_done, high_done, low_done = (
            m.sem(s) for s in ("rstd_done", "xn_done", "tr_done", "high_done", "low_done"))
        pairs = sum(n for _, n in sources) // 2
        by_k = lambda t: t.rearrange("p (k t) -> p k t", k=KC)
        with nc.Block() as block:
            @block.sync
            def _(sp):
                def load(i, u):
                    sp.wait_ge(xn_done, free(2 * i + u))
                    sp.dma_start(x[:, u, :], rows_of(sources, i, u)).then_inc(x_in[u], 16)

                load(0, 0)
                with nc.allow_non_contiguous_dma(reason="one row for all partitions"):
                    sp.dma_start(g[:], gain.rearrange("(a n) -> a n", a=1).to_broadcast([P, D])).then_inc(g_in, 16)
                load(0, 1)
                skewed_pairs(sp, pairs - 1, (0, lambda i, u: load(i + 1, u)), looped=sources[0][1] // 2 - 1)

            @block.gpsimd
            def _(pool):
                if rows_out is None:
                    return
                with pool.Fori(0, pairs) as i:
                    for u in range(2):
                        pool.wait_ge(xn_done, ready(2 * i + u))
                        pool.dma_start(rows_out[ds(i * (2 * P) + u * P, P), :], xn[:, u, :]).then_inc(stored[u], 16)
                for u in range(2):
                    pool.wait_ge(stored[u], 16 * pairs)

            @block.scalar
            def _(act):
                act.preload_act_table_set(ACT_SET)

                def find_rstd(i, u):
                    n = 2 * i + u
                    act.wait_ge(x_in[u], 16 * (i + 1))
                    act.activation(junk[:], x[:, u, :], ACT.Square, accum_out=ss[:, u:u + 1])
                    act.drain()
                    act.activation(rstd[:, u:u + 1], ss[:, u:u + 1], ACT.Ln, scale=1.0 / D, bias=eps[:, 0:1])
                    act.drain()
                    act.activation(rstd[:, u:u + 1], rstd[:, u:u + 1], ACT.Exp, scale=-0.5).then_inc(rstd_done, 1)

                def high_part(i, u):
                    n = 2 * i + u
                    act.wait_ge(tr_done, ready(n))
                    act.activation(high[:, :, ds(n * P, P)], by_k(xT[:, u, :]), ACT.Copy).then_inc(high_done, 1)

                skewed_pairs(act, pairs, (0, high_part), (2, find_rstd))

            @block.vector
            def _(dve):
                dve.sem_inc(xn_done, PRIME)
                dve.sem_inc(low_done, PRIME)
                dve.wait_ge(g_in, 16)

                def scale(i, u):
                    n = 2 * i + u
                    dve.wait_ge(rstd_done, n + 1)
                    dve.wait_ge(tr_done, free(n))
                    if rows_out is not None:
                        dve.wait_ge(stored[u], 16 * i)
                    dve.scalar_tensor_tensor(xn[:, u, :], x[:, u, :], rstd[:, u:u + 1], g[:], ALU.mult,
                                             ALU.mult).then_inc(xn_done, 1)

                def low_part(i, u):
                    n = 2 * i + u
                    dve.wait_ge(high_done, n + 1)
                    wait_apart(dve)
                    dve.tensor_tensor(low[:, :, ds(n * P, P)], by_k(xT[:, u, :]),
                                      high[:, :, ds(n * P, P)].bitcast(F32), ALU.subtract).then_inc(low_done, 1)

                skewed_pairs(dve, pairs, (1, scale), (0, low_part))

            @block.tensor
            def _(pe):
                pe.sem_inc(tr_done, PRIME)
                with pe.Fori(0, pairs) as i:
                    for u in range(2):
                        n = 2 * i + u
                        pe.wait_ge(xn_done, ready(n))
                        pe.wait_ge(low_done, free(n))
                        for k in range(KC):
                            last = pe.transpose(xT[:, u, k * P:(k + 1) * P], xn[:, u, k * P:(k + 1) * P], ident[:])
                        last.then_inc(tr_done, 1)


class WeightSplit:

    def __init__(self, m, weight, high, low):
        self.weight, self.high, self.low = weight, high, low
        self.raw = m.sb("split_raw", [P, 2, D])
        self.rows_in = [m.sem(f"split_in{u}") for u in range(2)]
        self.high_done, self.low_done = m.sem("split_high_done"), m.sem("split_low_done")

    def start(self, dve):
        dve.sem_inc(self.low_done, PRIME)

    def load(self, sp, i, u):
        n = 2 * i + u
        sp.wait_ge(self.low_done, free(n))
        sp.dma_start(self.raw[:, u], self.weight[ds(n * P, P), :]).then_inc(self.rows_in[u], 16)

    def round(self, act, i, u):
        act.wait_ge(self.rows_in[u], 16 * (i + 1))
        wait_apart(act)
        act.activation(self.high[:, ds(2 * i + u, 1)], self.raw[:, u:u + 1], ACT.Copy).then_inc(self.high_done, 1)

    def subtract(self, dve, i, u):
        dve.wait_ge(self.high_done, 2 * i + u + 1)
        wait_apart(dve)
        dve.tensor_tensor(self.low[:, ds(2 * i + u, 1)], self.raw[:, u:u + 1],
                          self.high[:, ds(2 * i + u, 1)].bitcast(F32), ALU.subtract).then_inc(self.low_done, 1)


def project(nc, tag, weight, columns, high, low, groups, out_t, split=None):
    tokens = sum(n for _, n in groups)
    with Mem(nc, tag) as m:
        raw = m.sb("raw", [P, 2, KC, P])
        w_high = m.sb("w_high", [P, 2, KC, P], F32R)
        w_low = m.sb("w_low", [P, 2, KC, P], F32R)
        staged = m.sb("staged", [P, 2, tokens])
        acc = m.ps("acc", [P, 2, -(-tokens // 512) * 512])
        w_in = [m.sem(f"w_in{u}") for u in range(2)]
        stored = [m.sem(f"stored{u}") for u in range(2)]
        high_done, low_done, mm_done, staged_done = (
            m.sem(s) for s in ("high_done", "low_done", "mm_done", "staged_done"))
        pairs = columns // P // 2
        rider = WeightSplit(m, *split) if split else None
        with nc.Block() as block:
            @block.sync
            def _(sp):
                with sp.Fori(0, pairs) as i:
                    for u in range(2):
                        sp.wait_ge(low_done, free(2 * i + u))
                        sp.dma_start(raw[:, u], weight[:, ds(i * (2 * P) + u * P, P)]
                                     .rearrange("(k p) n -> p k n", p=P)).then_inc(w_in[u], 16)
                        if rider:
                            rider.load(sp, i, u)

            @block.scalar
            def _(act):
                act.preload_act_table_set(ACT_SET)
                act.sem_inc(high_done, PRIME)
                act.sem_inc(staged_done, PRIME)

                def round_weight(i, u):
                    act.wait_ge(w_in[u], 16 * (i + 1))
                    act.wait_ge(mm_done, free(2 * i + u))
                    act.activation(w_high[:, u], raw[:, u], ACT.Copy).then_inc(high_done, 1)

                def stage(i, u):
                    act.wait_ge(mm_done, ready(2 * i + u))
                    act.wait_ge(stored[u], 16 * i)
                    act.activation(staged[:, u], acc[:, u, 0:tokens], ACT.Copy).then_inc(staged_done, 1)

                for u in range(2):
                    round_weight(0, u)
                with act.Fori(0, pairs - 1) as i:
                    for u in range(2):
                        stage(i, u)
                        round_weight(i + 1, u)
                        if rider:
                            rider.round(act, i, u)
                for u in range(2):
                    if rider:
                        rider.round(act, pairs - 1, u)
                    stage(pairs - 1, u)

            @block.vector
            def _(dve):
                dve.sem_inc(low_done, PRIME)
                if rider:
                    rider.start(dve)

                def low_part(i, u):
                    n = 2 * i + u
                    dve.wait_ge(high_done, ready(n))
                    dve.wait_ge(mm_done, free(n))
                    dve.tensor_tensor(w_low[:, u], raw[:, u], w_high[:, u].bitcast(F32),
                                      ALU.subtract).then_inc(low_done, 1)

                for u in range(2):
                    low_part(0, u)
                with dve.Fori(0, pairs - 1) as i:
                    for u in range(2):
                        low_part(i + 1, u)
                        if rider:
                            rider.subtract(dve, i, u)
                if rider:
                    for u in range(2):
                        rider.subtract(dve, pairs - 1, u)

            @block.tensor
            def _(pe):
                pe.sem_inc(mm_done, PRIME)
                with pe.Fori(0, pairs) as i:
                    for u in range(2):
                        n = 2 * i + u
                        pe.wait_ge(low_done, ready(n))
                        pe.wait_ge(staged_done, free(n))
                        for at, size in groups:
                            for k in range(KC):
                                last = product3(pe, acc[:, u, at:at + size], (w_high[:, u, k], w_low[:, u, k]),
                                                (high[:, k, at:at + size], low[:, k, at:at + size]),
                                                k == 0, k == KC - 1)
                        last.then_inc(mm_done, 1)

            @block.gpsimd
            def _(pool):
                with pool.Fori(0, pairs) as i:
                    for u in range(2):
                        pool.wait_ge(staged_done, ready(2 * i + u))
                        pool.dma_start(out_t[ds(i * (2 * P) + u * P, P), :], staged[:, u]).then_inc(stored[u], 16)
                for u in range(2):
                    pool.wait_ge(stored[u], 16 * pairs)


def lower_bound(nc, hg_lb, lb, one_minus_lb):
    with Mem(nc, "lb") as m:
        rows = m.sb("rows", [P, 2, HEADS])
        top = m.sb("top", [P, HEADS])
        e = m.sb("e", [P, 2, HEADS])
        total = m.sb("total", [P, HEADS])
        rows_in, shifted, exp_done = (m.sem(s) for s in ("rows_in", "shifted", "exp_done"))
        with nc.Block() as block:
            @block.sync
            def _(sp):
                with nc.allow_non_contiguous_dma(reason="a few columns of 128 numbers"):
                    for r in range(2):
                        sp.dma_start(rows[:, r], hg_lb[r].rearrange("(h p) -> p h", p=P)).then_inc(rows_in, 16)

            @block.vector
            def _(dve):
                dve.wait_ge(rows_in, 32)
                dve.tensor_tensor(top[:], rows[:, 0], rows[:, 1], ALU.max)
                dve.drain()
                dve.tensor_tensor(rows[:], rows[:], top[:].unsqueeze(1).to_broadcast([P, 2, HEADS]),
                                  ALU.subtract).then_inc(shifted, 1)
                dve.wait_ge(exp_done, 1)
                dve.tensor_tensor(total[:], e[:, 0], e[:, 1], ALU.add)
                dve.drain()
                dve.reciprocal(total[:], total[:])
                dve.drain()
                dve.tensor_tensor(lb[:], e[:, 0], total[:], ALU.mult)
                dve.drain()
                dve.tensor_scalar(one_minus_lb[:], lb[:], -1.0, 1.0, ALU.mult, ALU.add)

            @block.scalar
            def _(act):
                act.preload_act_table_set(ACT_SET)
                act.wait_ge(shifted, 1)
                act.activation(e[:], rows[:], ACT.Exp).then_inc(exp_done, 1)


LEVELS = (64, 32, 16)
CENTRE = LEVELS[-1] // 2 - 1


def hgrn(nc, tag, proj_t, lb, one_minus_lb, ident, o_fwd, o_bwd, weight, high, low, out_t):
    n_lev = len(LEVELS)
    base = LEVELS[-1]
    early, late = (0, 1), (1, 0)
    last_t = (P - 1, 0)
    anew_after = (NT_P - 1, NT - NT_P - 1)
    outputs = (o_fwd, o_bwd)
    tokens = high.shape[2]
    w_pairs = weight.shape[1] // P // 2
    with Mem(nc, tag) as m:
        x = m.sb("x", [P, 2, 2, HEADS, P])
        v_t = m.sb("v_t", [P, 2, HEADS, P])
        sig = m.sb("sig", [P, 2, 2 * HW])
        q = m.sb("q", [P, 2, HW])
        k = m.sb("k", [P, 2, HW])
        f = m.sb("f", [P, 2, HW])
        lf = m.sb("lf", [P, 2, HEADS, P])
        b = m.sb("b", [P, 2, HEADS, P])
        diff = m.sb("diff", [P, 2, n_lev + 2, HW])
        decay = diff
        uncentre = m.sb("uncentre", [P, 2, HW])
        from_start = m.sb("from_start", [P, 2, HW])
        whole = m.sb("whole", [P, 2, HEADS])
        q_dec = m.sb("q_dec", [P, 2, n_lev + 2, HW])
        k_dec = m.sb("k_dec", [P, 2, n_lev + 2, HW])
        v = m.sb("v", [P, 2, HW])
        k_tok = m.sb("k_tok", [P, HW])
        s_t = m.sb("s_t", [P, HW])
        state = m.sb("state", [P, 2, HW])
        o = m.sb("o", [P, 2, HW])
        one = m.sb("one", [P, 1])
        raw = m.sb("raw", [P, 2, KC, P])
        w_high, w_low = m.sb("w_high", [P, 2, KC, P], F32R), m.sb("w_low", [P, 2, KC, P], F32R)
        staged = m.sb("staged", [P, 2, tokens])
        where = m.sb("where", [P, 2, HW])
        where_i = m.sb("where_i", [P, 2, HW], I32)
        v_ps, kt_ps, o_ps, st_ps = (m.ps(s, [P, HW]) for s in ("v_ps", "kt_ps", "o_ps", "st_ps"))
        s_ps = m.ps("s_ps", [P, 2, HW])
        acc = m.ps("acc", [P, 2, 512])
        w_in, w_stored = ([m.sem(f"{s}{u}") for u in range(2)] for s in ("w_in", "w_stored"))
        w_high_done, w_low_done, acc_ready, staged_done = (
            m.sem(s) for s in ("w_high_done", "w_low_done", "acc_ready", "staged_done"))
        x_in = [m.sem(f"x_in{u}") for u in range(2)]
        v_in = [m.sem(f"v_in{u}") for u in range(2)]
        o_stored = [m.sem(f"o_stored{u}") for u in range(2)]
        (ones_done, where_done, where_i_done, clamp_done, sig_done, f_done, lf_done, diff_done, decay_done,
         base_done, levels_done, v_ready, v_done, scores_ready, s_done, kt_done, o_ready, o_done, state_done) = (
            m.sem(s) for s in (
                "ones_done", "where_done", "where_i_done", "clamp_done", "sig_done", "f_done", "lf_done",
                "diff_done", "decay_done", "base_done", "levels_done", "v_ready", "v_done", "scores_ready",
                "s_done", "kt_done", "o_ready", "o_done", "state_done"))

        def memory(part):
            def step(i, u):
                if not (isinstance(i, int) and i >= w_pairs):
                    part(i, u)
            return step

        def token(i, u):
            return i * P if u == 0 else i * -P + (NT - 1) * P

        with nc.Block() as block:
            @block.sync
            def _(sp):
                def load_gates(i, u):
                    sp.wait_ge(f_done, free(2 * i + u))
                    for j, row in enumerate((ROW_Q, (ROW_FF, ROW_FB)[u])):
                        sp.dma_start(x[:, u, j], proj_t[row:row + HW, ds(token(i, u), P)]
                                     .rearrange("(h p) t -> p h t", p=P)).then_inc(x_in[u], 16)

                def load_v(i, u):
                    sp.wait_ge(v_ready, free(2 * i + u))
                    sp.dma_start(v_t[:, u], proj_t[ROW_V:ROW_V + HW, ds(token(i, u), P)]
                                 .rearrange("(h p) t -> p h t", p=P)).then_inc(v_in[u], 16)

                def store(i, u):
                    sp.wait_ge(o_done, 2 * i + u + 1)
                    sp.dma_start(outputs[u][ds(token(i, u), P), :], o[:, u]).then_inc(o_stored[u], 16)

                def load_weight(i, u):
                    sp.wait_ge(w_low_done, free(2 * i + u))
                    sp.dma_start(raw[:, u], weight[:, ds(i * (2 * P) + u * P, P)]
                                 .rearrange("(k p) n -> p k n", p=P)).then_inc(w_in[u], 16)

                skewed_pairs(sp, NT, (2, load_v), (5, load_gates), (0, store), (4, memory(load_weight)),
                             looped=w_pairs - 2)
                for u in range(2):
                    sp.wait_ge(o_stored[u], 16 * NT)

            @block.gpsimd
            def _(pool):
                pool.sem_inc(levels_done, PRIME)
                pool.memset(where[:], 1.0).then_inc(ones_done, 1)
                pool.memset(q_dec[:, :, 0:n_lev], 0.0).then_inc(ones_done, 1)
                pool.memset(k_dec[:, :, 0:n_lev], 0.0).then_inc(ones_done, 1)
                pool.wait_ge(ones_done, 3)
                count = 0
                for u in range(2):
                    view = where[:, u].rearrange("p (h m l) -> p h m l", h=HEADS, l=base)
                    sides = [(0, 1, [[0, HEADS], [-base, P // base], [0, base]]),
                             (base - 1, -1, [[0, HEADS], [base, P // base], [0, base]]),
                             (0, -1, [[0, HEADS], [base, P // base], [1, base]]) if u == 0 else
                             (0, 1, [[0, HEADS], [-base, P // base], [-1, base]])]
                    for start, mult, pattern in sides:
                        pool.affine_select(out=view, in_=view, compare_op=ALU.is_ge, fill=0.0, base=start,
                                           pattern=pattern, channel_multiplier=mult).then_inc(where_done, 1)
                        count += 1
                        pool.wait_ge(where_done, count)
                pool.tensor_copy(where_i[:], where[:]).then_inc(where_i_done, 1)

                def levels(i, u):
                    n = 2 * i + u
                    pool.wait_ge(decay_done, n + 1)
                    pool.wait_ge(scores_ready, free(n))
                    for j, w in enumerate(LEVELS):
                        halves = lambda t: t.rearrange("p (g two l) -> p g two l", two=2, l=w)
                        e, qd, kd = (halves(t[:, u, j]) for t in (decay, q_dec, k_dec))
                        pool.tensor_tensor(qd[:, :, late[u]], e[:, :, late[u]], halves(q[:, u])[:, :, late[u]],
                                           ALU.mult)
                        pool.tensor_tensor(kd[:, :, early[u]], e[:, :, early[u]],
                                           halves(k[:, u])[:, :, early[u]], ALU.mult)
                    pool.wait_ge(o_ready, free(n))
                    pool.tensor_tensor(q_dec[:, u, n_lev + 1], q[:, u], from_start[:, u],
                                       ALU.mult).then_inc(levels_done, 1)

                def store_product(i, u):
                    pool.wait_ge(staged_done, ready(2 * i + u))
                    pool.dma_start(out_t[ds(i * (2 * P) + u * P, P), :], staged[:, u]).then_inc(w_stored[u], 16)

                skewed_pairs(pool, NT, (2, levels), (0, memory(store_product)), looped=w_pairs)
                for u in range(2):
                    pool.wait_ge(w_stored[u], 16 * w_pairs)

            @block.scalar
            def _(act):
                act.preload_act_table_set(ACT_SET)
                act.sem_inc(staged_done, PRIME)
                act.wait_ge(where_i_done, 1)

                def key_tokens(i, u):
                    act.wait_ge(scores_ready, ready(2 * i + u))
                    act.activation(k_tok[:], kt_ps[:], ACT.Copy).then_inc(kt_done, 1)

                def log_f(i, u):
                    n = 2 * i + u
                    act.wait_ge(f_done, ready(n))
                    act.activation(lf[:, u].rearrange("p h t -> p (h t)"), f[:, u], ACT.Ln).then_inc(lf_done, 1)

                def decays(i, u):
                    n = 2 * i + u
                    act.wait_ge(diff_done, n + 1)
                    act.wait_ge(levels_done, free(n))
                    act.wait_ge(base_done, free(n))
                    act.activation(uncentre[:, u], diff[:, u, n_lev + 1], ACT.Exp, scale=-1.0)
                    act.drain()
                    act.activation(decay[:, u], diff[:, u], ACT.Exp)
                    act.activation(from_start[:, u], b[:, u].rearrange("p h t -> p (h t)"),
                                   ACT.Exp).then_inc(decay_done, 1)

                def copy_v(i, u):
                    act.wait_ge(v_ready, ready(2 * i + u))
                    act.activation(v[:, u], v_ps[:], ACT.Copy).then_inc(v_done, 1)

                def sigmoid(i, u):
                    n = 2 * i + u
                    act.wait_ge(clamp_done, n + 1)
                    act.activation(sig[:, u], sig[:, u], ACT.Exp, scale=-1.0)
                    act.drain()
                    act.activation(sig[:, u], sig[:, u], ACT.Ln, bias=one[:, 0:1])
                    act.drain()
                    act.activation(sig[:, u], sig[:, u], ACT.Exp, scale=-1.0).then_inc(sig_done, 1)

                def round_weight(i, u):
                    n = 2 * i + u
                    act.wait_ge(w_in[u], 16 * (i + 1))
                    act.wait_ge(acc_ready, free(n))
                    act.activation(w_high[:, u], raw[:, u], ACT.Copy).then_inc(w_high_done, 1)

                def stage(i, u):
                    act.wait_ge(acc_ready, ready(2 * i + u))
                    act.wait_ge(w_stored[u], 16 * i)
                    act.activation(staged[:, u], acc[:, u, 0:tokens], ACT.Copy).then_inc(staged_done, 1)

                def copy_out(i, u):
                    act.wait_ge(o_ready, ready(2 * i + u))
                    act.wait_ge(o_stored[u], 16 * i)
                    act.activation(o[:, u], o_ps[:], ACT.Copy).then_inc(o_done, 1)

                skewed_pairs(act, NT, (0, key_tokens), (3, log_f), (2, decays), (1, copy_v), (4, sigmoid),
                             (2, memory(round_weight)), (0, memory(stage)), (0, copy_out), looped=w_pairs - 1)

            @block.vector
            def _(dve):
                dve.sem_inc(f_done, PRIME)
                dve.sem_inc(state_done, PRIME)
                dve.sem_inc(base_done, PRIME)
                dve.sem_inc(w_low_done, PRIME)
                dve.memset(state[:], 0.0)
                dve.memset(one[:], 1.0)
                dve.wait_ge(where_i_done, 1)
                dve.drain()

                def clamp(i, u):
                    n = 2 * i + u
                    dve.wait_ge(x_in[u], 32 * (i + 1))
                    dve.tensor_scalar(sig[:, u], x[:, u].rearrange("p a h t -> p (a h t)"), -44.0, None,
                                      ALU.max).then_inc(clamp_done, 1)

                def gates(i, u):
                    n = 2 * i + u
                    dve.drain()
                    dve.wait_ge(sig_done, n + 1)
                    dve.wait_ge(levels_done, free(n))
                    dve.tensor_tensor(q[:, u], sig[:, u, 0:HW], x[:, u, 0].rearrange("p h t -> p (h t)"), ALU.mult)
                    for h in range(HEADS):
                        cols = slice(h * P, (h + 1) * P)
                        done = dve.tensor_scalar(f[:, u, cols], sig[:, u, HW + h * P:HW + (h + 1) * P],
                                                 one_minus_lb[:, h:h + 1], lb[:, h:h + 1], ALU.mult, ALU.add)
                    done.then_inc(f_done, 1)
                    dve.drain()
                    dve.tensor_scalar(k[:, u], f[:, u], -1.0, 1.0, ALU.mult, ALU.add)

                def differences(i, u):
                    n = 2 * i + u
                    dve.wait_ge(lf_done, n + 1)
                    for h in range(HEADS):
                        src, dst = lf[:, u, h], b[:, u, h]
                        if u == 1:
                            src, dst = src[:, ::-1], dst[:, ::-1]
                        dve.tensor_tensor_scan(dst, src, src, 0.0, ALU.add, ALU.bypass)
                    dve.drain()
                    for j, w in enumerate(LEVELS):
                        bv = b[:, u].rearrange("p h (m two l) -> p (h m) two l", two=2, l=w)
                        dv = diff[:, u, j].rearrange("p (g two l) -> p g two l", two=2, l=w)
                        at = (w - 1, 0)[u]
                        ref = bv[:, :, early[u], at:at + 1].to_broadcast([P, HW // (2 * w), w])
                        dve.tensor_tensor(dv[:, :, late[u]], bv[:, :, late[u]], ref, ALU.subtract)
                        dve.tensor_tensor(dv[:, :, early[u]], ref, bv[:, :, early[u]], ALU.subtract)
                    dve.tensor_tensor(diff[:, u, n_lev].rearrange("p (h t) -> p h t", h=HEADS),
                                      b[:, u, :, last_t[u]:last_t[u] + 1].to_broadcast([P, HEADS, P]), b[:, u],
                                      ALU.subtract)
                    bv = b[:, u].rearrange("p h (m l) -> p (h m) l", l=base)
                    dve.tensor_tensor(diff[:, u, n_lev + 1].rearrange("p (g l) -> p g l", l=base), bv,
                                      bv[:, :, CENTRE:CENTRE + 1].to_broadcast([P, HW // base, base]),
                                      ALU.subtract).then_inc(diff_done, 1)

                def base_and_state(i, u):
                    n = 2 * i + u
                    dve.drain()
                    dve.wait_ge(decay_done, n + 1)
                    dve.tensor_tensor(q_dec[:, u, n_lev], q[:, u], decay[:, u, n_lev + 1], ALU.mult)
                    dve.tensor_tensor(k_dec[:, u, n_lev], k[:, u], uncentre[:, u], ALU.mult)
                    dve.tensor_copy(whole[:, u].unsqueeze(2),
                                    from_start[:, u].rearrange("p (h t) -> p h t", h=HEADS)[:, :, last_t[u]:last_t[u] + 1])
                    dve.tensor_tensor(k_dec[:, u, n_lev + 1], k[:, u], decay[:, u, n_lev],
                                      ALU.mult).then_inc(base_done, 1)

                def mask(i, u):
                    dve.wait_ge(scores_ready, ready(2 * i + u))
                    dve.tensor_copy(s_t[:], s_ps[:, 0])
                    dve.drain()
                    dve.copy_predicated(s_t[:], where_i[:, u], s_ps[:, 1]).then_inc(s_done, 1)

                def carry(i, u):
                    dve.wait_ge(o_ready, ready(2 * i + u))
                    if isinstance(i, int) and i == anew_after[u]:
                        done = dve.memset(state[:, u], 0.0)
                    else:
                        for h in range(HEADS):
                            cols = slice(h * P, (h + 1) * P)
                            done = dve.scalar_tensor_tensor(state[:, u, cols], state[:, u, cols],
                                                            whole[:, u, h:h + 1], st_ps[:, cols],
                                                            ALU.mult, ALU.add)
                    done.then_inc(state_done, 1)

                def split_low(i, u):
                    n = 2 * i + u
                    dve.wait_ge(w_high_done, n + 1)
                    dve.tensor_tensor(w_low[:, u], raw[:, u], w_high[:, u].bitcast(F32),
                                      ALU.subtract).then_inc(w_low_done, 1)

                skewed_pairs(dve, NT, (0, mask), (3, differences), (0, carry), (2, base_and_state), (4, gates),
                             (5, clamp), (2, memory(split_low)), apart=(anew_after[1],), looped=w_pairs - 1)

            @block.tensor
            def _(pe):
                pe.sem_inc(v_ready, PRIME)
                pe.sem_inc(scores_ready, PRIME)
                pe.sem_inc(o_ready, PRIME)
                pe.sem_inc(acc_ready, PRIME)
                pe.wait_ge(ones_done, 3)

                def transpose_v(i, u):
                    n = 2 * i + u
                    pe.wait_ge(v_in[u], 16 * (i + 1))
                    pe.wait_ge(v_done, n)
                    for h in range(HEADS):
                        done = pe.transpose(v_ps[:, h * P:(h + 1) * P], v_t[:, u, h], ident[:])
                    done.then_inc(v_ready, 1)

                def scores(i, u):
                    n = 2 * i + u
                    pe.wait_ge(base_done, ready(n))
                    pe.wait_ge(levels_done, ready(n))
                    pe.wait_ge(s_done, n)
                    pe.wait_ge(kt_done, n)
                    for h in range(HEADS):
                        cols = slice(h * P, (h + 1) * P)
                        pe.transpose(kt_ps[:, cols], k_dec[:, u, n_lev + 1, cols], ident[:])
                    for h in range(HEADS):
                        for j, w in enumerate(LEVELS):
                            for at in range(0, P, 2 * w):
                                cols = slice(h * P + at, h * P + at + 2 * w)
                                pe.matmul(s_ps[at:at + 2 * w, 0, cols], k_dec[:, u, j, cols], q_dec[:, u, j, cols],
                                          start=(j == 0), stop=(j == n_lev - 1))
                    for h in range(HEADS):
                        cols = slice(h * P, (h + 1) * P)
                        done = pe.matmul(s_ps[:, 1, cols], k_dec[:, u, n_lev, cols], q_dec[:, u, n_lev, cols],
                                         start=True, stop=True)
                    done.then_inc(scores_ready, 1)

                def output(i, u):
                    n = 2 * i + u
                    pe.wait_ge(v_done, n + 1)
                    pe.wait_ge(kt_done, n + 1)
                    pe.wait_ge(state_done, n + PRIME)
                    pe.wait_ge(o_done, n)
                    for h in range(HEADS):
                        cols = slice(h * P, (h + 1) * P)
                        pe.matmul(st_ps[:, cols], k_tok[:, cols], v[:, u, cols], start=True, stop=True)
                    pe.wait_ge(s_done, n + 1)
                    for h in range(HEADS):
                        cols = slice(h * P, (h + 1) * P)
                        pe.matmul(o_ps[:, cols], q_dec[:, u, n_lev + 1, cols], state[:, u, cols],
                                  start=True, stop=False)
                        done = pe.matmul(o_ps[:, cols], s_t[:, cols], v[:, u, cols], start=False, stop=True)
                    done.then_inc(o_ready, 1)

                def product(i, u):
                    n = 2 * i + u
                    pe.wait_ge(w_low_done, ready(n))
                    pe.wait_ge(staged_done, free(n))
                    for k in range(KC):
                        last = product3(pe, acc[:, u, 0:tokens], (w_high[:, u, k], w_low[:, u, k]),
                                        (high[:, k], low[:, k]), k == 0, k == KC - 1)
                    last.then_inc(acc_ready, 1)

                skewed_pairs(pe, NT, (1, transpose_v), (0, output), (1, scores), (1, memory(product)),
                             looped=w_pairs - 1)


def lambda_of(nc, q1, k1, q2, k2, lam):
    with Mem(nc, "lam") as m:
        vecs = m.sb("vecs", [DK, 4])
        prods = m.sb("prods", [DK, 2])
        ones = m.sb("ones", [DK, P])
        e = m.sb("e", [P, 2])
        sums = m.ps("sums", [P, 2])
        vecs_in, prods_done, sums_done, exp_done = (
            m.sem(s) for s in ("vecs_in", "prods_done", "sums_done", "exp_done"))
        with nc.Block() as block:
            @block.sync
            def _(sp):
                with nc.allow_non_contiguous_dma(reason="four columns of 64 numbers"):
                    for j, vec in enumerate((q1, q2, k1, k2)):
                        sp.dma_start(vecs[:, j:j + 1], vec.rearrange("(p a) -> p a", a=1)).then_inc(vecs_in, 16)

            @block.vector
            def _(dve):
                dve.memset(ones[:], 1.0)
                dve.wait_ge(vecs_in, 64)
                dve.tensor_tensor(prods[:], vecs[:, 0:2], vecs[:, 2:4], ALU.mult).then_inc(prods_done, 1)
                dve.wait_ge(exp_done, 1)
                dve.tensor_tensor(lam[:], e[:, 0:1], e[:, 1:2], ALU.subtract)
                dve.drain()
                dve.tensor_scalar(lam[:], lam[:], LAM_INIT, None, ALU.add)

            @block.tensor
            def _(pe):
                pe.wait_ge(prods_done, 1)
                pe.matmul(sums[:], ones[:], prods[:], start=True, stop=True).then_inc(sums_done, 1)

            @block.scalar
            def _(act):
                act.preload_act_table_set(ACT_SET)
                act.wait_ge(sums_done, 1)
                act.activation(e[:], sums[:], ACT.Exp).then_inc(exp_done, 1)


def diff_attention(nc, tag, proj_t, first, seq, g_da, lam, ident, eps, mix_out, split=None):
    nk = seq // P
    slopes = [2.0 ** (-8.0 * (h + 1) / HEADS) for h in range(HEADS)]
    width = 2 * seq - P
    banks = [(at, min(512, seq)) for at in range(0, seq, 512)]
    with Mem(nc, tag) as m:
        keys = m.sb("keys", [DK, 2, HEADS * seq])
        v_t = m.sb("v_t", [P, HEADS, seq])
        v = m.sb("v", [P, nk, HW])
        where = m.sb("where", [P, width])
        bias = m.sb("bias", [P, width])
        gain = m.sb("gain", [P, P])
        query = m.sb("query", [DK, 2, HEADS * seq])
        scaled = m.sb("scaled", [DK, 2, 2, P])
        q_factor, slope, minus_slope = (m.sb(s, [P, HEADS]) for s in ("q_factor", "slope", "minus_slope"))
        score = m.sb("score", [P, 2, 2, seq])
        prob = m.sb("prob", [P, 2, 2, seq])
        attn_t = m.sb("attn_t", [P, seq])
        top = m.sb("top", [P, 2, 2])
        total = m.sb("total", [P, 2, 2])
        o_in = m.sb("o_in", [P, 2, P])
        sq = m.sb("sq", [P, P])
        ss, rstd = m.sb("ss", [P, 1]), m.sb("rstd", [P, 1])
        o = m.sb("o", [P, 2, P])
        score_ps = m.ps("score_ps", [P, 2, max(512, seq)])
        attn_ps = m.ps("attn_ps", [P, max(512, seq)])
        o_ps = m.ps("o_ps", [P, 2, 512])
        stored = [m.sem(f"stored{u}") for u in range(2)]
        (loaded, v_in, gain_in, slopes_done, where_done, q_done, v_ready, v_done, scores_ready, top_done, prob_done,
         attn_done, attn_t_ready, attn_t_done, o_ready, rstd_done, o_done) = (m.sem(s) for s in (
             "loaded", "v_in", "gain_in", "slopes_done", "where_done", "q_done", "v_ready", "v_done", "scores_ready", "top_done",
             "prob_done", "attn_done", "attn_t_ready", "attn_t_done", "o_ready", "rstd_done",
             "o_done"))
        v_ps = (attn_ps[:, 0:HW], o_ps[:, 0])
        score_read = [m.sem(f"score_read{c}") for c in range(2)]
        per_buffer = HEADS * nk // 2

        rider = WeightSplit(m, *split) if split else None

        def skewed(eng, *parts, values=None):
            lead_max = max(lead for lead, _ in parts)

            def slot(h, t, heads_left):
                for lead, part in parts:
                    if 0 <= t + lead < nk * heads_left:
                        part(h + (t + lead) // nk, (t + lead) % nk)

            for t in range(-lead_max, 0):
                if t == -1 and values:
                    values()
                slot(0, t, HEADS)
            looped = HEADS - 1 if nk > lead_max else 0
            if looped:
                with eng.Fori(0, looped) as h:
                    for t in range(nk):
                        slot(h, t, 2)
            for h in range(looped, HEADS):
                for t in range(nk):
                    slot(h, t, HEADS - h)

        def step(h, t):
            return h * nk + t

        def uses(h, t):
            return h * (nk // 2) + t // 2

        with nc.Block() as block:
            @block.sync
            def _(sp):
                for heads, row in ((query, ROW_DQ), (keys, ROW_DK)):
                    for c in range(2):
                        sp.dma_start(heads[:, c].rearrange("p (h t) -> p h t", h=HEADS),
                                     proj_t[row:row + HW, first:first + seq]
                                     .rearrange("(h c p) t -> c p h t", c=2, p=DK)[c]).then_inc(loaded, 16)
                sp.dma_start(v_t[:], proj_t[ROW_DV:ROW_DV + HW, first:first + seq]
                             .rearrange("(h p) t -> p h t", p=P)).then_inc(v_in, 16)
                with nc.allow_non_contiguous_dma(reason="one row for all partitions"):
                    sp.dma_start(gain[:], g_da.rearrange("(a n) -> a n", a=1).to_broadcast([P, P])).then_inc(gain_in, 16)
                if rider:
                    for h in range(HEADS):
                        for t in range(nk):
                            rider.load(sp, h, t)

            @block.gpsimd
            def _(pool):
                pool.iota(where[:], [[-1, width]], base=seq - P, channel_multiplier=1,
                          allow_small_or_imprecise_dtypes=True).then_inc(where_done, 1)
                with pool.Fori(0, HEADS) as h:
                    for t in range(nk):
                        pool.wait_ge(o_done, step(h, t) + 1)
                        pool.dma_start(mix_out[first + t * P:first + (t + 1) * P, ds(h * P + HW, P)],
                                       o[:, t % 2]).then_inc(stored[t % 2], 16)
                for u in range(2):
                    pool.wait_ge(stored[u], 16 * per_buffer)

            @block.vector
            def _(dve):
                for h in range(HEADS):
                    dve.memset(q_factor[:, h:h + 1], DA_SCALE / slopes[h])
                    dve.memset(slope[:, h:h + 1], slopes[h])
                    last = dve.memset(minus_slope[:, h:h + 1], -slopes[h])
                last.then_inc(slopes_done, 1)
                dve.wait_ge(where_done, 1)
                dve.scalar_tensor_tensor(bias[:], where[:], -1.0, where[:], ALU.mult, ALU.min)
                dve.wait_ge(loaded, 64)
                dve.wait_ge(gain_in, 16)
                dve.tensor_scalar(gain[:], gain[:], 1.0 - LAM_INIT, None, ALU.mult)
                dve.drain()

                def scale_query(h, t):
                    n, u = step(h, t), t % 2
                    dve.wait_ge(scores_ready, 2 * n + 2)
                    wait_apart(dve)
                    dve.tensor_scalar(scaled[:, u], query[:, :, ds(h * seq + t * P, P)], q_factor[0:DK, ds(h, 1)],
                                      None, ALU.mult).then_inc(q_done, 1)

                def find_top(h, t):
                    n, u = step(h, t), t % 2
                    col = seq - P - t * P
                    for c in range(2):
                        dve.wait_ge(scores_ready, 2 * n + c + 1 + 2 * PRIME)
                        wait_apart(dve)
                        dve.tensor_tensor_reduce(out=score[:, u, c], in0=score_ps[:, c, 0:seq],
                                                 in1=bias[:, col:col + seq], scale=1.0, scalar=-3.0e38,
                                                 op0=ALU.add, op1=ALU.max,
                                                 accum_out=top[:, u, c:c + 1]).then_inc(score_read[c], 1)
                    dve.drain()
                    dve.tensor_scalar(top[:, u], top[:, u], minus_slope[:, ds(h, 1)], None,
                                      ALU.mult).then_inc(top_done, 1)

                def attention(h, t):
                    n, u = step(h, t), t % 2
                    dve.wait_ge(prob_done, n + 1)
                    dve.reciprocal(total[:, u], total[:, u])
                    dve.drain()
                    dve.tensor_tensor(total[:, u, 1:2], total[:, u, 1:2], lam[:], ALU.mult)
                    dve.drain()
                    dve.tensor_scalar(prob[:, u, 1], prob[:, u, 1], total[:, u, 1:2], None, ALU.mult)
                    dve.drain()
                    dve.scalar_tensor_tensor(prob[:, u, 0], prob[:, u, 0], total[:, u, 0:1], prob[:, u, 1],
                                             ALU.mult, ALU.subtract).then_inc(attn_done, 1)

                def head_norm(h, t):
                    n, u = step(h, t), t % 2
                    dve.wait_ge(rstd_done, ready(n))
                    dve.wait_ge(stored[u], uses(h, t) * 16)
                    dve.scalar_tensor_tensor(o[:, u], o_in[:, u], rstd[:, 0:1], gain[:], ALU.mult,
                                             ALU.mult).then_inc(o_done, 1)

                side = [(0, lambda h, t: rider.subtract(dve, h, t))] if rider else []
                if rider:
                    rider.start(dve)
                skewed(dve, (1, attention), (3, find_top), (4, scale_query), (0, head_norm), *side)

            @block.scalar
            def _(act):
                act.preload_act_table_set(ACT_SET)
                act.sem_inc(rstd_done, PRIME)
                act.wait_ge(slopes_done, 1)

                def values():
                    for t in range(nk):
                        act.wait_ge(v_ready, t + 1)
                        act.activation(v[:, t], v_ps[t % 2], ACT.Copy).then_inc(v_done, 1)

                def exps(h, t):
                    n, u = step(h, t), t % 2
                    act.wait_ge(top_done, n + 1)
                    act.wait_ge(attn_t_ready, free(n))
                    wait_apart(act)
                    for c in range(2):
                        done = act.activation(prob[:, u, c], score[:, u, c], ACT.Exp, scale=slope[:, ds(h, 1)],
                                              bias=top[:, u, c:c + 1], accum_out=total[:, u, c:c + 1])
                    done.then_inc(prob_done, 1)

                def copy_attention(h, t):
                    n = step(h, t)
                    act.wait_ge(attn_t_ready, ready(n))
                    act.wait_ge(o_ready, n)
                    act.activation(attn_t[:], attn_ps[:, 0:seq], ACT.Copy).then_inc(attn_t_done, 1)

                def head_rstd(h, t):
                    n, u = step(h, t), t % 2
                    act.wait_ge(o_ready, n + 1)
                    act.wait_ge(o_done, n)
                    act.activation(o_in[:, u], o_ps[:, u, 0:P], ACT.Copy)
                    act.activation(sq[:], o_ps[:, u, 0:P], ACT.Square, accum_out=ss[:])
                    act.drain()
                    act.activation(rstd[:], ss[:], ACT.Ln, scale=1.0 / P, bias=eps[:, 0:1])
                    act.drain()
                    act.activation(rstd[:], rstd[:], ACT.Exp, scale=-0.5).then_inc(rstd_done, 1)

                side = [(0, lambda h, t: rider.round(act, h, t))] if rider else []
                skewed(act, (2, exps), (0, head_rstd), (1, copy_attention), *side, values=values)

            @block.tensor
            def _(pe):
                pe.sem_inc(scores_ready, 2 * PRIME)
                pe.sem_inc(attn_t_ready, PRIME)
                pe.wait_ge(loaded, 64)

                def values():
                    pe.wait_ge(v_in, 16)
                    for t in range(nk):
                        if t >= 2:
                            pe.wait_ge(v_done, t - 1)
                        for h in range(HEADS):
                            last = pe.transpose(v_ps[t % 2][:, h * P:(h + 1) * P], v_t[:, h, t * P:(t + 1) * P], ident[:])
                        last.then_inc(v_ready, 1)
                    pe.wait_ge(v_done, nk)

                def scores(h, t):
                    n, u = step(h, t), t % 2
                    pe.wait_ge(q_done, n + 1)
                    for c in range(2):
                        pe.wait_ge(score_read[c], n)
                        wait_apart(pe)
                        for at, size in banks:
                            last = pe.matmul(score_ps[:, c, at:at + size], scaled[:, u, c],
                                             keys[:, c, ds(h * seq + at, size)], start=True, stop=True)
                        last.then_inc(scores_ready, 1)

                def transposes(h, t):
                    n, u = step(h, t), t % 2
                    pe.wait_ge(attn_done, n + 1)
                    pe.wait_ge(attn_t_done, n)
                    for c in range(nk):
                        last = pe.transpose(attn_ps[:, c * P:(c + 1) * P], prob[:, u, 0, c * P:(c + 1) * P], ident[:])
                    last.then_inc(attn_t_ready, 1)

                def output(h, t):
                    n, u = step(h, t), t % 2
                    pe.wait_ge(attn_t_done, n + 1)
                    pe.wait_ge(rstd_done, free(n))
                    for c in range(nk):
                        last = pe.matmul(o_ps[:, u, 0:P], attn_t[:, c * P:(c + 1) * P], v[:, c, ds(h * P, P)],
                                         start=(c == 0), stop=(c == nk - 1))
                    last.then_inc(o_ready, 1)

                skewed(pe, (3, scores), (0, output), (1, transposes), values=values)


def mix_out(nc, tag, o_fwd, o_bwd, proj_t, mix, x_rows, g_hg, w_high, w_low, ident, eps, x1_out, g_next, high, low):
    with Mem(nc, tag) as m:
        of = m.sb("of", [P, 2, HW])
        ob = m.sb("ob", [P, 2, HW])
        gate_t = m.sb("gate_t", [P, 2, HEADS, P])
        mixed = m.sb("mixed", [P, 2, D])
        x = m.sb("x", [P, 2, D])
        gain = m.sb("gain", [P, HW])
        one = m.sb("one", [P, 1])
        sig = m.sb("sig", [P, HW])
        sq = m.sb("sq", [P, HW])
        silu = m.sb("silu", [P, HW])
        ss, rstd = m.sb("ss", [P, HEADS]), m.sb("rstd", [P, HEADS])
        m_high, m_low = m.sb("m_high", [P, 2, KC, P], F32R), m.sb("m_low", [P, 2, KC, P], F32R)
        gain_next = m.sb("gain_next", [P, D])
        xn = m.sb("xn", [P, D])
        ss_next, rstd_next = m.sb("ss_next", [P, 1]), m.sb("rstd_next", [P, 1])
        gate_ps = m.ps("gate_ps", [P, HW])
        mt_ps = m.ps("mt_ps", [P, D])
        out_ps = m.ps("out_ps", [P, D])
        xt_ps = m.ps("xt_ps", [P, D])
        gate_in, heads_in, x_in = ([m.sem(f"{s}{u}") for u in range(2)] for s in ("gate_in", "heads_in", "x_in"))
        stored = [m.sem(f"stored{u}") for u in range(2)]
        (gain_in, gate_ready, clamp_done, sig_done, ss_done, rstd_done, mixed_done, mt_ready, high_done, low_done, out_ready,
         x1_done) = (m.sem(s) for s in ("gain_in", "gate_ready", "clamp_done", "sig_done", "ss_done",
                                        "rstd_done", "mixed_done", "mt_ready", "high_done", "low_done", "out_ready", "x1_done"))
        next_rstd_done, xn_done, xt_ready, xt_high_done, xt_low_done = (
            m.sem(s) for s in ("next_rstd_done", "xn_done", "xt_ready", "xt_high_done", "xt_low_done"))
        by_k = lambda t: t.rearrange("p (k t) -> p k t", k=KC)
        with nc.Block() as block:
            @block.sync
            def _(sp):
                with nc.allow_non_contiguous_dma(reason="one row for all partitions"):
                    sp.dma_start(gain[:], g_hg.rearrange("(a n) -> a n", a=1).to_broadcast([P, HW])).then_inc(gain_in, 16)
                    sp.dma_start(gain_next[:], g_next.rearrange("(a n) -> a n", a=1).to_broadcast([P, D])).then_inc(gain_in, 16)

                def load_gate(i, u):
                    sp.wait_ge(gate_ready, free(2 * i + u))
                    sp.dma_start(gate_t[:, u], proj_t[ROW_G:ROW_G + HW, ds(i * (2 * P) + u * P, P)]
                                 .rearrange("(h p) t -> p h t", p=P)).then_inc(gate_in[u], 16)

                def load_heads(i, u):
                    t = ds(i * (2 * P) + u * P, P)
                    sp.wait_ge(mt_ready, free(2 * i + u))
                    sp.dma_start(of[:, u], o_fwd[t, :]).then_inc(heads_in[u], 16)
                    sp.dma_start(ob[:, u], o_bwd[t, :]).then_inc(heads_in[u], 16)
                    sp.dma_start(mixed[:, u, HW:], mix[t, HW:]).then_inc(heads_in[u], 16)

                skewed_pairs(sp, NT // 2, (4, load_heads), (5, load_gate))

            @block.gpsimd
            def _(pool):
                def load_x(i, u):
                    pool.wait_ge(xn_done, free(2 * i + u))
                    pool.wait_ge(stored[u], 16 * i)
                    wait_apart(pool)
                    pool.dma_start(x[:, u], rows_of(x_rows, i, u)).then_inc(x_in[u], 16)

                def store(i, u):
                    pool.wait_ge(x1_done, 2 * i + u + 1)
                    wait_apart(pool)
                    pool.dma_start(x1_out[ds(i * (2 * P) + u * P, P), :], x[:, u]).then_inc(stored[u], 16)

                skewed_pairs(pool, NT // 2, (2, load_x), (1, store), looped=NT_P // 2 - 1)
                for u in range(2):
                    pool.wait_ge(stored[u], 16 * (NT // 2))

            @block.scalar
            def _(act):
                act.preload_act_table_set(ACT_SET)
                act.sem_inc(sig_done, PRIME)

                def sigmoid(i, u):
                    n = 2 * i + u
                    act.wait_ge(clamp_done, n + 1)
                    act.activation(sig[:], sig[:], ACT.Exp, scale=-1.0)
                    act.drain()
                    act.activation(sig[:], sig[:], ACT.Ln, bias=one[:, 0:1])
                    act.drain()
                    act.activation(sig[:], sig[:], ACT.Exp, scale=-1.0).then_inc(sig_done, 1)
                    act.wait_ge(ss_done, n + 1)
                    act.activation(rstd[:], ss[:], ACT.Ln, scale=1.0 / P, bias=eps[:, 0:1])
                    act.drain()
                    act.activation(rstd[:], rstd[:], ACT.Exp, scale=-0.5).then_inc(rstd_done, 1)

                def round_mixed(i, u):
                    n = 2 * i + u
                    act.wait_ge(mt_ready, ready(n))
                    act.wait_ge(out_ready, free(n))
                    act.activation(m_high[:, u].rearrange("p k t -> p (k t)"), mt_ps[:], ACT.Copy).then_inc(high_done, 1)

                def find_next_rstd(i, u):
                    n = 2 * i + u
                    act.wait_ge(x1_done, n + 1)
                    act.activation(xn[:], x[:, u], ACT.Square, accum_out=ss_next[:])
                    act.drain()
                    act.activation(rstd_next[:], ss_next[:], ACT.Ln, scale=1.0 / D, bias=eps[:, 0:1])
                    act.drain()
                    act.activation(rstd_next[:], rstd_next[:], ACT.Exp, scale=-0.5).then_inc(next_rstd_done, 1)

                def round_next(i, u):
                    n = 2 * i + u
                    act.wait_ge(xt_ready, n + 1)
                    wait_apart(act)
                    act.activation(high[:, :, ds(n * P, P)], by_k(xt_ps[:]), ACT.Copy).then_inc(xt_high_done, 1)

                skewed_pairs(act, NT // 2, (0, find_next_rstd), (2, round_mixed), (3, sigmoid), (0, round_next))

            @block.vector
            def _(dve):
                dve.sem_inc(xn_done, PRIME)
                dve.memset(one[:], 1.0)
                dve.wait_ge(gain_in, 32)

                def heads(t):
                    return t.rearrange("p (h c) -> p h c", h=HEADS)

                def sum_heads(i, u):
                    n = 2 * i + u
                    dve.drain()
                    dve.wait_ge(gate_ready, ready(n))
                    dve.tensor_scalar(sig[:], gate_ps[:], -44.0, None, ALU.max).then_inc(clamp_done, 1)
                    dve.wait_ge(heads_in[u], 48 * (i + 1))
                    dve.tensor_tensor(of[:, u], of[:, u], ob[:, u], ALU.add)
                    dve.drain()
                    dve.tensor_tensor(sq[:], of[:, u], of[:, u], ALU.mult)
                    dve.drain()
                    dve.tensor_reduce(ss[:], heads(sq[:]), AX.X, ALU.add).then_inc(ss_done, 1)

                def low_part(i, u):
                    dve.wait_ge(high_done, 2 * i + u + 1)
                    dve.tensor_tensor(m_low[:, u].rearrange("p k t -> p (k t)"), mt_ps[:],
                                      m_high[:, u].rearrange("p k t -> p (k t)").bitcast(F32),
                                      ALU.subtract).then_inc(low_done, 1)

                def gate(i, u):
                    n = 2 * i + u
                    dve.tensor_tensor(of[:, u], of[:, u], gain[:], ALU.mult)
                    dve.wait_ge(sig_done, ready(n))
                    dve.tensor_tensor(silu[:], gate_ps[:], sig[:], ALU.mult)
                    dve.drain()
                    dve.tensor_tensor(silu[:], silu[:], of[:, u], ALU.mult)
                    dve.drain()
                    dve.wait_ge(rstd_done, n + 1)
                    dve.tensor_tensor(heads(mixed[:, u, 0:HW]), heads(silu[:]),
                                      rstd[:].unsqueeze(2).to_broadcast([P, HEADS, P]),
                                      ALU.mult).then_inc(mixed_done, 1)

                def residual(i, u):
                    n = 2 * i + u
                    dve.wait_ge(out_ready, ready(n))
                    dve.wait_ge(x_in[u], 16 * (i + 1))
                    dve.tensor_tensor(x[:, u], out_ps[:], x[:, u], ALU.add).then_inc(x1_done, 1)

                def scale_next(i, u):
                    dve.wait_ge(next_rstd_done, 2 * i + u + 1)
                    dve.scalar_tensor_tensor(xn[:], x[:, u], rstd_next[:], gain_next[:], ALU.mult,
                                             ALU.mult).then_inc(xn_done, 1)

                def low_next(i, u):
                    n = 2 * i + u
                    dve.wait_ge(xt_high_done, n + 1)
                    wait_apart(dve)
                    dve.tensor_tensor(low[:, :, ds(n * P, P)], by_k(xt_ps[:]),
                                      high[:, :, ds(n * P, P)].bitcast(F32), ALU.subtract).then_inc(xt_low_done, 1)

                skewed_pairs(dve, NT // 2, (3, sum_heads), (0, scale_next), (2, low_part), (3, gate), (1, residual),
                             (0, low_next))

            @block.tensor
            def _(pe):
                pe.sem_inc(mt_ready, PRIME)
                pe.sem_inc(gate_ready, PRIME)
                pe.sem_inc(out_ready, PRIME)

                def gate_transposes(i, u):
                    pe.wait_ge(gate_in[u], 16 * (i + 1))
                    pe.wait_ge(mixed_done, 2 * i + u)
                    for h in range(HEADS):
                        last = pe.transpose(gate_ps[:, h * P:(h + 1) * P], gate_t[:, u, h], ident[:])
                    last.then_inc(gate_ready, 1)

                def mixed_transposes(i, u):
                    n = 2 * i + u
                    pe.wait_ge(heads_in[u], 48 * (i + 1))
                    pe.wait_ge(mixed_done, n + 1)
                    pe.wait_ge(low_done, n)
                    for k in range(KC):
                        last = pe.transpose(mt_ps[:, k * P:(k + 1) * P], mixed[:, u, k * P:(k + 1) * P], ident[:])
                    last.then_inc(mt_ready, 1)

                def product(i, u):
                    n = 2 * i + u
                    pe.wait_ge(low_done, n + 1)
                    pe.wait_ge(x1_done, n)
                    for half in (slice(0, 512), slice(512, D)):
                        for k in range(KC):
                            last = product3(pe, out_ps[:, half], (m_high[:, u, k], m_low[:, u, k]),
                                            (w_high[:, k, half], w_low[:, k, half]), k == 0, k == KC - 1)
                    last.then_inc(out_ready, 1)

                def next_transposes(i, u):
                    n = 2 * i + u
                    pe.wait_ge(xn_done, ready(n))
                    pe.wait_ge(xt_low_done, n)
                    for k in range(KC):
                        last = pe.transpose(xt_ps[:, k * P:(k + 1) * P], xn[:, k * P:(k + 1) * P], ident[:])
                    last.then_inc(xt_ready, 1)

                skewed_pairs(pe, NT // 2, (2, mixed_transposes), (1, product), (0, next_transposes),
                             (4, gate_transposes))


def cross_attention(nc, tag, q_t, kv_t, x1_rows, w_high, w_low, ident, x2_out):
    NM = 2 * N_MEM
    MC = N_MEM // P
    DC = CA_DH // P
    with Mem(nc, tag) as m:
        keys = m.sb("keys", [P, KC, NM])
        v_t = m.sb("v_t", [P, KC, NM])
        v = m.sb("v", [P, NM // P, D])
        q = m.sb("q", [P, 2, KC, P])
        x1 = m.sb("x1", [P, 2, D])
        top = m.sb("top", [P, 2, HEADS])
        total = m.sb("total", [P, 2, HEADS])
        prob = m.sb("prob", [P, 2, D])
        prob_t = m.sb("prob_t", [P, 2 * HEADS, P])
        o_high, o_low = m.sb("o_high", [P, 2, KC, P], F32R), m.sb("o_low", [P, 2, KC, P], F32R)
        x2 = m.sb("x2", [P, 2, D])
        score_ps, pt_ps, ot_ps, out_ps = (m.ps(s, [P, D]) for s in ("score_ps", "pt_ps", "ot_ps", "out_ps"))
        q_in, x1_in = ([m.sem(f"{s}{u}") for u in range(2)] for s in ("q_in", "x1_in"))
        stored = [m.sem(f"stored{u}") for u in range(2)]
        (loaded, v_in, v_ready, v_done, scores_ready, top_done, exp_done, prob_done, pt_ready, pt_done, ot_ready,
         high_done, low_done, out_ready, x2_done) = (m.sem(s) for s in (
             "loaded", "v_in", "v_ready", "v_done", "scores_ready", "top_done", "exp_done", "prob_done", "pt_ready",
             "pt_done", "ot_ready", "high_done", "low_done", "out_ready", "x2_done"))

        looped = NT_P // 2 - 2

        def group_of(i):
            return int(isinstance(i, int) and 2 * i >= NT_P)

        with nc.Block() as block:
            @block.sync
            def _(sp):
                def load_values():
                    for k in range(0, KC, 2):
                        sp.dma_start(v_t[:, k:k + 2], kv_t[D + k * P:D + (k + 2) * P, :]
                                     .rearrange("(k p) t -> p k t", p=P)).then_inc(v_in, 16)

                for k in range(0, KC, 2):
                    sp.dma_start(keys[:, k:k + 2], kv_t[k * P:(k + 2) * P, :]
                                 .rearrange("(k p) t -> p k t", p=P)).then_inc(loaded, 16)

                def load_q(i, u):
                    sp.wait_ge(scores_ready, free(2 * i + u))
                    sp.dma_start(q[:, u], q_t[:, ds(i * (2 * P) + u * P, P)]
                                 .rearrange("(k p) t -> p k t", p=P)).then_inc(q_in[u], 16)

                def load_x1(i, u):
                    sp.wait_ge(x2_done, free(2 * i + u))
                    sp.dma_start(x1[:, u], x1_rows[ds(i * (2 * P) + u * P, P), :]).then_inc(x1_in[u], 16)

                skewed_pairs(sp, NT // 2, (1, load_x1), (4, load_q), looped=looped, worked_in=(-2, load_values))

            @block.gpsimd
            def _(pool):
                with pool.Fori(0, NT // 2) as i:
                    for u in range(2):
                        pool.wait_ge(x2_done, ready(2 * i + u))
                        pool.dma_start(x2_out[ds(i * (2 * P) + u * P, P), :], x2[:, u]).then_inc(stored[u], 16)
                for u in range(2):
                    pool.wait_ge(stored[u], 16 * (NT // 2))

            @block.scalar
            def _(act):
                act.preload_act_table_set(ACT_SET)

                def values():
                    for t in range(NM // P):
                        act.wait_ge(v_ready, t + 1)
                        act.activation(v[:, t], pt_ps[:], ACT.Copy).then_inc(v_done, 1)

                def exps(i, u):
                    n = 2 * i + u
                    act.wait_ge(top_done, n + 1)
                    act.wait_ge(pt_ready, free(n))
                    for h in range(HEADS):
                        cols = slice(h * N_MEM, (h + 1) * N_MEM)
                        done = act.activation(prob[:, u, cols], score_ps[:, cols], ACT.Exp, scale=CA_SCALE,
                                              bias=top[:, u, h:h + 1], accum_out=total[:, u, h:h + 1])
                    done.then_inc(exp_done, 1)

                def copy_prob(i, u):
                    n = 2 * i + u
                    act.wait_ge(pt_ready, ready(n))
                    act.wait_ge(ot_ready, n)
                    act.activation(prob_t[:].rearrange("p c t -> p (c t)"), pt_ps[:], ACT.Copy).then_inc(pt_done, 1)

                def round_out(i, u):
                    n = 2 * i + u
                    act.wait_ge(ot_ready, n + 1)
                    act.wait_ge(out_ready, free(n))
                    act.activation(o_high[:, u].rearrange("p k t -> p (k t)"), ot_ps[:], ACT.Copy).then_inc(high_done, 1)

                skewed_pairs(act, NT // 2, (1, round_out), (2, copy_prob), (3, exps), looped=looped,
                             worked_in=(-2, values))

            @block.vector
            def _(dve):
                dve.sem_inc(x2_done, PRIME)

                def find_top(i, u):
                    n = 2 * i + u
                    dve.wait_ge(scores_ready, ready(n))
                    dve.tensor_reduce(top[:, u], score_ps[:].rearrange("p (h c) -> p h c", h=HEADS), AX.X, ALU.max)
                    dve.drain()
                    dve.tensor_scalar(top[:, u], top[:, u], -CA_SCALE, None, ALU.mult).then_inc(top_done, 1)

                def normalise(i, u):
                    n = 2 * i + u
                    dve.wait_ge(exp_done, n + 1)
                    dve.reciprocal(total[:, u], total[:, u])
                    dve.drain()
                    heads = prob[:, u].rearrange("p (h c) -> p h c", h=HEADS)
                    dve.tensor_tensor(heads, heads, total[:, u].unsqueeze(2).to_broadcast([P, HEADS, N_MEM]),
                                      ALU.mult).then_inc(prob_done, 1)

                def low_part(i, u):
                    dve.wait_ge(high_done, 2 * i + u + 1)
                    dve.tensor_tensor(o_low[:, u].rearrange("p k t -> p (k t)"), ot_ps[:],
                                      o_high[:, u].rearrange("p k t -> p (k t)").bitcast(F32),
                                      ALU.subtract).then_inc(low_done, 1)

                def residual(i, u):
                    n = 2 * i + u
                    dve.wait_ge(out_ready, ready(n))
                    dve.wait_ge(x1_in[u], 16 * (i + 1))
                    dve.wait_ge(stored[u], 16 * i)
                    dve.tensor_tensor(x2[:, u], out_ps[:], x1[:, u], ALU.add).then_inc(x2_done, 1)

                skewed_pairs(dve, NT // 2, (1, low_part), (3, find_top), (3, normalise), (0, residual), looped=looped)

            @block.tensor
            def _(pe):
                pe.sem_inc(pt_ready, PRIME)
                pe.sem_inc(scores_ready, PRIME)
                pe.sem_inc(out_ready, PRIME)
                pe.wait_ge(loaded, 16 * KC // 2)

                def values():
                    pe.wait_ge(v_in, 16 * KC // 2)
                    for t in range(NM // P):
                        pe.wait_ge(v_done, t)
                        for k in range(KC):
                            last = pe.transpose(pt_ps[:, k * P:(k + 1) * P], v_t[:, k, t * P:(t + 1) * P], ident[:])
                        last.then_inc(v_ready, 1)
                    pe.wait_ge(v_done, NM // P)

                def scores(i, u):
                    n, group = 2 * i + u, group_of(i)
                    pe.wait_ge(q_in[u], 16 * (i + 1))
                    pe.wait_ge(exp_done, n)
                    for h in range(HEADS):
                        for c in range(DC):
                            k = h * DC + c
                            last = pe.matmul(score_ps[:, h * N_MEM:(h + 1) * N_MEM], q[:, u, k],
                                             keys[:, k, group * N_MEM:(group + 1) * N_MEM],
                                             start=(c == 0), stop=(c == DC - 1))
                    last.then_inc(scores_ready, 1)

                def transposes(i, u):
                    n = 2 * i + u
                    pe.wait_ge(prob_done, n + 1)
                    pe.wait_ge(pt_done, n)
                    for c in range(2 * HEADS):
                        last = pe.transpose(pt_ps[:, c * P:(c + 1) * P], prob[:, u, c * P:(c + 1) * P], ident[:])
                    last.then_inc(pt_ready, 1)

                def heads_out(i, u):
                    n, group = 2 * i + u, group_of(i)
                    pe.wait_ge(pt_done, n + 1)
                    pe.wait_ge(low_done, n)
                    for k in range(KC):
                        h = k // DC
                        for c in range(MC):
                            last = pe.matmul(ot_ps[:, k * P:(k + 1) * P], v[:, group * MC + c, k * P:(k + 1) * P],
                                             prob_t[:, h * MC + c], start=(c == 0), stop=(c == MC - 1))
                    last.then_inc(ot_ready, 1)

                def product(i, u):
                    n = 2 * i + u
                    pe.wait_ge(low_done, n + 1)
                    pe.wait_ge(x2_done, n + PRIME)
                    for half in (slice(0, 512), slice(512, D)):
                        for k in range(KC):
                            last = product3(pe, out_ps[:, half], (o_high[:, u, k], o_low[:, u, k]),
                                            (w_high[:, k, half], w_low[:, k, half]), k == 0, k == KC - 1)
                    last.then_inc(out_ready, 1)

                skewed_pairs(pe, NT // 2, (1, heads_out), (2, transposes), (3, scores), (0, product), looped=looped,
                             worked_in=(-2, values))


def router(nc, tag, h_high, h_low, w_rg, b_rg, w_re, b_re, ident, slots, slot_i, weight, expert_i, last_pair):
    NL = N_GROUPS + N_EXP
    NB = MAX_BLOCKS
    with Mem(nc, tag) as m:
        w = m.sb("w", [P, KC, P])
        w_high, w_low = m.sb("w_high", [P, KC, P], F32R), m.sb("w_low", [P, KC, P], F32R)
        logits_t = m.sb("logits_t", [P, T])
        bias = m.sb("bias", [P, NL])
        logits = m.sb("logits", [P, NT, NL])
        first_g = m.sb("first_g", [P, N_GROUPS])
        first_e = m.sb("first_e", [P, N_EXP])
        before = m.sb("before", [P, P])
        ones = m.sb("ones", [P, P])
        block_no = m.sb("block_no", [P, NB])
        entry = m.sb("entry", [P, 2, NT, 2], I32)
        unused = m.sb("unused", [P, NB, 2], I32)
        g_top, g_sum, e_top1, e_top2, e_diff, e_sum, pick = (
            m.sb(s, [P, NT]) for s in ("g_top", "g_sum", "e_top1", "e_top2", "e_diff", "e_sum", "pick"))
        g_one = m.sb("g_one", [P, NT, N_GROUPS])
        g_exp = m.sb("g_exp", [P, NT, N_GROUPS])
        masked = m.sb("masked", [P, NT, N_EXP])
        chosen = m.sb("chosen", [P, 2, NT, N_EXP])
        both = m.sb("both", [P, NT, N_EXP])
        place = m.sb("place", [P, NT, N_EXP])
        carry = m.sb("carry", [P, NT + 1, N_EXP])
        blocks = m.sb("blocks", [P, N_EXP])
        blocks_i = m.sb("blocks_i", [P, N_EXP], I32)
        block_end = m.sb("block_end", [P, N_EXP])
        start = m.sb("start", [P, N_EXP])
        dest = m.sb("dest", [P, 2, NT])
        dest_i = m.sb("dest_i", [P, 2, NT], I32)
        table_i = m.sb("table_i", [NB, P, 2], I32)
        table = m.sb("table", [NB, 2, P])
        past = m.sb("past", [P, NB, N_EXP])
        expert = m.sb("expert", [P, NB])
        logits_ps = m.ps("logits_ps", [P, 1536])
        tr_ps = m.ps("tr_ps", [P, 512])
        rank_ps = m.ps("rank_ps", [P, 512])
        sum_ps = m.ps("sum_ps", [P, 512])
        (loaded, cleared, tables, w_done, w_high_done, w_low_done, lt_ready, lt_done, tr_ready, g_shifted,
         g_exp_done, e_diff_done, e_exp_done, both_done, rank_ready, dest_done, table_cleared, scattered, table_in, table_done, table_ready) = (
            m.sem(s) for s in (
                "loaded", "cleared", "tables", "w_done", "w_high_done", "w_low_done", "lt_ready", "lt_done",
                "tr_ready", "g_shifted", "g_exp_done", "e_diff_done", "e_exp_done", "both_done", "rank_ready",
                "dest_done", "table_cleared", "scattered", "table_in", "table_done", "table_ready"))
        with nc.Block() as block:
            @block.sync
            def _(sp):
                sp.wait_ge(w_done, 1)
                with nc.allow_non_contiguous_dma(reason="short rows of router weights"):
                    sp.dma_start(w[:, :, 0:N_GROUPS], w_rg.rearrange("(k p) n -> p k n", p=P)).then_inc(loaded, 16)
                    sp.dma_start(w[:, :, N_GROUPS:NL], w_re.rearrange("(k p) n -> p k n", p=P)).then_inc(loaded, 16)
                    sp.dma_start(bias[:, 0:N_GROUPS],
                                 b_rg.rearrange("(a n) -> a n", a=1).to_broadcast([P, N_GROUPS])).then_inc(loaded, 16)
                    sp.dma_start(bias[:, N_GROUPS:NL],
                                 b_re.rearrange("(a n) -> a n", a=1).to_broadcast([P, N_EXP])).then_inc(loaded, 16)
                sp.wait_ge(cleared, 3)
                sp.dma_start(slots.rearrange("(p b) a -> p b a", p=P), unused[:]).then_inc(table_cleared, 16)
                sp.wait_ge(scattered, 16 * 2 * NT)
                sp.dma_start(table_i[:], slots.rearrange("(b p) a -> b p a", p=P)).then_inc(table_in, 16)

            @block.gpsimd
            def _(pool):
                pool.memset(before[:], 1.0).then_inc(cleared, 1)
                pool.memset(unused[:, :, 0], 0).then_inc(cleared, 1)
                pool.memset(unused[:, :, 1], 2 * T).then_inc(cleared, 1)
                pool.memset(ones[:], 1.0).then_inc(tables, 1)
                pool.wait_ge(cleared, 3)
                pool.affine_select(out=before[:], in_=before[:], compare_op=ALU.is_gt, fill=0.0, base=0,
                                   pattern=[[1, P]], channel_multiplier=-1).then_inc(tables, 1)
                for table, step, base, width in ((first_g, -1, N_GROUPS, N_GROUPS), (first_e, -1, N_EXP, N_EXP),
                                                 (block_no, 1, 0, NB)):
                    pool.iota(table[:], [[step, width]], base=base, channel_multiplier=0,
                              allow_small_or_imprecise_dtypes=True).then_inc(tables, 1)
                pool.iota(entry[:, :, :, 0], [[0, 2], [P, NT]], base=0, channel_multiplier=1).then_inc(tables, 1)
                pool.iota(entry[:, :, :, 1], [[T, 2], [P, NT]], base=0, channel_multiplier=1).then_inc(tables, 1)
                pool.wait_ge(tables, 7)
                pool.wait_ge(dest_done, 1)
                pool.wait_ge(table_cleared, 16)
                for c in range(2):
                    for t in range(NT):
                        pool.indirect_dma_start(
                            out=slots, out_offset=bass.IndirectOffsetOnAxis(ap=dest_i[:, c, t:t + 1], axis=0),
                            in_=entry[:, c, t], in_offset=None).then_inc(scattered, 16)
                pool.wait_ge(scattered, 16 * 2 * NT)

            @block.scalar
            def _(act):
                act.preload_act_table_set(ACT_SET)
                act.wait_ge(loaded, 64)
                act.activation(w_high[:], w[:], ACT.Copy).then_inc(w_high_done, 1)
                act.wait_ge(g_shifted, 1)
                act.activation(g_exp[:], g_exp[:], ACT.Exp).then_inc(g_exp_done, 1)
                act.wait_ge(e_diff_done, 1)
                act.activation(e_diff[:], e_diff[:], ACT.Exp).then_inc(e_exp_done, 1)

            @block.vector
            def _(dve):
                def over(t, n):
                    return t.unsqueeze(2).to_broadcast([P, NT, n])

                def pick_first(values, top_of, order, one, n):
                    dve.tensor_reduce(top_of[:], values, AX.X, ALU.max)
                    dve.drain()
                    dve.tensor_tensor(one, values, over(top_of[:], n), ALU.is_equal)
                    dve.drain()
                    dve.tensor_tensor(one, one, order[:].unsqueeze(1).to_broadcast([P, NT, n]), ALU.mult)
                    dve.drain()
                    dve.tensor_reduce(pick[:], one, AX.X, ALU.max)
                    dve.drain()
                    dve.tensor_tensor(one, one, over(pick[:], n), ALU.is_equal)
                    dve.drain()

                dve.memset(w[:], 0.0).then_inc(w_done, 1)
                dve.memset(carry[:, 0], 0.0)
                dve.wait_ge(w_high_done, 1)
                dve.tensor_tensor(w_low[:], w[:], w_high[:].bitcast(F32), ALU.subtract).then_inc(w_low_done, 1)
                dve.wait_ge(lt_ready, 1)
                dve.tensor_copy(logits_t[:], logits_ps[:, 0:T]).then_inc(lt_done, 1)
                dve.wait_ge(tr_ready, 1)
                dve.wait_ge(tables, 7)
                dve.tensor_tensor(logits[:], tr_ps[:, 0:NT * NL].rearrange("p (t n) -> p t n", n=NL),
                                  bias[:].unsqueeze(1).to_broadcast([P, NT, NL]), ALU.add)
                dve.drain()
                pick_first(logits[:, :, 0:N_GROUPS], g_top, first_g, g_one[:], N_GROUPS)
                dve.tensor_tensor(g_exp[:], logits[:, :, 0:N_GROUPS], over(g_top[:], N_GROUPS),
                                  ALU.subtract).then_inc(g_shifted, 1)
                by_group = lambda t: t.rearrange("p t (g e) -> p (t g) e", g=N_GROUPS)
                sel = g_one[:].rearrange("p t g -> p (t g)").unsqueeze(2).to_broadcast([P, NT * N_GROUPS, EPG])
                for t in range(NT):
                    dve.tensor_tensor(masked[:, t].rearrange("p (g e) -> p g e", g=N_GROUPS),
                                      logits[:, t, N_GROUPS:].rearrange("p (g e) -> p g e", g=N_GROUPS),
                                      g_one[:, t].unsqueeze(2).to_broadcast([P, N_GROUPS, EPG]), ALU.mult)
                dve.drain()
                dve.tensor_scalar(g_one[:], g_one[:], -1.0, 1e30, ALU.add, ALU.mult)
                dve.drain()
                dve.tensor_tensor(by_group(masked[:]), by_group(masked[:]), sel, ALU.add)
                dve.drain()
                pick_first(masked[:], e_top1, first_e, chosen[:, 0], N_EXP)
                dve.scalar_tensor_tensor(masked[:], chosen[:, 0], -3e30, masked[:], ALU.mult, ALU.add)
                dve.drain()
                pick_first(masked[:], e_top2, first_e, chosen[:, 1], N_EXP)
                dve.tensor_tensor(e_diff[:], e_top2[:], e_top1[:], ALU.subtract).then_inc(e_diff_done, 1)
                dve.tensor_tensor(both[:], chosen[:, 0], chosen[:, 1], ALU.add).then_inc(both_done, 1)
                dve.wait_ge(g_exp_done, 1)
                dve.tensor_reduce(g_sum[:], g_exp[:], AX.X, ALU.add)
                dve.wait_ge(e_exp_done, 1)
                dve.tensor_scalar(e_sum[:], e_diff[:], 1.0, None, ALU.add)
                dve.drain()
                dve.tensor_tensor(e_sum[:], e_sum[:], g_sum[:], ALU.mult)
                dve.drain()
                dve.reciprocal(weight[:, 0], e_sum[:])
                dve.drain()
                dve.tensor_tensor(weight[:, 1], weight[:, 0], e_diff[:], ALU.mult)
                dve.wait_ge(rank_ready, 1)
                for t in range(NT):
                    dve.drain()
                    dve.tensor_tensor(carry[:, t + 1], carry[:, t], sum_ps[:, t * N_EXP:(t + 1) * N_EXP], ALU.add)
                dve.drain()
                dve.tensor_scalar(blocks[:], carry[:, NT], float(P - 1), None, ALU.add)
                dve.drain()
                dve.tensor_copy(blocks_i[:], blocks[:])
                dve.drain()
                dve.tensor_scalar(blocks_i[:], blocks_i[:], P.bit_length() - 1, None, ALU.arith_shift_right)
                dve.drain()
                dve.tensor_copy(blocks[:], blocks_i[:])
                dve.drain()
                dve.tensor_tensor_scan(block_end[:], blocks[:], blocks[:], 0.0, ALU.add, ALU.bypass)
                dve.drain()
                dve.tensor_tensor(start[:], block_end[:], blocks[:], ALU.subtract)
                dve.drain()
                dve.tensor_scalar(start[:], start[:], float(P), None, ALU.mult)
                dve.tensor_tensor(place[:], rank_ps[:, 0:NT * N_EXP].rearrange("p (t e) -> p t e", e=N_EXP),
                                  carry[:, 0:NT], ALU.add)
                dve.drain()
                dve.tensor_tensor(place[:], place[:], start[:].unsqueeze(1).to_broadcast([P, NT, N_EXP]), ALU.add)
                dve.drain()
                for c in range(2):
                    dve.tensor_tensor(chosen[:, c], chosen[:, c], place[:], ALU.mult)
                dve.drain()
                for c in range(2):
                    dve.tensor_reduce(dest[:, c], chosen[:, c], AX.X, ALU.add)
                dve.drain()
                dve.tensor_copy(dest_i[:], dest[:]).then_inc(dest_done, 1)
                dve.tensor_tensor(past[:], block_end[:].unsqueeze(1).to_broadcast([P, NB, N_EXP]),
                                  block_no[:].unsqueeze(2).to_broadcast([P, NB, N_EXP]), ALU.is_le)
                dve.drain()
                dve.tensor_reduce(expert[:], past[:], AX.X, ALU.add)
                dve.drain()
                dve.tensor_scalar(expert[:], expert[:], float(N_EXP - 1), None, ALU.min)
                dve.tensor_scalar(blocks[:, 0:1], block_end[:, N_EXP - 1:N_EXP], -1.0, None, ALU.add)
                dve.drain()
                dve.tensor_copy(expert_i[:], expert[:])
                dve.tensor_copy(last_pair[:, 0:1], blocks[:, 0:1])
                dve.drain()
                dve.tensor_scalar(last_pair[:, 0:1], last_pair[:, 0:1], 1, None, ALU.arith_shift_right)
                dve.drain()
                dve.tensor_scalar(last_pair[:, 1:2], last_pair[:, 0:1], 1, None, ALU.subtract)
                dve.wait_ge(table_in, 16)
                dve.tensor_copy(table[:], table_i[:].rearrange("b p a -> b a p")).then_inc(table_done, 1)
                dve.wait_ge(table_ready, 1)
                dve.tensor_copy(slot_i[:], tr_ps[:, 0:2 * NB].rearrange("p (a b) -> p a b", a=2))

            @block.tensor
            def _(pe):
                pe.wait_ge(w_low_done, 1)
                for at, size in TOKEN_GROUPS:
                    for k in range(KC):
                        last = product3(pe, logits_ps[:, at:at + size], (w_high[:, k], w_low[:, k]),
                                        (h_high[:, k, at:at + size], h_low[:, k, at:at + size]), k == 0, k == KC - 1)
                last.then_inc(lt_ready, 1)
                pe.wait_ge(lt_done, 1)
                for t in range(NT):
                    last = pe.transpose(tr_ps[:, t * NL:(t + 1) * NL], logits_t[0:NL, t * P:(t + 1) * P],
                                        ident[0:NL, 0:NL])
                last.then_inc(tr_ready, 1)
                pe.wait_ge(both_done, 1)
                pe.wait_ge(tables, 7)
                rows = both[:].rearrange("p t e -> p (t e)")
                pe.matmul(rank_ps[:, 0:NT * N_EXP], before[:], rows, start=True, stop=True)
                pe.matmul(sum_ps[:, 0:NT * N_EXP], ones[:], rows, start=True, stop=True).then_inc(rank_ready, 1)
                pe.wait_ge(table_done, 1)
                for a in range(2):
                    last = pe.transpose(tr_ps[:, a * NB:(a + 1) * NB], table[:, a], ident[0:NB, 0:NB])
                last.then_inc(table_ready, 1)


def experts(nc, tag, h_rows, slot_i, w_gate, w_up, w_down, expert_i, last_pair, ident, y_out):
    with Mem(nc, tag) as m:
        kinds = ("gate", "up", "down")
        raw = {s: m.sb(f"raw_{s}", [P, KC * D_EXP]) for s in kinds}
        w_high = {s: m.sb(f"high_{s}", [P, KC * D_EXP], F32R) for s in kinds}
        w_low = {s: m.sb(f"low_{s}", [P, KC * D_EXP], F32R) for s in kinds}
        width = {"gate": D_EXP, "up": D_EXP, "down": D}
        token = [m.sb(f"token{u}", [P, 1], I32) for u in range(2)]
        result = [m.sb(f"result{u}", [P, 1], I32) for u in range(2)]
        rows = m.sb("rows", [P, 2, D])
        one = m.sb("one", [P, 1])
        x_high, x_low = m.sb("x_high", [P, 2, KC, P], F32R), m.sb("x_low", [P, 2, KC, P], F32R)
        sig = m.sb("sig", [P, D_EXP])
        hidden = m.sb("hidden", [P, D_EXP])
        ht_high, ht_low = m.sb("ht_high", [P, FC, P], F32R), m.sb("ht_low", [P, FC, P], F32R)
        y = m.sb("y", [P, 2, D])
        xt_ps = m.ps("xt_ps", [P, D])
        ht_ps = m.ps("ht_ps", [P, D_EXP])
        gate_ps = m.ps("gate_ps", [P, D_EXP])
        up_ps = m.ps("up_ps", [P, D_EXP])
        y_ps = m.ps("y_ps", [P, D])
        row_in, stored = ([m.sem(f"{s}{u}") for u in range(2)] for s in ("row_in", "stored"))
        w_in, w_high_done, w_low_done, w_used = (
            {s: m.sem(f"{what}_{s}") for s in kinds} for what in ("w_in", "w_high_done", "w_low_done", "w_used"))
        (token_done, result_done, one_done, xt_ready, x_high_done, x_low_done, clamp_done, sig_done, silu_done,
         hidden_done, ht_ready, ht_high_done, ht_low_done, y_done) = (m.sem(s) for s in (
             "token_done", "result_done", "one_done", "xt_ready", "x_high_done", "x_low_done", "clamp_done",
             "sig_done", "silu_done", "hidden_done", "ht_ready", "ht_high_done", "ht_low_done", "y_done"))

        def last_of(eng, before=0):
            least, most = 2 * T // P // 2 - 1 - before, MAX_BLOCKS // 2 - 1 - before
            return eng.value_load(last_pair[0:1, before:before + 1], min_val=least, max_val=most)

        def skewed(eng, *parts):
            last = last_of(eng)
            lead_max = max(lead for lead, _ in parts)

            def pair(i, us=(0, 1), limit=6):
                for u in us:
                    for lead, part in parts:
                        if 0 <= u + lead < limit:
                            part(i + (u + lead) // 2, (u + lead) % 2)

            for n in range(-lead_max, 0):
                pair(0, (n,))
            if lead_max > 2:
                last_but_one = last_of(eng, before=1)
                with eng.Fori(0, last_but_one) as i:
                    pair(i)
                pair(last_but_one, limit=4)
            else:
                with eng.Fori(0, last) as i:
                    pair(i)
            pair(last, limit=2)
            return last

        with nc.Block() as block:
            @block.sync
            def _(sp):
                def load(s, weight):
                    depth = KC * D_EXP // width[s] * P

                    def part(i, u):
                        n = 2 * i + u
                        e = sp.value_load(expert_i[0:1, ds(n, 1)], min_val=0, max_val=N_EXP - 1)
                        sp.wait_ge(w_low_done[s], 2 * n + PRIME)
                        sp.dma_start(raw[s][:].rearrange("p (k n) -> p k n", n=width[s]),
                                     weight[ds(e * depth, depth), :].rearrange("(k p) n -> p k n", p=P)
                                     ).then_inc(w_in[s], 16)
                    return part

                skewed(sp, (1, load("up", w_up)), (0, load("down", w_down)), (2, load("gate", w_gate)))

            @block.gpsimd
            def _(pool):
                pool.memset(one[:], 1.0).then_inc(one_done, 1)

                def gather(i, u):
                    n = 2 * i + u
                    pool.wait_ge(xt_ready, free(n))
                    wait_apart(pool)
                    pool.tensor_copy(token[u][:], slot_i[:, 0, ds(n, 1)]).then_inc(token_done, 1)
                    pool.wait_ge(token_done, n + 1)
                    wait_apart(pool)
                    pool.indirect_dma_start(out=rows[:, u], out_offset=None, in_=h_rows,
                                            in_offset=bass.IndirectOffsetOnAxis(ap=token[u][:], axis=0)
                                            ).then_inc(row_in[u], 16)

                def scatter(i, u):
                    n = 2 * i + u
                    pool.wait_ge(y_done, ready(n))
                    wait_apart(pool)
                    pool.tensor_copy(result[u][:], slot_i[:, 1, ds(n, 1)]).then_inc(result_done, 1)
                    pool.wait_ge(result_done, n + 1)
                    wait_apart(pool)
                    pool.indirect_dma_start(out=y_out, in_=y[:, u], in_offset=None,
                                            out_offset=bass.IndirectOffsetOnAxis(ap=result[u][:], axis=0),
                                            bounds_check=2 * T - 1, oob_is_err=False).then_inc(stored[u], 16)

                last = skewed(pool, (4, gather), (0, scatter))
                for u in range(2):
                    pool.wait_ge(stored[u], last * 16 + 16)

            def halves(s):
                size = KC * D_EXP // 2
                return ((half, slice(half * size, (half + 1) * size)) for half in range(2))

            @block.scalar
            def _(act):
                act.preload_act_table_set(ACT_SET)
                act.sem_inc(y_done, PRIME)
                act.wait_ge(one_done, 1)

                def round_weight(s):
                    def part(i, u):
                        n = 2 * i + u
                        act.wait_ge(w_in[s], n * 16 + 16)
                        for half, cols in halves(s):
                            act.wait_ge(w_used[s], free(2 * n + half))
                            act.activation(w_high[s][:, cols], raw[s][:, cols], ACT.Copy).then_inc(w_high_done[s], 1)
                    return part

                def round_hidden(i, u):
                    act.wait_ge(ht_ready, ready(2 * i + u))
                    act.activation(ht_high[:].rearrange("p k t -> p (k t)"), ht_ps[:], ACT.Copy).then_inc(ht_high_done, 1)

                def sigmoid(i, u):
                    act.wait_ge(clamp_done, 2 * i + u + 1)
                    act.activation(sig[:], sig[:], ACT.Exp, scale=-1.0)
                    act.drain()
                    act.activation(sig[:], sig[:], ACT.Ln, bias=one[:, 0:1])
                    act.drain()
                    act.activation(sig[:], sig[:], ACT.Exp, scale=-1.0).then_inc(sig_done, 1)

                def round_x(i, u):
                    n = 2 * i + u
                    act.wait_ge(xt_ready, ready(n))
                    act.activation(x_high[:, u].rearrange("p k t -> p (k t)"), xt_ps[:], ACT.Copy).then_inc(x_high_done, 1)

                def copy_y(i, u):
                    n = 2 * i + u
                    act.wait_ge(w_used["down"], ready(2 * n + 1))
                    act.wait_ge(stored[u], i * 16)
                    act.activation(y[:, u], y_ps[:], ACT.Copy).then_inc(y_done, 1)

                skewed(act, (1, round_weight("up")), (0, round_hidden), (2, round_x), (0, round_weight("down")),
                       (1, sigmoid), (2, round_weight("gate")), (0, copy_y))

            @block.vector
            def _(dve):
                for s in kinds:
                    dve.sem_inc(w_low_done[s], PRIME)

                def split_weight_low(s):
                    def part(i, u):
                        n = 2 * i + u
                        for half, cols in halves(s):
                            dve.wait_ge(w_high_done[s], 2 * n + half + 1)
                            dve.tensor_tensor(w_low[s][:, cols], raw[s][:, cols], w_high[s][:, cols].bitcast(F32),
                                              ALU.subtract).then_inc(w_low_done[s], 1)
                    return part

                def low_hidden(i, u):
                    dve.wait_ge(ht_high_done, 2 * i + u + 1)
                    dve.tensor_tensor(ht_low[:].rearrange("p k t -> p (k t)"), ht_ps[:],
                                      ht_high[:].rearrange("p k t -> p (k t)").bitcast(F32),
                                      ALU.subtract).then_inc(ht_low_done, 1)

                def clamp(i, u):
                    n = 2 * i + u
                    dve.drain()
                    dve.wait_ge(w_used["gate"], ready(2 * n + 1))
                    dve.tensor_scalar(sig[:], gate_ps[:], -44.0, None, ALU.max).then_inc(clamp_done, 1)

                def silu(i, u):
                    dve.wait_ge(sig_done, 2 * i + u + 1)
                    dve.tensor_tensor(sig[:], gate_ps[:], sig[:], ALU.mult).then_inc(silu_done, 1)

                def low_x(i, u):
                    dve.wait_ge(x_high_done, 2 * i + u + 1)
                    dve.tensor_tensor(x_low[:, u].rearrange("p k t -> p (k t)"), xt_ps[:],
                                      x_high[:, u].rearrange("p k t -> p (k t)").bitcast(F32),
                                      ALU.subtract).then_inc(x_low_done, 1)

                def hidden_of(i, u):
                    n = 2 * i + u
                    dve.drain()
                    dve.wait_ge(w_used["up"], ready(2 * n + 1))
                    dve.wait_ge(ht_ready, n + PRIME)
                    dve.tensor_tensor(hidden[:], up_ps[:], sig[:], ALU.mult).then_inc(hidden_done, 1)

                skewed(dve, (1, split_weight_low("up")), (0, low_hidden), (1, clamp), (2, low_x),
                       (0, split_weight_low("down")), (1, silu), (1, hidden_of), (2, split_weight_low("gate")))

            @block.tensor
            def _(pe):
                for s in (xt_ready, ht_ready, *w_used.values()):
                    pe.sem_inc(s, PRIME)

                def product(s, n, out, lhs, chunks):
                    banks = [slice(at, at + 512) for at in range(0, width[s], 512)]
                    for half in range(2):
                        pe.wait_ge(w_low_done[s], ready(2 * n + half))
                        for k in range(half * chunks // 2, (half + 1) * chunks // 2):
                            for bank in banks:
                                cols = slice(k * width[s] + bank.start, k * width[s] + bank.stop)
                                last = product3(pe, out[:, bank], lhs(k), (w_high[s][:, cols], w_low[s][:, cols]),
                                                k == 0, k == chunks - 1)
                        last.then_inc(w_used[s], 1)

                def gate(i, u):
                    n = 2 * i + u
                    pe.wait_ge(x_low_done, n + 1)
                    pe.wait_ge(silu_done, n)
                    product("gate", n, gate_ps, lambda k: (x_high[:, u, k], x_low[:, u, k]), KC)

                def up(i, u):
                    n = 2 * i + u
                    pe.wait_ge(hidden_done, n)
                    product("up", n, up_ps, lambda k: (x_high[:, u, k], x_low[:, u, k]), KC)

                def transpose_hidden(i, u):
                    n = 2 * i + u
                    pe.wait_ge(hidden_done, n + 1)
                    pe.wait_ge(ht_low_done, n)
                    for k in range(FC):
                        last = pe.transpose(ht_ps[:, k * P:(k + 1) * P], hidden[:, k * P:(k + 1) * P], ident[:])
                    last.then_inc(ht_ready, 1)

                def transpose_x(i, u):
                    n = 2 * i + u
                    pe.wait_ge(row_in[u], i * 16 + 16)
                    pe.wait_ge(x_low_done, n)
                    for k in range(KC):
                        last = pe.transpose(xt_ps[:, k * P:(k + 1) * P], rows[:, u, k * P:(k + 1) * P], ident[:])
                    last.then_inc(xt_ready, 1)

                def down(i, u):
                    n = 2 * i + u
                    pe.wait_ge(ht_low_done, n + 1)
                    pe.wait_ge(y_done, n + PRIME)
                    product("down", n, y_ps, lambda k: (ht_high[:, k], ht_low[:, k]), FC)

                skewed(pe, (0, transpose_hidden), (1, gate), (2, transpose_x), (1, up), (0, down))


def combine(nc, tag, x2_rows, y_rows, weight, g_final, eps, outputs):
    with Mem(nc, tag) as m:
        x = m.sb("x", [P, 2, D])
        y = m.sb("y", [P, 2, 2, D])
        total = m.sb("total", [P, 2, D])
        gain = m.sb("gain", [P, D])
        junk = m.sb("junk", [P, D])
        ss, rstd = m.sb("ss", [P, 2]), m.sb("rstd", [P, 2])
        out = m.sb("out", [P, 2, D])
        gain_in = m.sem("gain_in")
        x_in, stored = ([m.sem(f"{s}{u}") for u in range(2)] for s in ("x_in", "stored"))
        sum_done, rstd_done, out_done = m.sem("sum_done"), m.sem("rstd_done"), m.sem("out_done")
        with nc.Block() as block:
            @block.sync
            def _(sp):
                with nc.allow_non_contiguous_dma(reason="one row for all partitions"):
                    sp.dma_start(gain[:], g_final.rearrange("(a n) -> a n", a=1).to_broadcast([P, D])).then_inc(gain_in, 16)
                with sp.Fori(0, NT // 2) as i:
                    for u in range(2):
                        sp.wait_ge(sum_done, free(2 * i + u))
                        t = i * (2 * P) + u * P
                        sp.dma_start(x[:, u], x2_rows[ds(t, P), :]).then_inc(x_in[u], 16)
                        for c in range(2):
                            sp.dma_start(y[:, u, c], y_rows[ds(t + c * T, P), :]).then_inc(x_in[u], 16)

            @block.vector
            def _(dve):
                dve.sem_inc(sum_done, PRIME)
                dve.wait_ge(gain_in, 16)

                def sum_up(i, u):
                    n = 2 * i + u
                    dve.drain()
                    dve.wait_ge(x_in[u], i * 48 + 48)
                    wait_apart(dve)
                    dve.scalar_tensor_tensor(total[:, u], y[:, u, 0], weight[:, 0, ds(n, 1)], x[:, u],
                                             ALU.mult, ALU.add)
                    dve.drain()
                    dve.scalar_tensor_tensor(total[:, u], y[:, u, 1], weight[:, 1, ds(n, 1)], total[:, u],
                                             ALU.mult, ALU.add).then_inc(sum_done, 1)

                def scale(i, u):
                    dve.wait_ge(rstd_done, 2 * i + u + 1)
                    dve.wait_ge(stored[u], i * 16)
                    dve.scalar_tensor_tensor(out[:, u], total[:, u], rstd[:, u:u + 1], gain[:], ALU.mult,
                                             ALU.mult).then_inc(out_done, 1)

                skewed_pairs(dve, NT // 2, (1, sum_up), (0, scale))

            @block.scalar
            def _(act):
                act.preload_act_table_set(ACT_SET)

                def find_rstd(i, u):
                    act.wait_ge(sum_done, ready(2 * i + u))
                    act.activation(junk[:], total[:, u], ACT.Square, accum_out=ss[:, u:u + 1])
                    act.drain()
                    act.activation(rstd[:, u:u + 1], ss[:, u:u + 1], ACT.Ln, scale=1.0 / D, bias=eps[:, 0:1])
                    act.drain()
                    act.activation(rstd[:, u:u + 1], rstd[:, u:u + 1], ACT.Exp, scale=-0.5).then_inc(rstd_done, 1)

                def store(i, u):
                    act.wait_ge(out_done, 2 * i + u + 1)
                    act.dma_start(rows_of(outputs, i, u), out[:, u]).then_inc(stored[u], 16)

                skewed_pairs(act, NT // 2, (1, find_rstd), (0, store), looped=NT_P // 2)
                for u in range(2):
                    act.wait_ge(stored[u], 16 * (NT // 2))


def encoder(nc, x_prompt, x_sample, mem_prompt, mem_sample, g_mix, w_in, hg_lb, g_hg, lam_q1, lam_k1, lam_q2,
            lam_k2, g_da, w_out, g_ca, g_mem, w_cq, w_ckv, w_co, g_ffn, w_rg, b_rg, w_re, b_re, w_gate, w_up,
            w_down, g_final, y_prompt, y_sample):
    def scratch(name, shape, dt=F32):
        return nc.dram_tensor(name, shape, dt, kind="Internal").ap()

    proj_t = scratch("proj_t", [w_in.shape[2], T])
    o_fwd, o_bwd = scratch("o_fwd", [T, HW]), scratch("o_bwd", [T, HW])
    mix = scratch("mix", [T, 2 * HW])
    x1, x2, h3 = scratch("x1", [T, D]), scratch("x2", [T, D]), scratch("h3", [T, D])
    kv_t = scratch("kv_t", [2 * D, 2 * N_MEM])
    q_t = scratch("q_t", [D, T])
    slots = scratch("slots", [MAX_BLOCKS * P, 2], I32)
    y_rows = scratch("y_rows", [2 * T, D])
    x_rows = [(x_prompt[0], NT_P), (x_sample[0], NT - NT_P)]

    with Mem(nc, "kept") as kept:
        ident, eps = kept.sb("ident", [P, P]), kept.sb("eps", [P, 1])
        lb, one_minus_lb = kept.sb("lb", [P, HEADS]), kept.sb("one_minus_lb", [P, HEADS])
        lam = kept.sb("lam", [P, 1])
        constants(nc, ident, eps)
        lower_bound(nc, hg_lb, lb, one_minus_lb)
        lambda_of(nc, lam_q1[0], lam_k1[0], lam_q2[0], lam_k2[0], lam)

        with Mem(nc, "in") as m:
            high, low = m.sb("high", [P, KC, T], F32R), m.sb("low", [P, KC, T], F32R)
            normed_transposed(nc, "norm_mix", x_rows, g_mix[0], ident, eps, high, low)
            project(nc, "proj_in", w_in[0], w_in.shape[2], high, low, TOKEN_GROUPS, proj_t)
        with Mem(nc, "mem") as m:
            high, low = m.sb("high", [P, KC, 2 * N_MEM], F32R), m.sb("low", [P, KC, 2 * N_MEM], F32R)
            normed_transposed(nc, "norm_mem", [(mem_prompt[0], N_MEM // P), (mem_sample[0], N_MEM // P)], g_mem[0],
                              ident, eps, high, low)
            hgrn(nc, "hgrn", proj_t, lb, one_minus_lb, ident, o_fwd, o_bwd, w_ckv[0], high, low, kv_t)

        diff_attention(nc, "da_prompt", proj_t, 0, SEQ_P, g_da[0], lam, ident, eps, mix)
        with Mem(nc, "w") as m:
            w_high, w_low = m.sb("w_high", [P, KC, D], F32R), m.sb("w_low", [P, KC, D], F32R)
            with Mem(nc, "cq") as m2:
                high, low = m2.sb("high", [P, KC, T], F32R), m2.sb("low", [P, KC, T], F32R)
                diff_attention(nc, "da_sample", proj_t, SEQ_P, SEQ_S, g_da[0], lam, ident, eps, mix,
                               split=(w_out[0], w_high, w_low))
                mix_out(nc, "mix_out", o_fwd, o_bwd, proj_t, mix, x_rows, g_hg[0], w_high, w_low, ident, eps, x1,
                        g_ca[0], high, low)
                project(nc, "proj_q", w_cq[0], D, high, low, TOKEN_GROUPS, q_t, split=(w_co[0], w_high, w_low))
            cross_attention(nc, "cross", q_t, kv_t, x1, w_high, w_low, ident, x2)

        slot_i, weight = kept.sb("slot_i", [P, 2, MAX_BLOCKS], I32), kept.sb("weight", [P, 2, NT])
        expert_i, last_pair = kept.sb("expert_i", [P, MAX_BLOCKS], I32), kept.sb("last_pair", [P, 2], I32)
        with Mem(nc, "moe") as m:
            high, low = m.sb("high", [P, KC, T], F32R), m.sb("low", [P, KC, T], F32R)
            normed_transposed(nc, "norm_ffn", [(x2, NT)], g_ffn[0], ident, eps, high, low, rows_out=h3)
            router(nc, "router", high, low, w_rg[0], b_rg[0], w_re[0], b_re[0], ident, slots, slot_i, weight,
                   expert_i, last_pair)
        experts(nc, "experts", h3, slot_i, w_gate[0].rearrange("e k n -> (e k) n"),
                w_up[0].rearrange("e k n -> (e k) n"), w_down[0].rearrange("e k n -> (e k) n"),
                expert_i, last_pair, ident, y_rows)
        combine(nc, "combine", x2, y_rows, weight, g_final, eps,
                [(y_prompt[0], NT_P), (y_sample[0], NT - NT_P)])


_INS = ["x_prompt", "x_sample", "mem_prompt", "mem_sample", "g_mix", "w_in", "hg_lb", "g_hg", "lam_q1", "lam_k1",
        "lam_q2", "lam_k2", "g_da", "w_out", "g_ca", "g_mem", "w_cq", "w_ckv", "w_co", "g_ffn", "w_rg", "b_rg",
        "w_re", "b_re", "w_gate", "w_up", "w_down", "g_final"]
_OUTS = [((1, SEQ_P, D), "float32"), ((1, SEQ_S, D), "float32")]


def kernel(**inputs):
    import numpy as _np
    import concourse.bacc as _bacc
    from concourse import mybir as _mybir
    from concourse.bass_utils import run_bass_kernel_spmd as _run

    nc = _bacc.Bacc("TRN2", target_bir_lowering=False, num_devices=1)
    arrays, args = {}, []
    for name in _INS:
        a = _np.ascontiguousarray(inputs[name])
        arrays[f"in_{name}_dram"] = a
        args.append(nc.dram_tensor(f"in_{name}_dram", a.shape, _mybir.dt.from_np(a.dtype), kind="ExternalInput").ap())
    for i, (shape, dtype) in enumerate(_OUTS):
        dt = _mybir.dt.from_np(_np.dtype(dtype))
        args.append(nc.dram_tensor(f"out_{i}_dram", shape, dt, kind="ExternalOutput").ap())
    encoder(nc, *args)
    r = _run(nc, [arrays], core_ids=[0])
    got = tuple(r.results[0][f"out_{i}_dram"] for i in range(len(_OUTS)))
    return got
```
